# Optimizing a Trainium2 kernel written in Bass

```python
import math
import jax, jax.numpy as jnp
from jax import lax
import numpy as np

D_MODEL = 1024
BATCH = 1
SEQ = 512
DEPTH = 1

MIX_DIM = D_MODEL
RWKV_HEADS = 8
RWKV_HEAD_DIM = 64
RWKV_DIM = RWKV_HEADS * RWKV_HEAD_DIM
LORA_W = 64
LORA_A = 64
LORA_G = 128
DIFF_HEADS = 4
DIFF_HEAD_DIM = 64
DIFF_DIM = DIFF_HEADS * 2 * DIFF_HEAD_DIM
RWKV_COLS = 3 * RWKV_DIM + LORA_W + LORA_A + LORA_G
DIFF_COLS = 3 * DIFF_DIM
IN_COLS = RWKV_COLS + DIFF_COLS
Q_BLOCK = 128
D_FF = 2816
CONV_WIDTH = 3
DECAY_SCALE = math.exp(-0.5)
RWKV_LN_EPS = 64e-5
NORM_EPS = 1e-6
SUBLN_EPS = 1e-5
NEG_INF = -1e30


def rms_norm(x, g, eps=NORM_EPS):
    x32 = x.astype(jnp.float32)
    y = x32 * lax.rsqrt(jnp.mean(x32 * x32, axis=-1, keepdims=True) + eps)
    return (y * g.astype(jnp.float32)).astype(x.dtype)

def alibi_slopes(n):
    return jnp.array([2.0 ** (-8.0 * (i + 1) / n) for i in range(n)], jnp.float32)

def token_shift(p):
    return jnp.pad(p[:, :-1], ((0, 0), (1, 0), (0, 0)))

def rwkv7_mix(p, mu, w_decay_up, w_decay0, w_iclr_up, w_iclr0, w_gate_up,
              k_k, k_a, r_k, ln_x_w, ln_x_b):
    B, S, _ = p.shape
    p = p.astype(jnp.float32)
    xs = p + (token_shift(p) - p) * mu
    cuts = [RWKV_DIM, 2 * RWKV_DIM, 3 * RWKV_DIM, 3 * RWKV_DIM + LORA_W,
            3 * RWKV_DIM + LORA_W + LORA_A]
    r, k, v, w_lo, a_lo, g_lo = jnp.split(xs, cuts, axis=-1)
    decay = jnp.exp(-DECAY_SCALE * jax.nn.sigmoid(w_decay0 + jnp.tanh(w_lo) @ w_decay_up))
    a = jax.nn.sigmoid(w_iclr0 + a_lo @ w_iclr_up)
    g = jax.nn.sigmoid(g_lo) @ w_gate_up
    hs = (B, S, RWKV_HEADS, RWKV_HEAD_DIM)
    kk = (k * k_k).reshape(hs)
    kk = kk / jnp.maximum(jnp.linalg.norm(kk, axis=-1, keepdims=True), 1e-12)
    k = k * (1.0 + (a - 1.0) * k_a)
    r, k, v, decay, a = (t.reshape(hs) for t in (r, k, v, decay, a))

    def step(state, inp):
        r_t, w_t, k_t, v_t, kk_t, a_t = inp
        sa = jnp.einsum('bhvk,bhk->bhv', state, -kk_t)
        state = (state * w_t[:, :, None, :]
                 + sa[..., None] * (kk_t * a_t)[:, :, None, :]
                 + v_t[..., None] * k_t[:, :, None, :])
        return state, jnp.einsum('bhvk,bhk->bhv', state, r_t)

    seq_major = tuple(jnp.moveaxis(t, 1, 0) for t in (r, decay, k, v, kk, a))
    s0 = jnp.zeros((B, RWKV_HEADS, RWKV_HEAD_DIM, RWKV_HEAD_DIM), jnp.float32)
    _, y = lax.scan(step, s0, seq_major)
    y = jnp.moveaxis(y, 0, 1)
    y = y + jnp.sum(r * k * r_k, axis=-1, keepdims=True) * v
    mean = jnp.mean(y, axis=-1, keepdims=True)
    var = jnp.mean(jnp.square(y - mean), axis=-1, keepdims=True)
    y = ((y - mean) * lax.rsqrt(var + RWKV_LN_EPS)).reshape(B, S, RWKV_DIM)
    y = y * ln_x_w + ln_x_b
    return y * g

def diff_attention(q, k, v, lam, slopes):
    B, S, H, _, d = q.shape
    nb = S // Q_BLOCK
    scale = d ** -0.5
    qh = q.transpose(0, 2, 3, 1, 4)
    kh = k.transpose(0, 2, 3, 1, 4).astype(jnp.float32)
    vh = v.transpose(0, 2, 1, 3).astype(jnp.float32)
    qb = qh.reshape(B, H, 2, nb, Q_BLOCK, d).transpose(3, 0, 1, 2, 4, 5)
    kpos = jnp.arange(S)

    def block(args):
        qblk, i = args
        qpos = i * Q_BLOCK + jnp.arange(Q_BLOCK)
        dist = (qpos[:, None] - kpos[None, :]).astype(jnp.float32)
        s = jnp.einsum('bhcqd,bhckd->bhcqk', qblk.astype(jnp.float32), kh) * scale
        s = s - slopes[None, :, None, None, None] * dist
        s = jnp.where(dist >= 0, s, NEG_INF)
        pr = jax.nn.softmax(s, axis=-1)
        attn = pr[:, :, 0] - lam * pr[:, :, 1]
        return jnp.einsum('bhqk,bhkv->bhqv', attn, vh)

    out = lax.map(block, (qb, jnp.arange(nb)))
    return out.transpose(1, 0, 3, 2, 4).reshape(B, S, H, 2 * d)

def causal_dwconv(h, w, b):
    C = h.shape[-1]
    y = lax.conv_general_dilated(h, w[:, None, :].astype(h.dtype), window_strides=(1,),
                                 padding=((CONV_WIDTH - 1, 0),),
                                 dimension_numbers=('NWC', 'WIO', 'NWC'),
                                 feature_group_count=C)
    return y + b.astype(h.dtype)

def first_inputs(seed: int = 0) -> dict:
    key = jax.random.key(seed)
    ks = jax.random.split(key, 32)
    L = DEPTH

    def nrm(k, shape, s):
        return jax.random.normal(k, shape, jnp.float32) * s

    return {
        "x": nrm(ks[0], (BATCH, SEQ, D_MODEL), 1.0),
        "ln_attn_pre": 1.0 + nrm(ks[1], (L, D_MODEL), 0.05),
        "w_in": nrm(ks[2], (L, D_MODEL, IN_COLS), D_MODEL ** -0.5),
        "mu_shift": jax.random.uniform(ks[3], (L, RWKV_COLS), jnp.float32),
        "w_decay_up": nrm(ks[4], (L, LORA_W, RWKV_DIM), LORA_W ** -0.5),
        "w_decay0": nrm(ks[5], (L, RWKV_DIM), 0.5),
        "w_iclr_up": nrm(ks[6], (L, LORA_A, RWKV_DIM), LORA_A ** -0.5),
        "w_iclr0": nrm(ks[7], (L, RWKV_DIM), 0.1),
        "w_gate_up": nrm(ks[8], (L, LORA_G, RWKV_DIM), LORA_G ** -0.5),
        "k_k": 0.85 + nrm(ks[9], (L, RWKV_DIM), 0.05),
        "k_a": 1.0 + nrm(ks[10], (L, RWKV_DIM), 0.05),
        "r_k": nrm(ks[11], (L, RWKV_HEADS, RWKV_HEAD_DIM), 0.1),
        "ln_x_w": 1.0 + nrm(ks[12], (L, RWKV_DIM), 0.05),
        "ln_x_b": nrm(ks[13], (L, RWKV_DIM), 0.02),
        "lambda_q1": nrm(ks[14], (L, DIFF_HEAD_DIM), 0.1),
        "lambda_k1": nrm(ks[15], (L, DIFF_HEAD_DIM), 0.1),
        "lambda_q2": nrm(ks[16], (L, DIFF_HEAD_DIM), 0.1),
        "lambda_k2": nrm(ks[17], (L, DIFF_HEAD_DIM), 0.1),
        "diff_subln": 1.0 + nrm(ks[18], (L, 2 * DIFF_HEAD_DIM), 0.05),
        "w_out": nrm(ks[19], (L, MIX_DIM, D_MODEL), MIX_DIM ** -0.5),
        "ln_attn_post": 1.0 + nrm(ks[20], (L, D_MODEL), 0.05),
        "ln_ffn_pre": 1.0 + nrm(ks[21], (L, D_MODEL), 0.05),
        "w_up": nrm(ks[22], (L, D_MODEL, 2 * D_FF), D_MODEL ** -0.5),
        "conv_w": nrm(ks[23], (L, CONV_WIDTH, 2 * D_FF), CONV_WIDTH ** -0.5),
        "conv_b": nrm(ks[24], (L, 2 * D_FF), 0.02),
        "w_down": nrm(ks[25], (L, D_FF, D_MODEL), D_FF ** -0.5),
        "ln_ffn_post": 1.0 + nrm(ks[26], (L, D_MODEL), 0.05),
    }

def first_block(x, ln_attn_pre, w_in, mu_shift, w_decay_up, w_decay0, w_iclr_up, w_iclr0,
              w_gate_up, k_k, k_a, r_k, ln_x_w, ln_x_b, lambda_q1, lambda_k1, lambda_q2,
              lambda_k2, diff_subln, w_out, ln_attn_post, ln_ffn_pre, w_up, conv_w, conv_b,
              w_down, ln_ffn_post):
    B, S, _ = x.shape
    slopes = alibi_slopes(DIFF_HEADS)
    h = x
    for l in range(DEPTH):
        xn = rms_norm(h, ln_attn_pre[l])
        proj = xn @ w_in[l]
        y_rwkv = rwkv7_mix(proj[..., :RWKV_COLS], mu_shift[l], w_decay_up[l], w_decay0[l],
                           w_iclr_up[l], w_iclr0[l], w_gate_up[l], k_k[l], k_a[l], r_k[l],
                           ln_x_w[l], ln_x_b[l])
        dq, dk, dv = jnp.split(proj[..., RWKV_COLS:], 3, axis=-1)
        dq = dq.reshape(B, S, DIFF_HEADS, 2, DIFF_HEAD_DIM)
        dk = dk.reshape(B, S, DIFF_HEADS, 2, DIFF_HEAD_DIM)
        dv = dv.reshape(B, S, DIFF_HEADS, 2 * DIFF_HEAD_DIM)
        lam_init = 0.8 - 0.6 * math.exp(-0.3 * l)
        lam = (jnp.exp(jnp.sum(lambda_q1[l] * lambda_k1[l]).astype(jnp.float32))
               - jnp.exp(jnp.sum(lambda_q2[l] * lambda_k2[l]).astype(jnp.float32)) + lam_init)
        o = diff_attention(dq, dk, dv, lam, slopes)
        o = rms_norm(o, diff_subln[l], eps=SUBLN_EPS) * (1.0 - lam_init)
        mix = jnp.concatenate([y_rwkv, o.reshape(B, S, DIFF_DIM)], axis=-1).astype(h.dtype)
        h = h + rms_norm(mix @ w_out[l], ln_attn_post[l])
        hn = rms_norm(h, ln_ffn_pre[l])
        u = causal_dwconv(hn @ w_up[l], conv_w[l], conv_b[l])
        gate, val = jnp.split(u, 2, axis=-1)
        f = (jax.nn.gelu(gate, approximate=True) * val) @ w_down[l]
        h = h + rms_norm(f, ln_ffn_post[l])
    return h


D_CONV = D_MODEL // 2
D_POOL = D_MODEL // 2
D_SC = D_MODEL // 2
CONV_A_K = 31
SC_K = 3
POOL_WINDOWS = (2, 4, 8, 16)
N_POOL_GROUPS = len(POOL_WINDOWS)
POOL_GROUP_DIM = D_POOL // N_POOL_GROUPS
POOL_OUT_DIM = D_MODEL // N_POOL_GROUPS
MAX_WINDOW = max(POOL_WINDOWS)
N_BRANCH = 3
PROJ_SPLITS = (D_CONV, 2 * D_CONV, 2 * D_CONV + D_POOL, 2 * D_CONV + D_POOL + D_SC,
               2 * D_CONV + D_POOL + 2 * D_SC, 2 * D_CONV + D_POOL + 3 * D_SC)
D_IN_PROJ = 2 * D_CONV + D_POOL + 3 * D_SC + N_BRANCH * D_MODEL
N_MEM = 256
XATTN_HEADS = 4
XATTN_HEAD_DIM = D_MODEL // XATTN_HEADS
MOE_GROUPS = 4
EXPERTS_PER_GROUP = 4
N_EXPERTS = MOE_GROUPS * EXPERTS_PER_GROUP
EXPERT_TOP_K = 2
D_EXPERT = D_MODEL // 4
EPS = 1e-6


def rmsnorm(x, g):
    xf = x.astype(jnp.float32)
    y = xf * lax.rsqrt(jnp.mean(xf * xf, axis=-1, keepdims=True) + EPS)
    return (y * g.astype(jnp.float32)).astype(x.dtype)

def layernorm(x, g, b):
    xf = x.astype(jnp.float32)
    mu = jnp.mean(xf, axis=-1, keepdims=True)
    var = jnp.mean(jnp.square(xf - mu), axis=-1, keepdims=True)
    y = (xf - mu) * lax.rsqrt(var + EPS)
    return (y * g.astype(jnp.float32) + b.astype(jnp.float32)).astype(x.dtype)

def causal_dwconv_2(u, w):
    k = w.shape[0]
    u_pad = jnp.pad(u, ((0, 0), (k - 1, 0), (0, 0)))
    return lax.conv_general_dilated(
        u_pad, w[:, None, :].astype(u.dtype), window_strides=(1,), padding='VALID',
        dimension_numbers=('NWC', 'WIO', 'NWC'), feature_group_count=u.shape[-1])

def multiscale_pool_minus_token(u):
    s = u.shape[1]
    uf = u.astype(jnp.float32)
    cs = jnp.cumsum(uf, axis=1)
    cs_pad = jnp.pad(cs, ((0, 0), (MAX_WINDOW, 0), (0, 0)))
    t = jnp.arange(s, dtype=jnp.int32)
    outs = []
    for i, w in enumerate(POOL_WINDOWS):
        c0, c1 = i * POOL_GROUP_DIM, (i + 1) * POOL_GROUP_DIM
        prev = cs_pad[:, MAX_WINDOW - w:MAX_WINDOW - w + s, c0:c1]
        cnt = jnp.minimum(t + 1, w).astype(jnp.float32)[None, :, None]
        outs.append((cs[:, :, c0:c1] - prev) / cnt - uf[:, :, c0:c1])
    return jnp.concatenate(outs, axis=-1).astype(u.dtype)

def gated_branch_mixer(h, w_in, conv_a_w, conv_a_b, ln_a_g, ln_a_b, w_a_out,
                       w_pool_grp, pool_scale, conv_c_w, w_c_out, w_o):
    bsz, s, _ = h.shape
    proj = h @ w_in
    a_val, a_gate, u_pool, c_x, c_b, c_c, g = jnp.split(proj, PROJ_SPLITS, axis=-1)
    a = a_val * jax.nn.sigmoid(a_gate)
    a = causal_dwconv_2(a, conv_a_w) + conv_a_b
    a = jax.nn.silu(layernorm(a, ln_a_g, ln_a_b)) @ w_a_out
    p = multiscale_pool_minus_token(u_pool).reshape(bsz, s, N_POOL_GROUPS, POOL_GROUP_DIM)
    p = jnp.einsum('bsgc,gco->bsgo', p, w_pool_grp).reshape(bsz, s, D_MODEL) * pool_scale
    c = (c_b * causal_dwconv_2(c_c * c_x, conv_c_w)) @ w_c_out
    gates = jax.nn.sigmoid(g).reshape(bsz, s, N_BRANCH, D_MODEL)
    merged = gates[:, :, 0] * a + gates[:, :, 1] * p + gates[:, :, 2] * c
    return merged @ w_o

def memory_cross_attention(h, mem_n, w_xq, w_xkv, w_xo):
    bsz, s, _ = h.shape
    q = (h @ w_xq).reshape(bsz, s, XATTN_HEADS, XATTN_HEAD_DIM)
    k, v = jnp.split(mem_n @ w_xkv, 2, axis=-1)
    k = k.reshape(bsz, N_MEM, XATTN_HEADS, XATTN_HEAD_DIM)
    v = v.reshape(bsz, N_MEM, XATTN_HEADS, XATTN_HEAD_DIM)
    scores = jnp.einsum('bshd,bmhd->bhsm', q, k).astype(jnp.float32) * (XATTN_HEAD_DIM ** -0.5)
    probs = jax.nn.softmax(scores, axis=-1).astype(v.dtype)
    o = jnp.einsum('bhsm,bmhd->bshd', probs, v).reshape(bsz, s, D_MODEL)
    return o @ w_xo

def hierarchical_moe(h, w_rg, b_rg, w_re, b_re, w_e_gate, w_e_up, w_e_down):
    bsz, s, d = h.shape
    t = h.reshape(-1, d)
    n = t.shape[0]
    p_grp = jax.nn.softmax((t @ w_rg + b_rg).astype(jnp.float32), axis=-1)
    g_val, g_idx = lax.top_k(p_grp, 1)
    le = (t @ w_re + b_re).astype(jnp.float32).reshape(n, MOE_GROUPS, EXPERTS_PER_GROUP)
    le_sel = jnp.take_along_axis(le, g_idx[:, :, None], axis=1)[:, 0]
    p_exp = jax.nn.softmax(le_sel, axis=-1)
    e_val, e_idx = lax.top_k(p_exp, EXPERT_TOP_K)
    e_val = e_val / jnp.sum(e_val, axis=-1, keepdims=True)
    weight = g_val * e_val
    eid = g_idx * EXPERTS_PER_GROUP + e_idx
    gate = jnp.sum(jax.nn.one_hot(eid, N_EXPERTS, dtype=jnp.float32) * weight[..., None], axis=1)
    act = jax.nn.silu(jnp.einsum('nd,edf->nef', t, w_e_gate)) * jnp.einsum('nd,edf->nef', t, w_e_up)
    act = act * gate[:, :, None].astype(act.dtype)
    out = jnp.einsum('nef,efd->nd', act, w_e_down)
    return out.reshape(bsz, s, d)

def second_inputs(seed: int = 0) -> dict:
    key = jax.random.key(seed)
    ks = jax.random.split(key, 32)
    f32 = jnp.float32

    def nrm(k, shape, scale):
        return jax.random.normal(k, shape, f32) * scale

    def gain(k, shape):
        return 1.0 + 0.02 * jax.random.normal(k, shape, f32)

    L = DEPTH
    return {
        "x": nrm(ks[0], (BATCH, SEQ, D_MODEL), 1.0),
        "mem": nrm(ks[1], (BATCH, N_MEM, D_MODEL), 1.0),
        "norm_mix_g": gain(ks[2], (L, D_MODEL)),
        "w_in": nrm(ks[3], (L, D_MODEL, D_IN_PROJ), D_MODEL ** -0.5),
        "conv_a_w": nrm(ks[4], (L, CONV_A_K, D_CONV), CONV_A_K ** -0.5),
        "conv_a_b": nrm(ks[5], (L, D_CONV), 0.02),
        "ln_a_g": gain(ks[6], (L, D_CONV)),
        "ln_a_b": nrm(ks[7], (L, D_CONV), 0.02),
        "w_a_out": nrm(ks[8], (L, D_CONV, D_MODEL), D_CONV ** -0.5),
        "w_pool_grp": nrm(ks[9], (L, N_POOL_GROUPS, POOL_GROUP_DIM, POOL_OUT_DIM), POOL_GROUP_DIM ** -0.5),
        "pool_scale": gain(ks[10], (L, D_MODEL)),
        "conv_c_w": nrm(ks[11], (L, SC_K, D_SC), SC_K ** -0.5),
        "w_c_out": nrm(ks[12], (L, D_SC, D_MODEL), D_SC ** -0.5),
        "w_o": nrm(ks[13], (L, D_MODEL, D_MODEL), D_MODEL ** -0.5),
        "norm_x_g": gain(ks[14], (L, D_MODEL)),
        "norm_mem_g": gain(ks[15], (L, D_MODEL)),
        "w_xq": nrm(ks[16], (L, D_MODEL, D_MODEL), D_MODEL ** -0.5),
        "w_xkv": nrm(ks[17], (L, D_MODEL, 2 * D_MODEL), D_MODEL ** -0.5),
        "w_xo": nrm(ks[18], (L, D_MODEL, D_MODEL), D_MODEL ** -0.5),
        "norm_ffn_g": gain(ks[19], (L, D_MODEL)),
        "w_rg": nrm(ks[20], (L, D_MODEL, MOE_GROUPS), D_MODEL ** -0.5),
        "b_rg": nrm(ks[21], (L, MOE_GROUPS), 0.01),
        "w_re": nrm(ks[22], (L, D_MODEL, N_EXPERTS), D_MODEL ** -0.5),
        "b_re": nrm(ks[23], (L, N_EXPERTS), 0.01),
        "w_e_gate": nrm(ks[24], (L, N_EXPERTS, D_MODEL, D_EXPERT), D_MODEL ** -0.5),
        "w_e_up": nrm(ks[25], (L, N_EXPERTS, D_MODEL, D_EXPERT), D_MODEL ** -0.5),
        "w_e_down": nrm(ks[26], (L, N_EXPERTS, D_EXPERT, D_MODEL), D_EXPERT ** -0.5),
        "norm_f_g": gain(ks[27], (D_MODEL,)),
    }

def second_block(x, mem, norm_mix_g, w_in, conv_a_w, conv_a_b, ln_a_g, ln_a_b, w_a_out,
              w_pool_grp, pool_scale, conv_c_w, w_c_out, w_o, norm_x_g, norm_mem_g,
              w_xq, w_xkv, w_xo, norm_ffn_g, w_rg, b_rg, w_re, b_re,
              w_e_gate, w_e_up, w_e_down, norm_f_g):
    for l in range(DEPTH):
        h = rmsnorm(x, norm_mix_g[l])
        x = x + gated_branch_mixer(h, w_in[l], conv_a_w[l], conv_a_b[l], ln_a_g[l], ln_a_b[l],
                                   w_a_out[l], w_pool_grp[l], pool_scale[l], conv_c_w[l],
                                   w_c_out[l], w_o[l])
        x = x + memory_cross_attention(rmsnorm(x, norm_x_g[l]), rmsnorm(mem, norm_mem_g[l]),
                                       w_xq[l], w_xkv[l], w_xo[l])
        x = x + hierarchical_moe(rmsnorm(x, norm_ffn_g[l]), w_rg[l], b_rg[l], w_re[l], b_re[l],
                                 w_e_gate[l], w_e_up[l], w_e_down[l])
    return rmsnorm(x, norm_f_g)


def setup_inputs(seed=0):
    out = dict(first_inputs(seed))
    for name, value in second_inputs(seed + 1).items():
        if name != "x":
            out[name + "_2"] = value
    return out


def reference(
    x, ln_attn_pre, w_in, mu_shift, w_decay_up, w_decay0, w_iclr_up, w_iclr0, w_gate_up, k_k,
    k_a, r_k, ln_x_w, ln_x_b, lambda_q1, lambda_k1, lambda_q2, lambda_k2, diff_subln, w_out,
    ln_attn_post, ln_ffn_pre, w_up, conv_w, conv_b, w_down, ln_ffn_post, mem_2, norm_mix_g_2,
    w_in_2, conv_a_w_2, conv_a_b_2, ln_a_g_2, ln_a_b_2, w_a_out_2, w_pool_grp_2, pool_scale_2,
    conv_c_w_2, w_c_out_2, w_o_2, norm_x_g_2, norm_mem_g_2, w_xq_2, w_xkv_2, w_xo_2,
    norm_ffn_g_2, w_rg_2, b_rg_2, w_re_2, b_re_2, w_e_gate_2, w_e_up_2, w_e_down_2, norm_f_g_2,
):
    x = first_block(
        x, ln_attn_pre, w_in, mu_shift, w_decay_up, w_decay0, w_iclr_up, w_iclr0, w_gate_up,
        k_k, k_a, r_k, ln_x_w, ln_x_b, lambda_q1, lambda_k1, lambda_q2, lambda_k2, diff_subln,
        w_out, ln_attn_post, ln_ffn_pre, w_up, conv_w, conv_b, w_down, ln_ffn_post,
    )
    return second_block(
        x, mem_2, norm_mix_g_2, w_in_2, conv_a_w_2, conv_a_b_2, ln_a_g_2, ln_a_b_2, w_a_out_2,
        w_pool_grp_2, pool_scale_2, conv_c_w_2, w_c_out_2, w_o_2, norm_x_g_2, norm_mem_g_2,
        w_xq_2, w_xkv_2, w_xo_2, norm_ffn_g_2, w_rg_2, b_rg_2, w_re_2, b_re_2, w_e_gate_2,
        w_e_up_2, w_e_down_2, norm_f_g_2,
    )


_drawn_inputs = setup_inputs


def setup_inputs(seed=0):
    import zlib

    import numpy as np

    out = dict(_drawn_inputs(seed))
    spreads = {}
    factors = {'k_k': 6.963,
     'ln_x_b': 4.177,
     'lambda_q1': 5.401,
     'conv_b': 2.723,
     'norm_mix_g_2': 3.634,
     'conv_a_b_2': 21.926,
     'ln_a_g_2': 34.076,
     'ln_a_b_2': 30.727,
     'pool_scale_2': 7.391,
     'norm_x_g_2': 8.0,
     'norm_mem_g_2': 8.0,
     'norm_ffn_g_2': 4.288,
     'b_rg_2': 29.867,
     'b_re_2': 49.485,
     'norm_f_g_2': 7.901}
    for name, (base, spread) in spreads.items():
        noise = np.random.default_rng([zlib.crc32(name.encode()), seed]).standard_normal(out[name].shape)
        drawn = base * np.exp(spread * noise) if base else spread * noise
        out[name] = __import__('jax').numpy.asarray(drawn.astype(out[name].dtype))
    for name, factor in factors.items():
        out[name] = (out[name] * factor).astype(out[name].dtype)
    return out
```

```python
import math
from contextlib import ExitStack

import concourse.bass as bass
from concourse import mybir

F32 = mybir.dt.float32
F32R = mybir.dt.float32r
ALU = mybir.AluOpType
ACT = mybir.ActivationFunctionType
AX = mybir.AxisListType

P = 128
D = 1024
S = 512
KT = D // P
TT = S // P
HD = 64
NCH = S // HD
LEVELS = 6
D_FF = 2816
N_MEM = 256
DECAY_SCALE = math.exp(-0.5)
LAM_INIT = 0.8 - 0.6 * math.exp(-0.3 * 0)
CONV_A = 31
POOL_PAD = 16
RAW, SPL = 2, 3
BLK = KT * 2 * P

STAGES = [("in", 13, 26, 14), ("out", 4, 8, 0), ("ffn", 34, 68, 68), ("mix", 12, 24, 24), ("gate", 16, 40, 40),
          ("o", 4, 8, 8), ("kv", 8, 16, 0), ("q", 4, 8, 0), ("xo", 4, 8, 8), ("moe", 48, 96, 96)]
B0, T0, E0, TILES_TO = {}, {}, {}, []
_b = _t = _e = 0
for _name, _nb, _nt, _ne in STAGES:
    B0[_name], T0[_name], E0[_name] = _b, _t, _e
    for _i in range(_nb):
        _per = (2 if _i % 2 == 0 else 3) if _name == "gate" else 2
        _t += _per
        TILES_TO.append(_t)
    _b, _e = _b + _nb, _e + _ne
    assert _t == T0[_name] + _nt
NBLK, NTILE = _b, _t

PCOLS = [("ln_attn_pre", 8), ("mu", 14), ("w_decay0", 4), ("w_iclr0", 4), ("k_k", 4), ("k_a", 4), ("r_k", 4),
         ("ln_x_w", 4), ("ln_x_b", 4), ("subln", 1), ("ln_attn_post", 8), ("ln_ffn_pre", 8), ("conv", 8 * 24),
         ("ln_ffn_post", 8), ("norm_mix", 8), ("conv_a_w", 4 * CONV_A), ("conv_a_b", 4), ("ln_a_g", 4),
         ("ln_a_b", 4), ("pool_scale", 8), ("conv_c", 12), ("norm_x", 8), ("norm_mem", 8), ("norm_ffn", 8),
         ("norm_f", 8), ("w_router", KT * 20), ("b_router", 20), ("lam", 4 * HD)]
CCOLS = [("ident", P), ("ones", P), ("blk", P), ("alibi", S), ("mask_nr", 2 * P), ("mask_lv", LEVELS * P),
         ("reset", S), ("id64", HD), ("invcnt", 4 * POOL_PAD), ("rank", 4), ("eps", 4)]


def offsets(cols):
    at, out = 0, {}
    for name, w in cols:
        out[name] = (at, w)
        at += w
    return out, at


PO, NPAR = offsets(PCOLS)
CO, NCST = offsets(CCOLS)


def build(nc, xT, memT, wstream, params, consts, lora, poolw, out):
    with ExitStack() as ctx:
        def sem(name):
            return ctx.enter_context(nc.semaphore(name))

        top = [nc.sbuf_base + (-nc.sbuf_base) % 64]
        KB = 1024

        def at(name, shape, offset, dt=F32):
            assert offset + 4 * math.prod(shape) <= nc.sbuf_usable_end, name
            return nc.alloc_sbuf_tensor_at(name, [P, *shape], dt, offset=offset)

        def sb(name, shape, dt=F32):
            t = at(name, shape, top[0], dt)
            top[0] += -(-4 * math.prod(shape) // 64) * 64
            return t

        raw = sb("raw", [RAW, BLK])
        wh = sb("wh", [SPL, KT, 2, P], F32R)
        wl = sb("wl", [SPL, KT, 2, P], F32R)
        cst = sb("cst", [NCST])
        par = sb("par", [NPAR])
        pw = sb("pw", [4, 2 * P])
        ev = sb("ev", [4, S + 2])
        tmp = sb("tmp", [2, S])
        sq = sb("sq", [2, S])
        sqa = sb("sqa", [S])
        sml = sb("sml", [64])
        rs, sd = sml[:, 0:4], sml[:, 4:8]
        lam_d, lam_e, lam_n, g08 = sml[:, 8:10], sml[:, 10:12], sml[:, 12:13], sml[:, 13:14]
        mx = sml[:, 16:20]
        nmx = sml[:, 20:24]
        den = sml[:, 24:28]
        rden = sml[:, 28:32]
        xt_off = top[0]
        XT = sb("XT", [KT, S])
        x_off = top[0]
        XH = sb("XH", [KT, S], F32R)
        XL = sb("XL", [KT, S], F32R)
        ar = top[0]

        R = at("R", [4, S], ar)
        K = at("K", [4, S], ar + 8 * KB)
        V = at("V", [4, S], ar + 16 * KB)
        LO = at("LO", [S], ar + 24 * KB)
        GLO = at("GLO", [S], ar + 26 * KB)
        OO = at("OO", [4, S], ar + 28 * KB)
        lor = at("lor", [2, S], ar + 36 * KB)
        QT = at("QT", [4, S], ar + 40 * KB)
        KD = at("KD", [4, S], xt_off)
        DV = at("DV", [TT, S], xt_off + 8 * KB)
        SC = at("SC", [2, 2, S], x_off)
        EX = at("EX", [2, 2, S], x_off + 8 * KB)
        APR = at("APR", [2, S], x_off + 16 * KB)
        AT = at("AT", [TT, S], x_off + 20 * KB)
        SQO = at("SQO", [2, S], x_off + 28 * KB)
        W = at("W", [8, S], x_off)
        AR = at("AR", [TT, 2, P], x_off + 16 * KB)
        BT = at("BT", [S], x_off + 20 * KB)
        KH = at("KH", [S], x_off + 22 * KB)
        BON = at("BON", [S], x_off + 24 * KB)
        G = at("G", [S], x_off + 26 * KB)
        AXb = at("AXb", [TT, 2, 2, HD], x_off + 28 * KB)
        Btok = at("Btok", [TT, P], xt_off)
        Ktok = at("Ktok", [TT, P], xt_off + 2 * KB)
        Vtok = at("Vtok", [TT, P], xt_off + 4 * KB)
        Tm = at("Tm", [TT, P], xt_off + 6 * KB)
        NR = at("NR", [2, TT, 2, P], xt_off + 8 * KB)
        AKRK = at("AKRK", [2, TT, 2, P], ar + 40 * KB)
        Qm = at("Qm", [TT, P], ar + 48 * KB)
        TTm = at("TTm", [TT, P], ar + 50 * KB)
        WU = at("WU", [2, TT, P], ar + 52 * KB)
        Z = at("Z", [TT, P], ar + 56 * KB)
        GT = at("GT", [NCH, HD], x_off + 10 * KB)
        ST = at("ST", [NCH, HD], x_off + 8 * KB)
        HS = at("HS", [NCH, HD], x_off + 14 * KB)
        Fo = at("Fo", [KT, S], ar + 32 * KB)
        HH = at("HH", [KT, S], ar, F32R)
        HL = at("HL", [KT, S], ar + 16 * KB, F32R)
        gl = at("gl", [2, S], ar + 48 * KB)
        yv = at("yv", [2, S], ar + 52 * KB)
        cpar = at("cpar", [64], ar + 56 * KB)
        gateg = at("gateg", [4, TT, 4], ar + 56 * KB + 256)
        gcur = at("gcur", [TT, 4], ar + 56 * KB + 512)
        rt = at("rt", [24, 16], ar + 32 * KB)
        rt3 = at("rt3", [TT, 4, 4], ar + 34 * KB)
        lg = at("lg", [TT, 20], ar + 36 * KB)
        wrh = at("wrh", [KT, 20], ar + 37 * KB, F32R)
        wrl = at("wrl", [KT, 20], ar + 38 * KB, F32R)
        APAD = at("APAD", [4, S + CONV_A - 1], ar)
        AH = at("AH", [4, S], ar, F32R)
        AL = at("AL", [4, S], ar + 8 * KB, F32R)
        CH = at("CH", [4, S], ar + 16 * KB, F32R)
        CL = at("CL", [4, S], ar + 24 * KB, F32R)
        CA = at("CA", [4, S], ar + 32 * KB)
        cpad = at("cpad", [S + 2], ar + 40 * KB)
        upad = at("upad", [2, S + POOL_PAD], ar + 42 * KB + 256)
        MG = at("MG", [KT, S], ar + 32 * KB)
        PL = at("PL", [4, S], ar + 48 * KB)
        MH = at("MH", [KT, N_MEM], ar, F32R)
        ML = at("ML", [KT, N_MEM], ar + 8 * KB, F32R)
        KX = at("KX", [KT, N_MEM], ar + 16 * KB)
        VX = at("VX", [2, D], ar + 24 * KB)
        QX = at("QX", [KT, S], ar + 32 * KB)
        MT = at("MT", [KT, N_MEM], ar + 48 * KB)
        EXx = at("EXx", [2, N_MEM], ar + 48 * KB)
        PX = at("PX", [2, N_MEM], ar + 50 * KB)
        PTx = at("PTx", [2, S], ar + 52 * KB)

        acc = ctx.enter_context(nc.psum_tensor("acc", [P, 4, S], F32))
        mb = ctx.enter_context(nc.psum_tensor("mb", [P, 4, S], F32))

        def cs(name, a=0, b=None):
            o, w = CO[name]
            return cst[:, o + a:o + (w if b is None else b)]

        def pr(name, a, b=None):
            o, _ = PO[name]
            return par[:, o + a:o + (a + 1 if b is None else b)]

        ident, ones, blk = cs("ident"), cs("ones"), cs("blk")

        loaded = [sem(f"loaded{i}") for i in range(RAW)]
        in_x, in_par, in_x2, in_mem = sem("in_x"), sem("in_par"), sem("in_x2"), sem("in_mem")
        hi_done, split_done = sem("hi_done"), sem("split_done")
        acc_ready, evac, ev_used = sem("acc_ready"), sem("evac"), sem("ev_used")
        sq_ready, sq_used = sem("sq_ready"), sem("sq_used")
        st_sum, sd_ready, rs_ready, rb_ready = sem("st_sum"), sem("sd_ready"), sem("rs_ready"), sem("rb_ready")
        xn_ready, x_ready = sem("xn_ready"), sem("x_ready")
        dchain, achain = sem("dchain"), sem("achain")
        names = ("lam_dot lam_exp lora_act at_sc at_mx at_e at_p at_t at_te at_o at_sq at_ss at_sd at_done "
                 "rk_up rk_sig rk_kk rk_cum rk_ksq rk_kss rk_kmx rk_ksd rk_exp rk_hat rk_bon rk_bsum rk_bonus rk_tok "
                 "rk_toke rk_nr rk_nrm rk_q rk_qm rk_t rk_tm rk_tt rk_tte rk_x rk_xe rk_wu rk_wue rk_z rk_zs rk_gh "
                 "rk_gs rk_hs rk_s rk_st rk_y rk_ys rk_mu rk_d rk_dsq rk_var rk_sd rk_done mixed gelu_done hid_ready "
                 "acc_added la_in la_mu la_d la_sq la_sum la_var la_sd la_y la_act ac_ready p_mm mg_ready "
                 "mem_ready xs_sc xs_mx xs_e xs_p xs_t xs_te xs_o xs_hi xs_done wr_ready rt_lg rt_sub rt_exp "
                 "gate_ready gb_ready final_ready stored").split()
        s = {n: sem(n) for n in names}

        block = ctx.enter_context(nc.Block())
        @block.sync
        def _(sp):
            sp.dma_start(XT[:, :, :], xT).then_inc(in_x, 16)
            sp.dma_start(cst[:, :], consts).then_inc(in_par, 16)
            sp.dma_start(par[:, :], params).then_inc(in_par, 16)
            for n in range(RAW):
                sp.dma_start(raw[:, n, :], wstream[n]).then_inc(loaded[n], 16)
            sp.dma_start(lor[:, :, :], lora).then_inc(in_par, 16)
            sp.dma_start(pw[:, :, :], poolw).then_inc(in_par, 16)

            def load(n, slot):
                sp.wait_ge(split_done, n - (RAW - 1))
                src = wstream[n] if isinstance(n, int) else wstream[bass.ds(n, 1)].rearrange("a p n -> p (a n)")
                sp.dma_start(raw[:, slot, :], src).then_inc(loaded[slot], 16)

            def load_range(a, b):
                assert a % RAW == 0 and (b - a) % RAW == 0
                with sp.Fori(0, (b - a) // RAW) as i:
                    for j in range(RAW):
                        load(i * RAW + (a + j), j)

            load_range(RAW, 16)
            sp.wait_ge(s["rk_done"], 4)
            sp.dma_start(XT[:, :, :], xT).then_inc(in_x2, 16)
            load_range(16, 80)
            sp.wait_ge(s["p_mm"], KT)
            sp.dma_start(MT[:, :, :], memT).then_inc(in_mem, 16)
            load_range(80, NBLK - 1)
            load(NBLK - 1, (NBLK - 1) % RAW)
            for m in range(KT):
                sp.wait_ge(s["final_ready"], m + 1)
                sp.dma_start(out[:, m, :], XT[:, m, :]).then_inc(s["stored"], 16)
            sp.wait_ge(s["stored"], 16 * KT)

        @block.gpsimd
        def _(pool):
            def lower(n, slot, rslot):
                pool.wait_ge(hi_done, n + 1)
                nc.gpsimd.tensor_tensor(wl[:, slot].rearrange("p a b c -> p (a b c)"), raw[:, rslot, :],
                                        wh[:, slot].rearrange("p a b c -> p (a b c)").bitcast(F32),
                                        ALU.subtract).then_inc(split_done, 1)

            end = NBLK
            per = RAW * SPL
            with pool.Fori(0, end // per) as i:
                for j in range(per):
                    lower(i * per + j, j % SPL, j % RAW)
            for n in range(end // per * per, end):
                lower(n, n % SPL, n % RAW)

        @block.tensor
        def _(pe):
            mm = nc.tensor.matmul

            def mm3(out_, a, b, start, stop):
                mm(out_, a[0], b[0], start=start, stop=False)
                mm(out_, a[0], b[1], start=False, stop=False)
                return mm(out_, a[1], b[0], start=False, stop=stop)

            def begin_block(n, t, tiles=2):
                pe.wait_ge(split_done, n + 1)
                for j in range(tiles):
                    if not isinstance(t, int) or t + j >= 4:
                        pe.wait_ge(evac, t + (j - 3))

            def block_tiles(n, t, slot, bank, xs=(XH, XL), kt=KT, ns=S, need=None):
                begin_block(n, t)
                for k in range(kt):
                    if need is not None:
                        pe.wait_ge(need[0], need[1] + k)
                    for j in range(2):
                        last = mm3(acc[:, (bank + j) % 4, 0:ns], (wh[:, slot, k, j, :], wl[:, slot, k, j, :]),
                                   (xs[0][:, k, 0:ns], xs[1][:, k, 0:ns]), k == 0, k == kt - 1)
                        if k == kt - 1:
                            last.then_inc(acc_ready, 1)

            def stage_blocks(name, count, need, xs=(XH, XL), ns=S, start=0):
                for b in range(start, start + count):
                    n, t = B0[name] + b, T0[name] + 2 * b
                    block_tiles(n, t, n % SPL, t % 4, xs, ns=ns, need=need if b == start else None)

            def token_tiles(n, t, xs, lots):
                begin_block(n, t)
                for j, toks in enumerate(lots):
                    for c, tok in enumerate(toks):
                        for k in range(KT):
                            last = mm3(acc[:, (t + j) % 4, c * 256:(c + 1) * 256],
                                       (xs[0][:, k, tok * P:(tok + 1) * P], xs[1][:, k, tok * P:(tok + 1) * P]),
                                       (wh[:, n % SPL, k].rearrange("p a b -> p (a b)"),
                                        wl[:, n % SPL, k].rearrange("p a b -> p (a b)")), k == 0, k == KT - 1)
                    last.then_inc(acc_ready, 1)

            def norm_sums(r, nt=TT):
                pe.wait_ge(sq_used, KT * (r + 1))
                for t in range(nt):
                    last = mm(mb[:, 0, t:t + 1], sqa[:, t * P:(t + 1) * P], ones[:, 0:1], start=True, stop=True)
                last.then_inc(st_sum, 1)

            def norm_spread(r, nt=TT):
                pe.wait_ge(rs_ready, r + 1)
                for t in range(nt):
                    last = mm(mb[:, 1, t * P:(t + 1) * P], rs[:, t:t + 1].to_broadcast([P, P]), ident,
                              start=True, stop=True)
                last.then_inc(rb_ready, 1)

            def norm(r):
                norm_sums(r)
                norm_spread(r)

            pe.wait_ge(in_par, 64)
            norm(0)
            stage_blocks("in", 11, (xn_ready, 1))
            for b in (11, 12):
                token_tiles(B0["in"] + b, T0["in"] + 2 * b, (XH, XL), ((0, 1), (2, 3)))

            def att_scores(u):
                h, i = divmod(u, TT)
                pe.wait_ge(evac, 26)
                if u >= 2:
                    pe.wait_ge(s["at_mx"], u - 1)
                w = (i + 1) * P
                for c in range(2):
                    last = mm(mb[:, 2 * (u % 2) + c, 0:w], QT[64 * c:64 * c + 64, h, i * P:(i + 1) * P],
                              KD[64 * c:64 * c + 64, h, 0:w], start=True, stop=True)
                last.then_inc(s["at_sc"], 1)

            def att_turn(u):
                h, i = divmod(u, TT)
                pe.wait_ge(s["at_p"], u + 1)
                if u >= 2:
                    pe.wait_ge(s["at_te"], u - 1)
                for j in range(i + 1):
                    last = nc.tensor.transpose(acc[:, u % 2, j * P:(j + 1) * P], APR[:, u % 2, j * P:(j + 1) * P],
                                               ident)
                last.then_inc(s["at_t"], 1)

            def att_out(h):
                pe.wait_ge(s["at_te"], TT * (h + 1))
                if h:
                    pe.wait_ge(s["at_done"], h)
                for j in range(TT):
                    last = mm(acc[:, 2, j * P:S], DV[:, j, h * P:(h + 1) * P], AT[:, j, j * P:S],
                              start=(j == 0), stop=(j == TT - 1))
                last.then_inc(s["at_o"], 1)
                pe.wait_ge(s["at_sq"], h + 1)
                mm(acc[:, 3, :], ones, SQO[:, 0, :], start=True, stop=True).then_inc(s["at_ss"], 1)

            att_scores(0)
            for u in range(4 * TT):
                if u + 1 < 4 * TT:
                    att_scores(u + 1)
                att_turn(u)
                if u % TT == TT - 1:
                    att_out(u // TT)

            def rk_head(ct, hh):
                u, hp = 2 * ct + hh, HD * hh
                ps = slice(hp, hp + HD)
                pe.wait_ge(s["rk_toke"], ct + 1)
                pe.wait_ge(s["rk_bonus"], ct + 1)
                if hh:
                    pe.wait_ge(s["rk_zs"], u)
                for t in range(TT):
                    o = 256 * (t % 2)
                    mm(acc[:, 2 + t // 2, o:o + 256], BT[ps, t * P:(t + 1) * P],
                       AR[ps, t].rearrange("p a b -> p (a b)"), start=True, stop=True)
                    last = mm(mb[:, t // 2, o:o + 256], KH[ps, t * P:(t + 1) * P],
                              AR[ps, t].rearrange("p a b -> p (a b)"), start=True, stop=True)
                last.then_inc(s["rk_nr"], 1)
                pe.wait_ge(s["rk_nrm"], u + 1)
                for t in range(TT):
                    last = nc.tensor.transpose(mb[:, 2, t * P:(t + 1) * P], NR[:, hh, t, 0, :], ident)
                last.then_inc(s["rk_q"], 1)
                for t in range(TT):
                    last = mm(acc[:, 3, t * HD:(t + 1) * HD], AKRK[:, hh, t, 0, :], Vtok[:, t, ps],
                              start=True, stop=True)
                last.then_inc(s["rk_x"], 1)
                for l in range(LEVELS):
                    if l:
                        for t in range(TT):
                            last = mm(mb[:, 2, t * P:(t + 1) * P], NR[:, hh, t, 0, :], Tm[:, t, :],
                                      start=True, stop=True)
                        last.then_inc(s["rk_q"], 1)
                        pe.wait_ge(s["rk_qm"], 5 * u + l)
                        pe.wait_ge(s["rk_tte"], 6 * u + l)
                        for t in range(TT):
                            last = mm(acc[:, 2, t * P:(t + 1) * P], TTm[:, t, :], Qm[:, t, :],
                                      start=True, stop=True)
                        last.then_inc(s["rk_t"], 1)
                    pe.wait_ge(s["rk_tm"], 6 * u + l + 1)
                    for t in range(TT):
                        last = nc.tensor.transpose(mb[:, 3, t * P:(t + 1) * P], Tm[:, t, :], ident)
                    last.then_inc(s["rk_tt"], 1)
                pe.wait_ge(s["rk_tte"], 6 * u + 6)
                pe.wait_ge(s["rk_xe"], u + 1)
                for t in range(TT):
                    last = mm(acc[:, 3, t * P:(t + 1) * P], TTm[:, t, :],
                              AXb[:, t, hh].rearrange("p a b -> p (a b)"), start=True, stop=True)
                last.then_inc(s["rk_wu"], 1)
                pe.wait_ge(s["rk_wue"], u + 1)
                for t in range(TT):
                    last = mm(mb[ps, 2, t * P:(t + 1) * P], WU[:, hh, t, 0:HD], NR[:, hh, t, 1, :],
                              start=True, stop=True)
                last.then_inc(s["rk_z"], 1)
                for c in range(NCH):
                    t, cp = c // 2, slice(HD * (c % 2), HD * (c % 2) + HD)
                    g, h = slice(t * HD, (t + 1) * HD), slice(256 + t * HD, 256 + (t + 1) * HD)
                    mm(acc[ps, c % 2, g], WU[cp, hh, t, 0:HD], Btok[cp, t, ps], start=True, stop=True)
                    mm(acc[ps, c % 2, h], Btok[cp, t, ps], WU[cp, hh, t, HD:P], start=True, stop=False)
                    last = mm(acc[ps, c % 2, h], Ktok[cp, t, ps], Vtok[cp, t, ps], start=False, stop=True)
                last.then_inc(s["rk_gh"], 1)

            def rk_pair(ct):
                if ct:
                    pe.wait_ge(s["rk_done"], ct)
                else:
                    pe.wait_ge(s["at_done"], 4)
                    pe.wait_ge(s["lora_act"], 1)
                c = slice(ct * P, (ct + 1) * P)
                mm(mb[:, 0, :], lor[0:64, 0, c], LO[0:64, :], start=True, stop=True)
                mm(mb[:, 1, :], lor[64:128, 0, c], LO[64:128, :], start=True, stop=True)
                mm(mb[:, 2, :], lor[:, 1, c], GLO[:, :], start=True, stop=True).then_inc(s["rk_up"], 1)
                pe.wait_ge(s["rk_ksq"], ct + 1)
                mm(mb[:, 3, :], blk, W[:, 5, :], start=True, stop=True).then_inc(s["rk_kss"], 1)
                pe.wait_ge(s["rk_hat"], ct + 1)
                mm(acc[:, 0, :], blk, W[:, 3, :], start=True, stop=True).then_inc(s["rk_bsum"], 1)
                for t in range(TT):
                    o = slice(t * P, (t + 1) * P)
                    nc.tensor.transpose(acc[:, 1, o], AR[:, t, 0, :], ident)
                    nc.tensor.transpose(acc[:, 2, o], W[:, 0, o], ident)
                    nc.tensor.transpose(acc[:, 3, o], W[:, 2, o], ident)
                    last = nc.tensor.transpose(mb[:, 0, o], V[:, ct, o], ident)
                last.then_inc(s["rk_tok"], 1)
                rk_head(ct, 0)
                rk_head(ct, 1)
                for c in range(2, NCH):
                    pe.wait_ge(s["rk_st"], 7 * ct + c - 1)
                    if c == 2:
                        pe.wait_ge(s["rk_gs"], ct + 1)
                    for hh in range(2):
                        ps = slice(HD * hh, HD * hh + HD)
                        last = mm(mb[ps, 3, 0:HD], GT[ps, c - 1, :], ST[ps, c - 1, :], start=True, stop=True)
                    last.then_inc(s["rk_s"], 1)
                pe.wait_ge(s["rk_st"], 7 * ct + 7)
                for hh in range(2):
                    ps = slice(HD * hh, HD * hh + HD)
                    for t in range(TT):
                        o = slice(t * P, (t + 1) * P)
                        mm(mb[ps, 0, o], WU[:, hh, t, HD:P], NR[:, hh, t, 1, :], start=True, stop=False)
                        mm(mb[ps, 0, o], Vtok[:, t, ps], AKRK[:, hh, t, 1, :], start=False, stop=False)
                        for c in (2 * t, 2 * t + 1):
                            if c:
                                last = mm(mb[ps, 0, c * HD:(c + 1) * HD], ST[ps, c, :],
                                          Z[ps, t, (c % 2) * HD:(c % 2 + 1) * HD], start=False,
                                          stop=(c % 2 == 1))
                last.then_inc(s["rk_y"], 1)
                pe.wait_ge(s["rk_ys"], ct + 1)
                mm(mb[:, 1, :], blk, W[:, 0, :], start=True, stop=True).then_inc(s["rk_mu"], 1)
                pe.wait_ge(s["rk_dsq"], ct + 1)
                mm(mb[:, 2, :], blk, W[:, 2, :], start=True, stop=True).then_inc(s["rk_var"], 1)

            for ct in range(4):
                rk_pair(ct)

            stage_blocks("out", 4, (s["mixed"], 1))
            norm(1)

            def group(name, i, hidden, need=None, spread=None):
                n0, t0 = i * 12 + B0[name], i * 24 + T0[name]
                for b in range(hidden):
                    if spread is not None and b % 2 == 0:
                        spread(i, b // 2)
                    block_tiles(n0 + b, t0 + 2 * b, (B0[name] + b) % SPL, (T0[name] + 2 * b) % 4,
                                need=need if b == 0 else None)
                for b in range(4):
                    block_tiles(n0 + hidden + b, t0 + 2 * (hidden + b), (B0[name] + hidden + b) % SPL,
                                (T0[name] + 2 * (hidden + b)) % 4, (HH, HL), kt=hidden,
                                need=(s["hid_ready"], i * 8 + (1 if name == "ffn" else 23)) if b == 0 else None)

            norm(2)
            pe.wait_ge(xn_ready, 16)
            with pe.Fori(0, 2) as i:
                group("ffn", i, 8)
            group("ffn", 2, 6)
            norm(3)

            norm(4)
            stage_blocks("mix", 12, (xn_ready, 17))

            def pooled(m):
                if m >= 2:
                    pe.wait_ge(s["mg_ready"], m - 1)
                mm(mb[:, 2 + m % 2, :], pw[:, m // 2, (m % 2) * P:(m % 2 + 1) * P], PL[:, m // 2, :],
                   start=True, stop=True).then_inc(s["p_mm"], 1)

            for m in range(KT):
                n, t = B0["gate"] + 2 * m, T0["gate"] + 5 * m
                block_tiles(n, t, n % SPL, t % 4)
                if m == 0:
                    pe.wait_ge(s["la_in"], 1)
                    mm(mb[:, 0, :], ones, sqa[:, :], start=True, stop=True).then_inc(s["la_mu"], 1)
                    pe.wait_ge(s["la_sum"], 4)
                    mm(mb[:, 1, :], ones, sqa[:, :], start=True, stop=True).then_inc(s["la_var"], 1)
                pooled(m)
                begin_block(n + 1, t + 2, 3)
                slot = (n + 1) % SPL
                for k in range(KT):
                    last = mm3(acc[:, (t + 2) % 4, :], (wh[:, slot, k, 0, :], wl[:, slot, k, 0, :]),
                               (XH[:, k, :], XL[:, k, :]), k == 0, k == KT - 1)
                last.then_inc(acc_ready, 1)
                for x, (xh, xl) in enumerate(((AH, AL), (CH, CL))):
                    for k in range(4):
                        if m == 0 and x == 0:
                            pe.wait_ge(s["ac_ready"], k + 1)
                        last = mm3(acc[:, (t + 3 + x) % 4, :],
                                   (wh[:, slot, 4 * x + k, 1, :], wl[:, slot, 4 * x + k, 1, :]),
                                   (xh[:, k, :], xl[:, k, :]), k == 0, k == 3)
                    last.then_inc(acc_ready, 1)

            stage_blocks("o", 1, (s["mg_ready"], KT + 1))
            norm_sums(5, 2)
            stage_blocks("o", 1, None, start=1)
            norm_spread(5, 2)
            stage_blocks("o", 2, None, start=2)
            stage_blocks("kv", 4, (s["mem_ready"], 1), (MH, ML), ns=N_MEM)
            for b in range(4, 8):
                token_tiles(B0["kv"] + b, T0["kv"] + 2 * b, (MH, ML), ((0,), (1,)))
            norm(6)
            stage_blocks("q", 4, (xn_ready, 25))

            def x_scores(u):
                h, i = divmod(u, TT)
                pe.wait_ge(evac, T0["q"] + 8)
                if u >= 2:
                    pe.wait_ge(s["xs_e"], u - 1)
                for k in range(2):
                    last = mm(mb[:, u % 2, 0:N_MEM], QX[:, 2 * h + k, i * P:(i + 1) * P], KX[:, 2 * h + k, :],
                              start=(k == 0), stop=(k == 1))
                last.then_inc(s["xs_sc"], 1)

            def x_turn(u):
                pe.wait_ge(s["xs_p"], u + 1)
                if u >= 2:
                    pe.wait_ge(s["xs_te"], u - 1)
                for j in range(2):
                    last = nc.tensor.transpose(mb[:, 2 + u % 2, j * P:(j + 1) * P], PX[:, u % 2, j * P:(j + 1) * P],
                                               ident)
                last.then_inc(s["xs_t"], 1)

            def x_out(h):
                pe.wait_ge(s["xs_te"], TT * (h + 1))
                if h:
                    pe.wait_ge(s["xs_done"], 2 * h)
                for v in range(2):
                    for j in range(2):
                        last = mm(acc[:, v, :], VX[:, j, h * 256 + v * P:h * 256 + (v + 1) * P], PTx[:, j, :],
                                  start=(j == 0), stop=(j == 1))
                    last.then_inc(s["xs_o"], 1)

            x_scores(0)
            for u in range(4 * TT):
                if u + 1 < 4 * TT:
                    x_scores(u + 1)
                x_turn(u)
                if u % TT == TT - 1:
                    x_out(u // TT)
            stage_blocks("xo", 4, (s["xs_done"], 1))

            def spread_gate(i, e):
                pe.wait_ge(s["gate_ready"], i + 1)
                if not isinstance(i, int) or 4 * i + e >= 2:
                    if isinstance(i, int) or e >= 2:
                        pe.wait_ge(s["hid_ready"], i * 8 + (22 + 2 * (e - 1)))
                for t in range(TT):
                    last = mm(mb[:, 2 + e % 2, t * P:(t + 1) * P], gcur[:, t, e:e + 1].to_broadcast([P, P]), ident,
                              start=True, stop=True)
                last.then_inc(s["gb_ready"], 1)

            norm(7)
            pe.wait_ge(xn_ready, 40)
            pe.wait_ge(s["wr_ready"], 1)
            for t in range(TT):
                for k in range(KT):
                    last = mm3(mb[:, 0, t * 20:(t + 1) * 20], (XH[:, k, t * P:(t + 1) * P],
                                                               XL[:, k, t * P:(t + 1) * P]),
                               (wrh[:, k, :], wrl[:, k, :]), k == 0, k == KT - 1)
            last.then_inc(s["rt_lg"], 1)
            with pe.Fori(0, 3) as i:
                group("moe", i, 8, spread=spread_gate)
            group("moe", 3, 8, spread=spread_gate)
            norm(8)

        @block.scalar
        def _(act):
            actv = nc.scalar.activation
            chain_n = [0]

            def link(ins):
                chain_n[0] += 1
                ins.then_inc(achain, 1)
                act.wait_ge(achain, chain_n[0])

            def split_hi(n, slot, rslot, value, tiles):
                act.wait_ge(loaded[rslot], value)
                if tiles is not None:
                    act.wait_ge(acc_ready, tiles)
                actv(wh[:, slot].rearrange("p a b c -> p (a b c)"), raw[:, rslot, :], ACT.Copy).then_inc(hi_done, 1)

            def ahead(n, i=None):
                n += 2
                if n >= NBLK:
                    return
                value, tiles = 16 * (n // RAW + 1), TILES_TO[n - SPL] if n >= SPL else None
                if i is not None:
                    value, tiles = i * (16 * 12 // RAW) + value, i * 24 + tiles
                split_hi(n, n % SPL, n % RAW, value, tiles)

            def take(t, e, func, bank, ring, scale=1.0):
                act.wait_ge(acc_ready, t + 1)
                if not isinstance(e, int) or e >= 4:
                    act.wait_ge(ev_used, e - 3)
                actv(ev[:, ring, 2:S + 2], acc[:, bank, :], func, scale=scale).then_inc(evac, 1)

            def take_s(t, e, func=ACT.Copy):
                take(t, e, func, t % 4, e % 4)

            def direct(t, dst, src, scale=1.0):
                act.wait_ge(acc_ready, t + 1)
                actv(dst, src, ACT.Copy, scale=scale).then_inc(evac, 1)

            def square(q, src):
                if q >= 2:
                    act.wait_ge(sq_used, q - 1)
                actv(sq[:, q % 2, 0:src.shape[-1]], src, ACT.Square).then_inc(sq_ready, 1)

            def norm_root(r, nt=TT):
                act.wait_ge(st_sum, r + 1)
                actv(sd[:, 0:nt], mb[:, 0, 0:nt], ACT.Sqrt, bias=cs("eps", 0, 1), scale=1.0 / D).then_inc(sd_ready, 1)

            act.wait_ge(in_x, 16)
            for k in range(KT):
                square(k, XT[:, k, :])
            act.wait_ge(in_par, 64)
            split_hi(0, 0, 0, 16, None)
            split_hi(1, 1, 1, 16, None)
            norm_root(0)
            for b in range(13):
                ahead(B0["in"] + b)
                for t in (2 * b, 2 * b + 1):
                    if t < 14:
                        take_s(t, t)
                    elif t < 18:
                        direct(t, QT[:, t - 14, :], acc[:, t % 4, :], 0.125)
                    elif t < 22:
                        direct(t, KD[:, t - 18, :], acc[:, t % 4, :])
                    else:
                        c, j = divmod(t - 22, 2)
                        direct(t, DV[:, 2 * j:2 * j + 2, c * 256:(c + 1) * 256],
                               acc[:, t % 4, :].rearrange("p (a b) -> p a b", a=2))
            act.wait_ge(s["lam_dot"], 1)
            actv(lam_e, lam_d, ACT.Exp).then_inc(s["lam_exp"], 1)

            def att_exp(u):
                h, i = divmod(u, TT)
                w = (i + 1) * P
                act.wait_ge(s["at_mx"], u + 1)
                for c in range(2):
                    last = actv(EX[:, u % 2, c, 0:w], SC[:, u % 2, c, 0:w], ACT.Exp,
                                bias=nmx[:, 2 * (u % 2) + c:2 * (u % 2) + c + 1],
                                accum_out=den[:, 2 * (u % 2) + c:2 * (u % 2) + c + 1])
                last.then_inc(s["at_e"], 1)

            def att_turned(u):
                h, i = divmod(u, TT)
                act.wait_ge(s["at_t"], u + 1)
                if i == 0 and h:
                    act.wait_ge(s["at_o"], h)
                actv(AT[:, 0:i + 1, i * P:(i + 1) * P],
                     acc[:, u % 2, 0:(i + 1) * P].rearrange("p (a b) -> p a b", b=P), ACT.Copy).then_inc(s["at_te"], 1)

            att_exp(0)
            for u in range(4 * TT):
                if u + 1 < 4 * TT:
                    att_exp(u + 1)
                att_turned(u)
                if u % TT == TT - 1:
                    h = u // TT
                    act.wait_ge(s["at_o"], h + 1)
                    actv(SQO[:, 0, :], acc[:, 2, :], ACT.Square).then_inc(s["at_sq"], 1)
                    act.wait_ge(s["at_ss"], h + 1)
                    actv(SQO[:, 1, :], acc[:, 3, :], ACT.Sqrt, bias=cs("eps", 1, 2),
                         scale=1.0 / P).then_inc(s["at_sd"], 1)

            def rk_pair(ct):
                act.wait_ge(s["rk_up"], ct + 1)
                actv(W[:, 0, :], mb[:, 0, :], ACT.Sigmoid, bias=pr("w_decay0", ct))
                actv(W[:, 1, :], mb[:, 1, :], ACT.Sigmoid, bias=pr("w_iclr0", ct))
                actv(G[:, :], mb[:, 2, :], ACT.Copy).then_inc(s["rk_sig"], 1)
                act.wait_ge(s["rk_kk"], ct + 1)
                actv(W[:, 5, :], W[:, 4, :], ACT.Square).then_inc(s["rk_ksq"], 1)
                act.wait_ge(s["rk_kmx"], ct + 1)
                actv(W[:, 5, :], W[:, 5, :], ACT.Sqrt).then_inc(s["rk_ksd"], 1)
                act.wait_ge(s["rk_cum"], ct + 1)
                actv(W[:, 6, :], W[:, 2, :], ACT.Exp)
                actv(W[:, 7, :], W[:, 2, :], ACT.Exp, scale=-1.0)
                actv(W[:, 3, :], W[:, 3, :], ACT.Exp).then_inc(s["rk_exp"], 1)
                act.wait_ge(s["rk_tok"], ct + 1)
                actv(AXb[:, :, :, 0, :], acc[:, 1, :].rearrange("p (t h c) -> p t h c", t=TT, h=2), ACT.Copy)
                actv(Btok[:, :, :].rearrange("p a b -> p (a b)"), acc[:, 2, :], ACT.Copy)
                actv(Ktok[:, :, :].rearrange("p a b -> p (a b)"), acc[:, 3, :], ACT.Copy)
                actv(Vtok[:, :, :].rearrange("p a b -> p (a b)"), mb[:, 0, :], ACT.Copy).then_inc(s["rk_toke"], 1)
                for hh in range(2):
                    u = 2 * ct + hh
                    act.wait_ge(s["rk_x"], u + 1)
                    actv(AXb[:, :, hh, 1, :], acc[:, 3, 0:TT * HD].rearrange("p (t c) -> p t c", t=TT),
                         ACT.Copy).then_inc(s["rk_xe"], 1)
                    for l in range(LEVELS):
                        act.wait_ge(s["rk_tt"], 6 * u + l + 1)
                        actv(TTm[:, :, :].rearrange("p a b -> p (a b)"), mb[:, 3, :], ACT.Copy).then_inc(s["rk_tte"], 1)
                    act.wait_ge(s["rk_wu"], u + 1)
                    actv(WU[:, hh].rearrange("p a b -> p (a b)"), acc[:, 3, :], ACT.Copy).then_inc(s["rk_wue"], 1)
                act.wait_ge(s["rk_gh"], 2 * ct + 2)
                actv(HS[:, :, :].rearrange("p (t a) j -> p a t j", a=2),
                     acc[:, 0:2, 256:512].rearrange("p a (t j) -> p a t j", t=TT), ACT.Copy).then_inc(s["rk_hs"], 1)
                act.wait_ge(s["rk_d"], ct + 1)
                actv(W[:, 2, :], W[:, 1, :], ACT.Square).then_inc(s["rk_dsq"], 1)
                act.wait_ge(s["rk_var"], ct + 1)
                actv(W[:, 3, :], mb[:, 2, :], ACT.Sqrt, bias=cs("eps", 2, 3), scale=1.0 / HD).then_inc(s["rk_sd"], 1)

            act.wait_ge(ev_used, 2)
            actv(LO[0:64, :], LO[0:64, :], ACT.Tanh)
            actv(GLO[:, :], GLO[:, :], ACT.Sigmoid).then_inc(s["lora_act"], 1)
            for ct in range(4):
                rk_pair(ct)

            def taken_out(t, dst, q):
                act.wait_ge(acc_ready, t + 1)
                if q >= 2:
                    act.wait_ge(sq_used, q - 1)
                actv(sq[:, q % 2, :], acc[:, t % 4, :], ACT.Square).then_inc(sq_ready, 1)
                actv(dst, acc[:, t % 4, :], ACT.Copy).then_inc(evac, 1)

            for b in range(4):
                ahead(B0["out"] + b)
                for m in (2 * b, 2 * b + 1):
                    taken_out(T0["out"] + m, Fo[:, m, :], 8 + m)
            norm_root(1)

            for m in range(KT):
                act.wait_ge(x_ready, m + 1)
                square(16 + m, XT[:, m, :])
            norm_root(2)

            def group(name, i, hidden):
                loop = None if isinstance(i, int) else i
                k = i if loop is None else 0
                n0, t0, e0 = B0[name] + 12 * k, T0[name] + 24 * k, E0[name] + 24 * k
                add = (lambda v, per: v) if loop is None else (lambda v, per: loop * per + v)
                for b in range(hidden + 4):
                    ahead(n0 + b, loop)
                    for j in range(2):
                        func = ACT.Copy
                        if name == "moe" and b < hidden and j == 0:
                            func = ACT.Silu
                        take(add(t0 + 2 * b + j, 24), add(e0 + 2 * b + j, 24), func, (t0 + 2 * b + j) % 4,
                             (e0 + 2 * b + j) % 4)
                    if name == "ffn" and b < hidden:
                        act.wait_ge(ev_used, add(e0 + 2 * b + 1, 24))
                        actv(gl[:, b % 2, :], gl[:, b % 2, :], ACT.Gelu_apprx_tanh).then_inc(s["gelu_done"], 1)
                    if b >= hidden and loop is None and k == (2 if name == "ffn" else 3):
                        for m in (2 * (b - hidden), 2 * (b - hidden) + 1):
                            if name == "ffn":
                                act.wait_ge(s["acc_added"], m + 1)
                                square(24 + m, Fo[:, m, :])
                            else:
                                act.wait_ge(x_ready, 32 + m + 1)
                                square(64 + m, XT[:, m, :])

            with act.Fori(0, 2) as i:
                group("ffn", i, 8)
            group("ffn", 2, 6)
            norm_root(3)

            for m in range(KT):
                act.wait_ge(x_ready, 8 + m + 1)
                square(32 + m, XT[:, m, :])
            norm_root(4)
            for b in range(12):
                ahead(B0["mix"] + b)
                for t in (2 * b, 2 * b + 1):
                    take_s(T0["mix"] + t, E0["mix"] + t, ACT.Sigmoid if t < 8 and t % 2 else ACT.Copy)

            for m in range(KT):
                n, t, e = B0["gate"] + 2 * m, T0["gate"] + 5 * m, E0["gate"] + 5 * m
                ahead(n)
                take_s(t, e, ACT.Sigmoid)
                take_s(t + 1, e + 1, ACT.Sigmoid)
                ahead(n + 1)
                if m == 0:
                    for c in range(4):
                        act.wait_ge(s["la_d"], c + 1)
                        if c >= 2:
                            act.wait_ge(s["la_sum"], c - 1)
                        actv(sq[:, c % 2, :], CA[:, c, :], ACT.Square).then_inc(s["la_sq"], 1)
                    act.wait_ge(s["la_var"], 1)
                    actv(sq[:, 0, :], mb[:, 1, :], ACT.Sqrt, bias=cs("eps", 0, 1),
                         scale=2.0 / D).then_inc(s["la_sd"], 1)
                    for c in range(4):
                        act.wait_ge(s["la_y"], c + 1)
                        actv(CA[:, c, :], CA[:, c, :], ACT.Silu, bias=pr("ln_a_b", c),
                             scale=pr("ln_a_g", c)).then_inc(s["la_act"], 1)
                take_s(t + 2, e + 2, ACT.Sigmoid)
                take_s(t + 3, e + 3)
                take_s(t + 4, e + 4)

            act.wait_ge(in_mem, 16)
            for k in range(KT):
                square(40 + k, MT[:, k, :])
            for b in range(4):
                ahead(B0["o"] + b)
                for m in (2 * b, 2 * b + 1):
                    take_s(T0["o"] + m, E0["o"] + m)
                if b == 0:
                    norm_root(5, 2)
            for m in range(KT):
                act.wait_ge(x_ready, 16 + m + 1)
                square(48 + m, XT[:, m, :])

            for b in range(8):
                ahead(B0["kv"] + b)
                for j in range(2):
                    t = T0["kv"] + 2 * b + j
                    if b < 4:
                        direct(t, KX[:, 2 * b + j, :], acc[:, t % 4, 0:N_MEM])
                    else:
                        direct(t, VX[:, j, (b - 4) * 256:(b - 3) * 256], acc[:, t % 4, 0:256])
            norm_root(6)
            for b in range(4):
                ahead(B0["q"] + b)
                for j in range(2):
                    t = T0["q"] + 2 * b + j
                    direct(t, QX[:, 2 * b + j, :], acc[:, t % 4, :], 1.0 / 16.0)

            def x_exp(u):
                act.wait_ge(s["xs_mx"], u + 1)
                actv(EXx[:, u % 2, :], mb[:, u % 2, 0:N_MEM], ACT.Exp, bias=nmx[:, u % 2:u % 2 + 1],
                     accum_out=den[:, u % 2:u % 2 + 1]).then_inc(s["xs_e"], 1)

            def x_turned(u):
                h, i = divmod(u, TT)
                act.wait_ge(s["xs_t"], u + 1)
                if i == 0 and h:
                    act.wait_ge(s["xs_o"], 2 * h)
                actv(PTx[:, :, i * P:(i + 1) * P], mb[:, 2 + u % 2, 0:2 * P].rearrange("p (a b) -> p a b", a=2),
                     ACT.Copy).then_inc(s["xs_te"], 1)

            x_exp(0)
            for u in range(4 * TT):
                if u + 1 < 4 * TT:
                    x_exp(u + 1)
                x_turned(u)
                if u % TT == TT - 1:
                    h = u // TT
                    for v in range(2):
                        act.wait_ge(s["xs_o"], 2 * h + v + 1)
                        actv(XH[:, 2 * h + v, :], acc[:, v, :], ACT.Copy).then_inc(s["xs_hi"], 1)
            for b in range(4):
                ahead(B0["xo"] + b)
                for m in (2 * b, 2 * b + 1):
                    take_s(T0["xo"] + m, E0["xo"] + m)
            for m in range(KT):
                act.wait_ge(x_ready, 24 + m + 1)
                square(56 + m, XT[:, m, :])

            norm_root(7)
            act.wait_ge(s["rt_sub"], 1)
            actv(rt[:, 2, :], rt[:, 1, :], ACT.Exp).then_inc(s["rt_exp"], 1)
            act.wait_ge(s["rt_sub"], 2)
            actv(rt[:, 12, :], rt[:, 11, :], ACT.Exp).then_inc(s["rt_exp"], 1)
            with act.Fori(0, 3) as i:
                group("moe", i, 8)
            group("moe", 3, 8)
            norm_root(8)

        @block.vector
        def _(dve):
            v = nc.vector
            state = {"base": 0, "n": 0}

            def link(ins):
                state["n"] += 1
                ins.then_inc(dchain, 1)
                dve.wait_ge(dchain, state["base"] + state["n"])

            def loop(count, per, body):
                b, n = state["base"], state["n"]
                with dve.Fori(0, count) as i:
                    state["base"], state["n"] = i * per + (b + n), 0
                    body(i)
                    assert state["n"] == per, state["n"]
                state["base"], state["n"] = b, n + count * per

            def add_squares(q, w=S):
                dve.wait_ge(sq_ready, q + 1)
                if q % KT == 0:
                    v.tensor_copy(sqa[:, 0:w], sq[:, q % 2, 0:w]).then_inc(sq_used, 1)
                else:
                    dve.wait_ge(sq_used, q)
                    v.tensor_tensor(sqa[:, 0:w], sqa[:, 0:w], sq[:, q % 2, 0:w], ALU.add).then_inc(sq_used, 1)

            def norm_recip(r, nt=TT):
                dve.wait_ge(sd_ready, r + 1)
                v.reciprocal(rs[:, 0:nt], sd[:, 0:nt]).then_inc(rs_ready, 1)

            def split(src, hi, lo, done):
                link(v.tensor_copy(hi, src))
                v.tensor_tensor(lo, src, hi.bitcast(F32), ALU.subtract).then_inc(done, 1)

            def operand(r, gname):
                dve.wait_ge(rb_ready, r + 1)
                for k in range(KT):
                    link(v.scalar_tensor_tensor(out=tmp[:, k % 2, :], in0=XT[:, k, :], scalar=pr(gname, k),
                                                in1=mb[:, 1, :], op0=ALU.mult, op1=ALU.mult))
                    split(tmp[:, k % 2, :], XH[:, k, :], XL[:, k, :], xn_ready)

            def residual(r, gname, q):
                dve.wait_ge(rb_ready, r + 1)
                for m in range(KT):
                    link(v.scalar_tensor_tensor(out=tmp[:, m % 2, :], in0=Fo[:, m, :], scalar=pr(gname, m),
                                                in1=mb[:, 1, :], op0=ALU.mult, op1=ALU.mult))
                    v.tensor_tensor(XT[:, m, :], XT[:, m, :], tmp[:, m % 2, :], ALU.add).then_inc(x_ready, 1)
                    if m:
                        add_squares(q + m - 1)
                add_squares(q + KT - 1)

            link(v.memset(ev[:, :, 0:2], 0.0))

            for k in range(KT):
                add_squares(k)
            norm_recip(0)
            dve.wait_ge(in_par, 64)
            operand(0, "ln_attn_pre")
            dsts = [LO[:, :], GLO[:, :]] + [K[:, c, :] for c in range(4)] + [R[:, c, :] for c in range(4)] \
                + [V[:, c, :] for c in range(4)]
            for t, dst in enumerate(dsts):
                dve.wait_ge(evac, t + 1)
                e = ev[:, t % 4, :]
                link(v.tensor_tensor(tmp[:, t % 2, :], e[:, 1:S + 1], e[:, 2:S + 2], ALU.subtract))
                v.scalar_tensor_tensor(out=dst, in0=tmp[:, t % 2, :], scalar=pr("mu", t), in1=e[:, 2:S + 2],
                                       op0=ALU.mult, op1=ALU.add).then_inc(ev_used, 1)
            o = PO["lam"][0]
            for j in range(2):
                a, b = par[:, o + 128 * j:o + 128 * j + 64], par[:, o + 128 * j + 64:o + 128 * j + 128]
                link(v.tensor_tensor(tmp[:, 0, 64 * j:64 * j + 64], a, b, ALU.mult))
            v.tensor_reduce(lam_d, tmp[:, 0, 0:128].rearrange("p (a b) -> p a b", a=2), AX.X,
                            ALU.add).then_inc(s["lam_dot"], 1)
            dve.wait_ge(s["lam_exp"], 1)
            link(v.tensor_tensor(lam_n, lam_e[:, 1:2], lam_e[:, 0:1], ALU.subtract))
            link(v.tensor_scalar(lam_n, lam_n, -LAM_INIT, None, ALU.add))
            link(v.tensor_scalar(g08, pr("subln", 0), 1.0 - LAM_INIT, None, ALU.mult))

            def att_max(u):
                h, i = divmod(u, TT)
                w = (i + 1) * P
                slope = 2.0 ** (-8.0 * (h + 1) / 4)
                dve.wait_ge(s["at_sc"], u + 1)
                for c in range(2):
                    link(v.scalar_tensor_tensor(out=SC[:, u % 2, c, 0:w], in0=cs("alibi", S - w, S), scalar=slope,
                                                in1=mb[:, 2 * (u % 2) + c, 0:w], op0=ALU.mult, op1=ALU.add))
                x = slice(2 * (u % 2), 2 * (u % 2) + 2)
                link(v.tensor_reduce(mx[:, x], SC[:, u % 2, :, 0:w], AX.X, ALU.max))
                v.tensor_scalar(nmx[:, x], mx[:, x], -1.0, None, ALU.mult).then_inc(s["at_mx"], 1)

            def att_weights(u):
                h, i = divmod(u, TT)
                w, x = (i + 1) * P, 2 * (u % 2)
                dve.wait_ge(s["at_e"], u + 1)
                link(v.reciprocal(rden[:, x:x + 2], den[:, x:x + 2]))
                link(v.tensor_scalar(rden[:, x + 1:x + 2], rden[:, x + 1:x + 2], lam_n, None, ALU.mult))
                if u >= 2:
                    dve.wait_ge(s["at_t"], u - 1)
                link(v.tensor_scalar(APR[:, u % 2, 0:w], EX[:, u % 2, 0, 0:w], rden[:, x:x + 1], None, ALU.mult))
                v.scalar_tensor_tensor(out=APR[:, u % 2, 0:w], in0=EX[:, u % 2, 1, 0:w],
                                       scalar=rden[:, x + 1:x + 2], in1=APR[:, u % 2, 0:w], op0=ALU.mult,
                                       op1=ALU.add).then_inc(s["at_p"], 1)

            att_max(0)
            for u in range(4 * TT):
                if u + 1 < 4 * TT:
                    att_max(u + 1)
                att_weights(u)
                if u % TT == TT - 1:
                    h = u // TT
                    dve.wait_ge(s["at_sd"], h + 1)
                    link(v.reciprocal(tmp[:, 0, :], SQO[:, 1, :]))
                    v.scalar_tensor_tensor(out=OO[:, h, :], in0=acc[:, 2, :], scalar=g08, in1=tmp[:, 0, :],
                                           op0=ALU.mult, op1=ALU.mult).then_inc(s["at_done"], 1)

            def lv(l):
                return cs("mask_lv", l * P, (l + 1) * P).unsqueeze(1).to_broadcast([P, TT, P])

            def rk_head(ct, hh):
                u = 2 * ct + hh
                dve.wait_ge(s["rk_nr"], u + 1)
                mask = cs("mask_nr").unsqueeze(1).to_broadcast([P, 2, 2 * P])
                for x in range(2):
                    v.tensor_tensor(NR[:, hh, 2 * x:2 * x + 2].rearrange("p t a b -> p t (a b)"),
                                    acc[:, 2 + x, :].rearrange("p (t c) -> p t c", t=2), mask, ALU.mult)
                    last = v.tensor_tensor(AKRK[:, hh, 2 * x:2 * x + 2].rearrange("p t a b -> p t (a b)"),
                                           mb[:, x, :].rearrange("p (t c) -> p t c", t=2), mask, ALU.mult)
                last.then_inc(s["rk_nrm"], 1)
                for l in range(LEVELS):
                    dve.wait_ge(s["rk_q"], 6 * u + l + 1)
                    qp = mb[:, 2, :].rearrange("p (t c) -> p t c", t=TT)
                    if l == 0:
                        link(v.tensor_tensor(Qm[:, :, :], qp, lv(0), ALU.mult))
                        v.tensor_tensor(Tm[:, :, :], Qm[:, :, :], ident.unsqueeze(1).to_broadcast([P, TT, P]),
                                        ALU.add).then_inc(s["rk_tm"], 1)
                    else:
                        v.tensor_tensor(Qm[:, :, :], qp, lv(l), ALU.mult).then_inc(s["rk_qm"], 1)
                        dve.wait_ge(s["rk_t"], 5 * u + l)
                        v.tensor_tensor(Tm[:, :, :], Tm[:, :, :], acc[:, 2, :].rearrange("p (t c) -> p t c", t=TT),
                                        ALU.add).then_inc(s["rk_tm"], 1)
                ps = slice(HD * hh, HD * hh + HD)
                dve.wait_ge(s["rk_z"], u + 1)
                v.tensor_tensor(Z[ps, :, :], mb[ps, 2, :].rearrange("p (t c) -> p t c", t=TT), AR[ps, :, 1, :],
                                ALU.add).then_inc(s["rk_zs"], 1)

            def rk_pair(ct):
                Kc, Rc, Vc = K[:, ct, :], R[:, ct, :], V[:, ct, :]
                v.tensor_scalar(W[:, 4, :], Kc, pr("k_k", ct), None, ALU.mult).then_inc(s["rk_kk"], 1)
                dve.wait_ge(s["rk_sig"], ct + 1)
                link(v.tensor_scalar(W[:, 0, :], W[:, 0, :], -DECAY_SCALE, None, ALU.mult))
                link(v.tensor_tensor_scan(W[:, 2, :], cs("reset"), W[:, 0, :], 0.0, ALU.mult, ALU.add))
                v.tensor_tensor(W[:, 3, :], W[:, 2, :], W[:, 0, :], ALU.subtract).then_inc(s["rk_cum"], 1)
                dve.wait_ge(s["rk_kss"], ct + 1)
                v.tensor_scalar(W[:, 5, :], mb[:, 3, :], 1e-24, None, ALU.max).then_inc(s["rk_kmx"], 1)
                dve.wait_ge(s["rk_ksd"], ct + 1)
                link(v.reciprocal(W[:, 5, :], W[:, 5, :]))
                link(v.tensor_tensor(W[:, 4, :], W[:, 4, :], W[:, 5, :], ALU.mult))
                link(v.tensor_scalar(W[:, 5, :], W[:, 1, :], -1.0, pr("k_a", ct), ALU.add, ALU.mult))
                link(v.scalar_tensor_tensor(out=Kc, in0=W[:, 5, :], scalar=1.0, in1=Kc, op0=ALU.add, op1=ALU.mult))
                link(v.tensor_tensor(W[:, 1, :], W[:, 4, :], W[:, 1, :], ALU.mult))
                dve.wait_ge(s["rk_exp"], ct + 1)
                ch = lambda a: a.rearrange("p (t c) -> p t c", t=TT)
                link(v.scalar_tensor_tensor(out=AR[:, :, 0, :], in0=ch(W[:, 4, :]), scalar=-1.0, in1=ch(W[:, 3, :]),
                                            op0=ALU.mult, op1=ALU.mult))
                link(v.tensor_tensor(AR[:, :, 1, :], ch(Rc), ch(W[:, 6, :]), ALU.mult))
                link(v.tensor_tensor(BT[:, :], W[:, 1, :], W[:, 7, :], ALU.mult))
                link(v.tensor_tensor(KH[:, :], Kc, W[:, 7, :], ALU.mult))
                cw = lambda a: a.rearrange("p (c j) -> p c j", c=NCH)
                pc = cw(W[:, 6, :])[:, :, HD - 1:HD].to_broadcast([P, NCH, HD])
                link(v.tensor_tensor(cw(W[:, 0, :]), cw(BT[:, :]), pc, ALU.mult))
                link(v.tensor_tensor(cw(W[:, 2, :]), cw(KH[:, :]), pc, ALU.mult))
                v.scalar_tensor_tensor(out=W[:, 3, :], in0=Rc, scalar=pr("r_k", ct), in1=Kc, op0=ALU.mult,
                                       op1=ALU.mult).then_inc(s["rk_hat"], 1)
                dve.wait_ge(s["rk_bsum"], ct + 1)
                v.tensor_tensor(BON[:, :], acc[:, 0, :], Vc, ALU.mult).then_inc(s["rk_bonus"], 1)
                rk_head(ct, 0)
                rk_head(ct, 1)
                dve.wait_ge(s["rk_gh"], 2 * ct + 2)
                link(v.tensor_tensor(GT[:, :, :], cs("id64").unsqueeze(1).to_broadcast([P, NCH, HD]), pc, ALU.mult))
                g2 = GT[:, :, :].rearrange("p (t a) j -> p a t j", a=2)
                dve.wait_ge(s["rk_hs"], ct + 1)
                v.tensor_tensor(g2, g2, acc[:, 0:2, 0:256].rearrange("p a (t j) -> p a t j", t=TT),
                                ALU.add).then_inc(s["rk_gs"], 1)
                v.tensor_copy(ST[:, 1, :], HS[:, 0, :]).then_inc(s["rk_st"], 1)
                for c in range(2, NCH):
                    dve.wait_ge(s["rk_s"], 6 * ct + c - 1)
                    v.tensor_tensor(ST[:, c, :], mb[:, 3, 0:HD], HS[:, c - 1, :], ALU.add).then_inc(s["rk_st"], 1)
                dve.wait_ge(s["rk_y"], ct + 1)
                v.tensor_tensor(W[:, 0, :], mb[:, 0, :], BON[:, :], ALU.add).then_inc(s["rk_ys"], 1)
                dve.wait_ge(s["rk_mu"], ct + 1)
                v.scalar_tensor_tensor(out=W[:, 1, :], in0=mb[:, 1, :], scalar=-1.0 / HD, in1=W[:, 0, :],
                                       op0=ALU.mult, op1=ALU.add).then_inc(s["rk_d"], 1)
                dve.wait_ge(s["rk_sd"], ct + 1)
                link(v.reciprocal(W[:, 3, :], W[:, 3, :]))
                link(v.tensor_tensor(W[:, 1, :], W[:, 1, :], W[:, 3, :], ALU.mult))
                link(v.tensor_scalar(W[:, 1, :], W[:, 1, :], pr("ln_x_w", ct), pr("ln_x_b", ct), ALU.mult, ALU.add))
                v.tensor_tensor(Rc, W[:, 1, :], G[:, :], ALU.mult).then_inc(s["rk_done"], 1)

            for ct in range(4):
                rk_pair(ct)

            dve.wait_ge(s["rk_done"], 4)
            for k in range(KT):
                src = R[:, k, :] if k < 4 else OO[:, k - 4, :]
                split(src, XH[:, k, :], XL[:, k, :], s["mixed"])
            for m in range(KT):
                add_squares(8 + m)
            norm_recip(1)
            dve.wait_ge(in_x2, 16)
            residual(1, "ln_attn_post", 16)

            def conv3(dst, e, w, b=None, done=None):
                if b is None:
                    link(v.tensor_scalar(dst, e[:, 2:S + 2], w[2], None, ALU.mult))
                else:
                    link(v.tensor_scalar(dst, e[:, 2:S + 2], w[2], b, ALU.mult, ALU.add))
                link(v.scalar_tensor_tensor(out=dst, in0=e[:, 1:S + 1], scalar=w[1], in1=dst, op0=ALU.mult,
                                            op1=ALU.add))
                return v.scalar_tensor_tensor(out=dst, in0=e[:, 0:S], scalar=w[0], in1=dst, op0=ALU.mult, op1=ALU.add)

            def group(name, i, hidden, last=False):
                loop_i = not isinstance(i, int)
                k = 0 if loop_i else i
                t0, e0 = T0[name] + 24 * k, E0[name] + 24 * k
                add = (lambda x, per: i * per + x) if loop_i else (lambda x, per: x)
                h0 = {"ffn": 0, "moe": 22}[name] + 8 * k
                if name == "ffn":
                    src = par[:, PO["conv"][0] + 64 * i:PO["conv"][0] + 64 * i + 64] if not loop_i else \
                        par[:, bass.ds(i * 64 + PO["conv"][0], 64)]
                    link(v.tensor_copy(cpar[:, :], src))
                else:
                    gsrc = gateg[:, :, :, :].rearrange("p g t e -> p (g t e)")
                    src = gsrc[:, 16 * i:16 * i + 16] if not loop_i else gsrc[:, bass.ds(i * 16, 16)]
                    v.tensor_copy(gcur[:, :, :].rearrange("p t e -> p (t e)"), src).then_inc(s["gate_ready"], 1)
                for b in range(hidden):
                    dve.wait_ge(evac, add(t0 + 2 * b + 1, 24))
                    ea, eb = ev[:, (e0 + 2 * b) % 4, :], ev[:, (e0 + 2 * b + 1) % 4, :]
                    if name == "ffn":
                        c = [cpar[:, 8 * b + x:8 * b + x + 1] for x in range(8)]
                        conv3(gl[:, b % 2, :], ea, c[0:3], c[3]).then_inc(ev_used, 1)
                        dve.wait_ge(evac, add(t0 + 2 * b + 2, 24))
                        conv3(yv[:, b % 2, :], eb, c[4:7], c[7]).then_inc(ev_used, 1)
                        dve.wait_ge(ev_used, add(e0 + 2 * b + 2, 24))
                        dve.wait_ge(s["gelu_done"], add(8 * k + b + 1, 8))
                        link(v.tensor_tensor(tmp[:, b % 2, :], gl[:, b % 2, :], yv[:, b % 2, :], ALU.mult))
                    else:
                        dve.wait_ge(evac, add(t0 + 2 * b + 2, 24))
                        v.tensor_tensor(gl[:, b % 2, :], ea[:, 2:S + 2], eb[:, 2:S + 2],
                                        ALU.mult).then_inc(ev_used, 2)
                        dve.wait_ge(ev_used, add(e0 + 2 * b + 2, 24))
                        dve.wait_ge(s["gb_ready"], add(4 * k + b // 2 + 1, 4))
                        link(v.tensor_tensor(tmp[:, b % 2, :], gl[:, b % 2, :], mb[:, 2 + b // 2 % 2, :], ALU.mult))
                    split(tmp[:, b % 2, :], HH[:, b, :], HL[:, b, :], s["hid_ready"])
                dst = Fo if name == "ffn" else XT
                for m in range(KT):
                    dve.wait_ge(evac, add(t0 + 2 * hidden + m + 1, 24))
                    e = ev[:, (e0 + 2 * hidden + m) % 4, 2:S + 2]
                    link(v.tensor_tensor(dst[:, m, :], dst[:, m, :], e, ALU.add))
                    v.nop().then_inc(ev_used, 1)
                    if last:
                        v.nop().then_inc(s["acc_added"] if name == "ffn" else x_ready, 1)
                        if m:
                            add_squares((24 if name == "ffn" else 64) + m - 1)
                if last:
                    add_squares((24 if name == "ffn" else 64) + KT - 1)

            norm_recip(2)
            operand(2, "ln_ffn_pre")
            link(v.memset(Fo[:, :, :], 0.0))
            loop(2, 1 + 8 * 6 + 8, lambda i: group("ffn", i, 8))
            group("ffn", 2, 6, last=True)
            norm_recip(3)
            residual(3, "ln_ffn_post", 32)
            norm_recip(4)
            operand(4, "norm_mix")
            link(v.memset(APAD[:, :, 0:CONV_A - 1], 0.0))
            link(v.memset(cpad[:, 0:2], 0.0))
            link(v.memset(upad[:, :, 0:POOL_PAD], 0.0))
            t0, e0 = T0["mix"], E0["mix"]
            for c in range(4):
                dve.wait_ge(evac, t0 + 2 * c + 2)
                v.tensor_tensor(APAD[:, c, CONV_A - 1:], ev[:, (e0 + 2 * c) % 4, 2:S + 2],
                                ev[:, (e0 + 2 * c + 1) % 4, 2:S + 2], ALU.mult).then_inc(ev_used, 2)
            dve.wait_ge(ev_used, e0 + 8)

            taps = [(c, j) for j in range(CONV_A) for c in range(4)]

            def tap():
                c, j = taps.pop(0)
                x, w = APAD[:, c, j:j + S], pr("conv_a_w", c * CONV_A + j)
                if j == 0:
                    link(v.tensor_scalar(CA[:, c, :], x, w, pr("conv_a_b", c), ALU.mult, ALU.add))
                else:
                    link(v.scalar_tensor_tensor(out=CA[:, c, :], in0=x, scalar=w, in1=CA[:, c, :],
                                                op0=ALU.mult, op1=ALU.add))

            for c in range(4):
                t, e = t0 + 8 + 3 * c, e0 + 8 + 3 * c
                for _ in range(16):
                    tap()
                dve.wait_ge(evac, t + 2)
                v.tensor_tensor(cpad[:, 2:], ev[:, e % 4, 2:S + 2], ev[:, (e + 1) % 4, 2:S + 2],
                                ALU.mult).then_inc(ev_used, 2)
                dve.wait_ge(ev_used, e + 2)
                link(conv3(tmp[:, 0, :], cpad, [pr("conv_c", 3 * c + x) for x in range(3)]))
                dve.wait_ge(evac, t + 3)
                v.tensor_tensor(tmp[:, 1, :], tmp[:, 0, :], ev[:, (e + 2) % 4, 2:S + 2],
                                ALU.mult).then_inc(ev_used, 1)
                dve.wait_ge(ev_used, e + 3)
                split(tmp[:, 1, :], CH[:, c, :], CL[:, c, :], dchain)
                state["n"] += 1
                for _ in range(8):
                    tap()
            for g in range(4):
                t, e = t0 + 20 + g, e0 + 20 + g
                for _ in range(7):
                    tap()
                dve.wait_ge(evac, t + 1)
                x = ev[:, e % 4, :]
                cur, oth = upad[:, 0, :], upad[:, 1, :]
                link(v.tensor_tensor(cur[:, POOL_PAD:], x[:, 2:S + 2], x[:, 1:S + 1], ALU.add))
                for step in [2, 4, 8][:g]:
                    link(v.tensor_tensor(oth[:, POOL_PAD:], cur[:, POOL_PAD:],
                                         cur[:, POOL_PAD - step:POOL_PAD - step + S], ALU.add))
                    cur, oth = oth, cur
                link(v.scalar_tensor_tensor(out=PL[:, g, :], in0=cur[:, POOL_PAD:], scalar=0.5 ** (g + 1),
                                            in1=x[:, 2:S + 2], op0=ALU.mult, op1=ALU.subtract))
                link(v.tensor_tensor(tmp[:, 0, 0:POOL_PAD], cur[:, POOL_PAD:2 * POOL_PAD],
                                     cs("invcnt", g * POOL_PAD, (g + 1) * POOL_PAD), ALU.mult))
                v.tensor_tensor(PL[:, g, 0:POOL_PAD], tmp[:, 0, 0:POOL_PAD], x[:, 2:POOL_PAD + 2],
                                ALU.subtract).then_inc(ev_used, 1)
                dve.wait_ge(ev_used, e + 1)
            while taps:
                tap()

            link(v.tensor_tensor(sqa[:, :], CA[:, 0, :], CA[:, 1, :], ALU.add))
            link(v.tensor_tensor(sqa[:, :], sqa[:, :], CA[:, 2, :], ALU.add))
            v.tensor_tensor(sqa[:, :], sqa[:, :], CA[:, 3, :], ALU.add).then_inc(s["la_in"], 1)
            dve.wait_ge(s["la_mu"], 1)
            for c in range(4):
                v.scalar_tensor_tensor(out=CA[:, c, :], in0=mb[:, 0, :], scalar=-2.0 / D, in1=CA[:, c, :],
                                       op0=ALU.mult, op1=ALU.add).then_inc(s["la_d"], 1)
            for c in range(4):
                dve.wait_ge(s["la_sq"], c + 1)
                if c == 0:
                    v.tensor_copy(sqa[:, :], sq[:, 0, :]).then_inc(s["la_sum"], 1)
                else:
                    dve.wait_ge(s["la_sum"], c)
                    v.tensor_tensor(sqa[:, :], sqa[:, :], sq[:, c % 2, :], ALU.add).then_inc(s["la_sum"], 1)
            dve.wait_ge(s["la_sd"], 1)
            link(v.reciprocal(tmp[:, 0, :], sq[:, 0, :]))
            for c in range(4):
                v.tensor_tensor(CA[:, c, :], CA[:, c, :], tmp[:, 0, :], ALU.mult).then_inc(s["la_y"], 1)
            for c in range(4):
                dve.wait_ge(s["la_act"], c + 1)
                split(CA[:, c, :], AH[:, c, :], AL[:, c, :], s["ac_ready"])
            dve.wait_ge(s["ac_ready"], 4)
            for m in range(KT):
                t, e = T0["gate"] + 5 * m, E0["gate"] + 5 * m
                tile = lambda x: ev[:, (e + x) % 4, 2:S + 2]
                dve.wait_ge(s["p_mm"], m + 1)
                dve.wait_ge(evac, t + 2)
                link(v.scalar_tensor_tensor(out=tmp[:, 0, :], in0=mb[:, 2 + m % 2, :], scalar=pr("pool_scale", m),
                                            in1=tile(1), op0=ALU.mult, op1=ALU.mult))
                dve.wait_ge(evac, t + 4)
                v.tensor_tensor(tmp[:, 1, :], tile(0), tile(3), ALU.mult).then_inc(ev_used, 2)
                dve.wait_ge(ev_used, e + 2)
                link(v.tensor_tensor(MG[:, m, :], tmp[:, 0, :], tmp[:, 1, :], ALU.add))
                dve.wait_ge(evac, t + 5)
                v.tensor_tensor(tmp[:, 1, :], tile(2), tile(4), ALU.mult).then_inc(ev_used, 3)
                dve.wait_ge(ev_used, e + 5)
                v.tensor_tensor(MG[:, m, :], MG[:, m, :], tmp[:, 1, :], ALU.add).then_inc(s["mg_ready"], 1)

            def add_tile(name, m):
                dve.wait_ge(evac, T0[name] + m + 1)
                link(v.tensor_tensor(XT[:, m, :], XT[:, m, :], ev[:, (E0[name] + m) % 4, 2:S + 2], ALU.add))
                v.nop().then_inc(ev_used, 1)
                v.nop().then_inc(x_ready, 1)

            dve.wait_ge(s["mg_ready"], KT)
            for k in range(KT):
                split(MG[:, k, :], XH[:, k, :], XL[:, k, :], s["mg_ready"])
            for k in range(KT):
                add_squares(40 + k, N_MEM)
            add_tile("o", 0)
            add_tile("o", 1)
            norm_recip(5, 2)
            add_tile("o", 2)
            add_tile("o", 3)
            dve.wait_ge(rb_ready, 6)
            for k in range(KT):
                link(v.scalar_tensor_tensor(out=tmp[:, k % 2, 0:N_MEM], in0=MT[:, k, :], scalar=pr("norm_mem", k),
                                            in1=mb[:, 1, 0:N_MEM], op0=ALU.mult, op1=ALU.mult))
                split(tmp[:, k % 2, 0:N_MEM], MH[:, k, :], ML[:, k, :], s["mem_ready"])
            for m in range(4, KT):
                add_tile("o", m)
            for m in range(KT):
                add_squares(48 + m)

            def x_max(u):
                dve.wait_ge(s["xs_sc"], u + 1)
                link(v.tensor_reduce(mx[:, u % 2:u % 2 + 1], mb[:, u % 2, 0:N_MEM], AX.X, ALU.max))
                v.tensor_scalar(nmx[:, u % 2:u % 2 + 1], mx[:, u % 2:u % 2 + 1], -1.0, None,
                                ALU.mult).then_inc(s["xs_mx"], 1)

            def x_weights(u):
                dve.wait_ge(s["xs_e"], u + 1)
                link(v.reciprocal(rden[:, u % 2:u % 2 + 1], den[:, u % 2:u % 2 + 1]))
                if u >= 2:
                    dve.wait_ge(s["xs_t"], u - 1)
                v.tensor_scalar(PX[:, u % 2, :], EXx[:, u % 2, :], rden[:, u % 2:u % 2 + 1], None,
                                ALU.mult).then_inc(s["xs_p"], 1)

            norm_recip(6)
            operand(6, "norm_x")
            x_max(0)
            for u in range(4 * TT):
                if u + 1 < 4 * TT:
                    x_max(u + 1)
                x_weights(u)
                if u % TT == TT - 1:
                    h = u // TT
                    for j in range(2):
                        dve.wait_ge(s["xs_hi"], 2 * h + j + 1)
                        v.tensor_tensor(XL[:, 2 * h + j, :], acc[:, j, :], XH[:, 2 * h + j, :].bitcast(F32),
                                        ALU.subtract).then_inc(s["xs_done"], 1)
            for m in range(KT):
                add_tile("xo", m)
            for m in range(KT):
                add_squares(56 + m)

            def route():
                r = lambda j: rt[:, j, :].rearrange("p (t c) -> p t c", t=TT)
                red = lambda j: rt[:, j, 0:TT]
                wide = lambda j: rt[:, j, 0:TT].unsqueeze(2).to_broadcast([P, TT, 4])
                rank = cs("rank").unsqueeze(1).to_broadcast([P, TT, 4])

                def best(p, eq, top, hot):
                    link(v.tensor_reduce(red(top), r(p), AX.X, ALU.max))
                    link(v.tensor_tensor(r(eq), r(p), wide(top), ALU.is_equal))
                    link(v.tensor_tensor(r(eq), r(eq), rank, ALU.mult))
                    link(v.tensor_reduce(red(23), r(eq), AX.X, ALU.max))
                    link(v.tensor_tensor(r(hot), r(eq), wide(23), ALU.is_equal))

                def softmax_in(src, to):
                    link(v.tensor_reduce(red(0), src, AX.X, ALU.max))
                    v.tensor_tensor(r(to), src, wide(0), ALU.subtract).then_inc(s["rt_sub"], 1)

                def softmax_out(p):
                    link(v.tensor_reduce(red(0), r(p), AX.X, ALU.add))
                    link(v.reciprocal(red(22), red(0)))
                    link(v.tensor_tensor(r(p), r(p), wide(22), ALU.mult))

                dve.wait_ge(s["rt_lg"], 1)
                link(v.tensor_tensor(lg[:, :, :], mb[:, 0, 0:TT * 20].rearrange("p (t c) -> p t c", t=TT),
                                     pr("b_router", 0, 20).unsqueeze(1).to_broadcast([P, TT, 20]), ALU.add))
                softmax_in(lg[:, :, 0:4], 1)
                dve.wait_ge(s["rt_exp"], 1)
                softmax_out(2)
                best(2, 3, 4, 5)
                for t in range(TT):
                    link(v.tensor_tensor(rt3[:, t], lg[:, t, 4:20].rearrange("p (g e) -> p g e", g=4),
                                         rt[:, 5, 4 * t:4 * t + 4].unsqueeze(2).to_broadcast([P, 4, 4]), ALU.mult))
                link(v.tensor_reduce(r(10), rt3[:, :, :, :].rearrange("p t g e -> p t e g"), AX.X, ALU.add))
                softmax_in(r(10), 11)
                dve.wait_ge(s["rt_exp"], 2)
                softmax_out(12)
                best(12, 13, 14, 15)
                link(v.scalar_tensor_tensor(out=r(16), in0=r(15), scalar=-2.0, in1=r(12), op0=ALU.mult, op1=ALU.add))
                best(16, 13, 17, 18)
                link(v.tensor_tensor(red(19), red(14), red(17), ALU.add))
                link(v.reciprocal(red(20), red(19)))
                link(v.tensor_tensor(red(20), red(20), red(4), ALU.mult))
                link(v.tensor_tensor(r(15), r(15), r(18), ALU.add))
                link(v.tensor_tensor(r(15), r(15), r(12), ALU.mult))
                link(v.tensor_tensor(r(15), r(15), wide(20), ALU.mult))
                for g in range(4):
                    link(v.tensor_tensor(gateg[:, g], r(15), r(5)[:, :, g:g + 1].to_broadcast([P, TT, 4]), ALU.mult))

            o = PO["w_router"][0]
            wr = par[:, o:o + KT * 20].rearrange("p (k c) -> p k c", k=KT)
            split(wr, wrh[:, :, :], wrl[:, :, :], s["wr_ready"])
            norm_recip(7)
            operand(7, "norm_ffn")
            route()
            loop(3, 16 + 8, lambda i: group("moe", i, 8))
            group("moe", 3, 8, last=True)
            norm_recip(8)
            dve.wait_ge(rb_ready, 9)
            for m in range(KT):
                v.scalar_tensor_tensor(out=XT[:, m, :], in0=XT[:, m, :], scalar=pr("norm_f", m), in1=mb[:, 1, :],
                                       op0=ALU.mult, op1=ALU.mult).then_inc(s["final_ready"], 1)



def pack(inputs):
    import numpy as np

    g = {n: np.asarray(a) for n, a in inputs.items()}
    W = {n: g[n][0] for n in ("w_in", "w_out", "w_up", "w_down", "w_in_2", "w_a_out_2", "w_c_out_2", "w_o_2",
                              "w_xq_2", "w_xkv_2", "w_xo_2", "w_e_gate_2", "w_e_up_2", "w_e_down_2")}

    def tile(w, c):
        t = w[:, c:c + P].reshape(-1, P, P).transpose(1, 0, 2)
        if t.shape[1] < KT:
            t = np.concatenate([t, np.zeros((P, KT - t.shape[1], P), t.dtype)], axis=1)
        return t

    tiles = []
    order = [12 * P, 13 * P] + [c * P for c in (4, 5, 6, 7, 0, 1, 2, 3, 8, 9, 10, 11)] \
        + [c * P for c in range(14, 26)]
    tiles += [tile(W["w_in"], c) for c in order]
    tiles += [tile(W["w_out"], m * P) for m in range(KT)]
    for a, b in ((0, 8), (8, 16), (16, 22)):
        for h in range(a, b):
            tiles += [tile(W["w_up"], h * P), tile(W["w_up"], D_FF + h * P)]
        tiles += [tile(W["w_down"][a * P:b * P], m * P) for m in range(KT)]
    w2 = W["w_in_2"]
    for c in range(4):
        tiles += [tile(w2, c * P), tile(w2, 512 + c * P)]
    for c in range(4):
        tiles += [tile(w2, o + c * P) for o in (2560, 1536, 2048)]
    tiles += [tile(w2, 1024 + c * P) for c in range(4)]
    for m in range(KT):
        tiles += [tile(w2, 3072 + x * D + m * P) for x in range(3)]
        tiles.append(np.concatenate([tile(W["w_a_out_2"], m * P)[:, :4], tile(W["w_c_out_2"], m * P)[:, :4]], axis=1))
    tiles += [tile(W["w_o_2"], m * P) for m in range(KT)]
    tiles += [tile(W["w_xkv_2"], m * P) for m in range(2 * KT)]
    tiles += [tile(W["w_xq_2"], m * P) for m in range(KT)]
    tiles += [tile(W["w_xo_2"], m * P) for m in range(KT)]
    down = W["w_e_down_2"].reshape(-1, D)
    for q in range(4):
        for e in range(4 * q, 4 * q + 4):
            for c in range(2):
                tiles += [tile(W["w_e_gate_2"][e], c * P), tile(W["w_e_up_2"][e], c * P)]
        tiles += [tile(down[q * D:(q + 1) * D], m * P) for m in range(KT)]
    ws = np.stack(tiles).reshape(NBLK, 2, P, KT, P).transpose(0, 2, 3, 1, 4)
    ws = np.ascontiguousarray(ws).reshape(NBLK, P, BLK)

    def cols(a):
        return np.asarray(a).reshape(-1, P).T

    def rows(a):
        return np.broadcast_to(np.asarray(a).reshape(1, -1), (P, np.asarray(a).size))

    mu = cols(g["mu_shift"][0])
    cw, cb = g["conv_w"][0], g["conv_b"][0]
    conv = []
    for h in range(22):
        for o in (0, D_FF):
            conv += [cw[x, o + h * P:o + (h + 1) * P] for x in range(3)] + [cb[o + h * P:o + (h + 1) * P]]
    conv = np.stack(conv + [np.zeros(P, cw.dtype)] * 16, axis=1)
    ca = np.concatenate([g["conv_a_w_2"][0][:, c * P:(c + 1) * P].T for c in range(4)], axis=1)
    cc = np.concatenate([g["conv_c_w_2"][0][:, c * P:(c + 1) * P].T for c in range(4)], axis=1)
    router = np.concatenate([g["w_rg_2"][0], g["w_re_2"][0]], axis=1)
    router = router.reshape(KT, P, 20).transpose(1, 0, 2).reshape(P, KT * 20)
    par = {
        "ln_attn_pre": cols(g["ln_attn_pre"]), "mu": mu[:, [12, 13, 4, 5, 6, 7, 0, 1, 2, 3, 8, 9, 10, 11]],
        "w_decay0": cols(g["w_decay0"]), "w_iclr0": cols(g["w_iclr0"]), "k_k": cols(g["k_k"]),
        "k_a": cols(g["k_a"]), "r_k": cols(g["r_k"]), "ln_x_w": cols(g["ln_x_w"]), "ln_x_b": cols(g["ln_x_b"]),
        "subln": cols(g["diff_subln"]), "ln_attn_post": cols(g["ln_attn_post"]),
        "ln_ffn_pre": cols(g["ln_ffn_pre"]), "conv": conv, "ln_ffn_post": cols(g["ln_ffn_post"]),
        "norm_mix": cols(g["norm_mix_g_2"]), "conv_a_w": ca, "conv_a_b": cols(g["conv_a_b_2"]),
        "ln_a_g": cols(g["ln_a_g_2"]), "ln_a_b": cols(g["ln_a_b_2"]), "pool_scale": cols(g["pool_scale_2"]),
        "conv_c": cc, "norm_x": cols(g["norm_x_g_2"]), "norm_mem": cols(g["norm_mem_g_2"]),
        "norm_ffn": cols(g["norm_ffn_g_2"]), "norm_f": cols(g["norm_f_g_2"]), "w_router": router,
        "b_router": np.concatenate([rows(g["b_rg_2"]), rows(g["b_re_2"])], axis=1),
        "lam": np.concatenate([rows(g[n]) for n in ("lambda_q1", "lambda_k1", "lambda_q2", "lambda_k2")], axis=1),
    }
    params = np.ascontiguousarray(np.concatenate([par[n] for n, _ in PCOLS], axis=1))
    lora = np.stack([np.concatenate([g["w_decay_up"][0], g["w_iclr_up"][0]], axis=0), g["w_gate_up"][0]], axis=1)
    xT = g["x"][0].T.reshape(KT, P, S).transpose(1, 0, 2)
    memT = g["mem_2"][0].T.reshape(KT, P, N_MEM).transpose(1, 0, 2)
    poolw = g["w_pool_grp_2"][0].transpose(1, 0, 2)
    return {k: np.ascontiguousarray(a) for k, a in
            dict(xT=xT, memT=memT, wstream=ws, params=params, consts=constants(), lora=lora, poolw=poolw).items()}


def constants():
    import numpy as np

    i, j = np.arange(P)[:, None], np.arange(P)[None, :]
    c = np.arange(S)[None, :] - (S - P)
    same = i // HD == j // HD
    lv = [((i >> l) % 2 == 1) & ((j >> l) % 2 == 0) & (i >> (l + 1) == j >> (l + 1)) for l in range(LEVELS)]
    cnt = [np.minimum(np.arange(POOL_PAD) + 1, 2 ** (g + 1)) for g in range(4)]
    eps = np.broadcast_to(np.array([[1e-6, 1e-5, 64e-5, 0.0]]), (P, 4))
    tab = {
        "ident": i == j, "ones": np.ones((P, P)), "blk": same, "alibi": np.where(c <= i, c - i, -1e30),
        "mask_nr": np.concatenate([same & (i < j), same & (i <= j)], axis=1),
        "mask_lv": np.concatenate(lv, axis=1), "reset": np.broadcast_to(np.arange(S)[None] % HD != 0, (P, S)),
        "id64": i % HD == np.arange(HD)[None], "invcnt": np.broadcast_to(1.0 / np.concatenate(cnt)[None], (P, 64)),
        "rank": np.broadcast_to(np.array([[4, 3, 2, 1]]), (P, 4)), "eps": eps,
    }
    return np.concatenate([tab[n].astype(np.float32) for n, _ in CCOLS], axis=1)


def kernel(**inputs):
    import numpy as np
    import concourse.bacc as bacc
    from concourse.bass_utils import run_bass_kernel_spmd

    arrays = pack(inputs)
    nc = bacc.Bacc("TRN2", target_bir_lowering=False, num_devices=1)
    aps = {n: nc.dram_tensor(n, a.shape, F32, kind="ExternalInput").ap() for n, a in arrays.items()}
    out = nc.dram_tensor("out", (P, KT, S), F32, kind="ExternalOutput").ap()
    build(nc, out=out, **aps)
    r = run_bass_kernel_spmd(nc, [arrays], core_ids=[0])
    got = r.results[0]["out"]
    return np.ascontiguousarray(got.transpose(2, 1, 0)).reshape(1, S, D)
```

```python
import math
from contextlib import ExitStack

import concourse.bass as bass
from concourse import mybir

F32 = mybir.dt.float32
F32R = mybir.dt.float32r
ALU = mybir.AluOpType
ACT = mybir.ActivationFunctionType
AX = mybir.AxisListType

P = 128
D = 1024
S = 512
KT = D // P
TT = S // P
HD = 64
NCH = S // HD
LEVELS = 6
D_FF = 2816
N_MEM = 256
DECAY_SCALE = math.exp(-0.5)
LAM_INIT = 0.8 - 0.6 * math.exp(-0.3 * 0)
CONV_A = 31
TAPS = 14
POOL_PAD = 16
RING = 4
K_DVE = 3
BLK = KT * 2 * P

STAGES = [("in", 13, 26, 14), ("out", 4, 8, 0), ("ffn", 34, 68, 68), ("mix", 12, 24, 24), ("gate", 16, 40, 40),
          ("o", 4, 8, 8), ("kv", 8, 16, 0), ("q", 4, 8, 0), ("xo", 4, 8, 8), ("moe", 48, 96, 96)]
B0, T0, E0, TILES_TO = {}, {}, {}, []
_b = _t = _e = 0
for _name, _nb, _nt, _ne in STAGES:
    B0[_name], T0[_name], E0[_name] = _b, _t, _e
    for _i in range(_nb):
        _per = (2 if _i % 2 == 0 else 3) if _name == "gate" else 2
        _t += _per
        TILES_TO.append(_t)
    _b, _e = _b + _nb, _e + _ne
    assert _t == T0[_name] + _nt
NBLK, NTILE = _b, _t

PCOLS = [("ln_attn_pre", 8), ("mu", 14), ("w_decay0", 4), ("w_iclr0", 4), ("k_k", 4), ("k_a", 4), ("r_k", 4),
         ("ln_x_w", 4), ("ln_x_b", 4), ("subln", 1), ("ln_attn_post", 8), ("ln_ffn_pre", 8), ("conv", 8 * 24),
         ("ln_ffn_post", 8), ("norm_mix", 8), ("conv_a_w", 4 * CONV_A), ("conv_a_b", 4), ("ln_a_g", 4),
         ("ln_a_b", 4), ("pool_scale", 8), ("conv_c", 12), ("norm_x", 8), ("norm_mem", 8), ("norm_ffn", 8),
         ("norm_f", 8), ("w_router", KT * 20), ("b_router", 20), ("lam", 4 * HD)]
CCOLS = [("ident", P), ("ones", P), ("blk", P), ("alibi", S), ("mask_nr", 2 * P), ("mask_lv", LEVELS * P),
         ("reset", S), ("id64", HD), ("invcnt", 4 * POOL_PAD), ("rank", 4), ("eps", 4),
         ("upto", P), ("count", P)]


BEATS = ["tok", "nr", "ak", "l0", "l1", "l2", "l3", "l4", "l5", "wu", "gh", "s2", "s3", "s4", "s5", "s6", "s7",
         "y", "mu", "var"]
SIDE = {"tok": ["scores0", "max0"], "nr": ["exp0", "weights0"], "ak": ["turn0", "turned0", "scores1"],
        "l0": ["max1", "exp1"], "l1": ["weights1", "turn1"], "l2": ["turned1", "scores2"], "l3": ["max2", "exp2"],
        "l4": ["weights2", "turn2"], "l5": ["turned2", "scores3"], "wu": ["max3", "exp3"], "gh": ["weights3"],
        "s2": ["turn3", "up"], "s3": ["turned3", "out", "decay", "up_gate"], "s4": ["square", "sums", "keys", "scaled"],
        "s5": ["norm", "key_norm", "decays"], "s6": ["hats"], "y": ["hat"], "mu": ["ends"]}


def offsets(cols):
    at, out = 0, {}
    for name, w in cols:
        out[name] = (at, w)
        at += w
    return out, at


PO, NPAR = offsets(PCOLS)
CO, NCST = offsets(CCOLS)


def build(nc, xT, memT, wstream, params, consts, lora, poolw, out):
    with ExitStack() as ctx:
        def sem(name):
            return ctx.enter_context(nc.semaphore(name))

        top = [nc.sbuf_base + (-nc.sbuf_base) % 64]
        KB = 1024

        def at(name, shape, offset, dt=F32):
            assert offset + 4 * math.prod(shape) <= nc.sbuf_usable_end, name
            return nc.alloc_sbuf_tensor_at(name, [P, *shape], dt, offset=offset)

        top_of = {}

        def sb(name, shape, dt=F32):
            top_of[name] = top[0]
            t = at(name, shape, top[0], dt)
            top[0] += -(-4 * math.prod(shape) // 64) * 64
            return t

        raw = sb("raw", [RING, BLK])
        wh = sb("wh", [RING, KT, 2, P], F32R)
        wl = at("wl", [RING, KT, 2, P], top_of["raw"], F32R)
        cst = sb("cst", [NCST])
        par = sb("par", [NPAR])
        pw = sb("pw", [4, 2 * P])
        ev = sb("ev", [4, S + 2])
        tmp = sb("tmp", [2, S])
        sq = sb("sq", [2, S])
        sqa = sb("sqa", [S])
        sml = sb("sml", [64])
        rs, sd = sml[:, 0:4], sml[:, 4:8]
        lam_d, lam_e, lam_n, g08 = sml[:, 8:10], sml[:, 10:12], sml[:, 12:13], sml[:, 13:14]
        mx = sml[:, 16:20]
        nmx = sml[:, 20:24]
        den = sml[:, 24:28]
        rden = sml[:, 28:32]
        xt_off = top[0]
        XT = sb("XT", [KT, S])
        x_off = top[0]
        XH = sb("XH", [KT, S], F32R)
        XL = sb("XL", [KT, S], F32R)
        ar = top[0]

        R = at("R", [4, S], ar)
        K = at("K", [4, S], ar + 8 * KB)
        V = at("V", [4, S], ar + 16 * KB)
        LO = at("LO", [S], ar + 24 * KB)
        GLO = at("GLO", [S], ar + 26 * KB)
        OO = at("OO", [4, S], ar + 28 * KB)
        lor = at("lor", [2, S], ar + 36 * KB)
        QT = at("QT", [4, S], ar + 40 * KB)
        KD = at("KD", [4, S], xt_off)
        DV = at("DV", [TT, S], xt_off + 8 * KB)
        SC = at("SC", [2, 2, S], ar + 48 * KB)
        SQO = sq
        ring = top_of["raw"] + 16 * KB
        AT = at("AT", [TT, S], ring + 40 * KB)
        Wt = [at("Wr", [8, S], top_of["raw"]), at("Wx", [8, S], x_off)]
        AR = at("AR", [TT, 2, P], x_off + 16 * KB)
        BT = at("BT", [S], x_off + 20 * KB)
        KH = at("KH", [S], x_off + 22 * KB)
        BON = at("BON", [S], x_off + 24 * KB)
        AXb = at("AXb", [TT, 2, 2, HD], x_off + 28 * KB)
        Btok = at("Btok", [TT, P], ring)
        Ktok = at("Ktok", [TT, P], ring + 2 * KB)
        Vtok = at("Vtok", [TT, P], ring + 4 * KB)
        Z = at("Z", [TT, P], ring + 6 * KB)
        NR = at("NR", [2, TT, 2, P], ring + 8 * KB)
        AKRK = at("AKRK", [2, TT, 2, P], ring + 16 * KB)
        Qm = at("Qm", [2, TT, P], ring + 24 * KB)
        Tm = at("Tm", [2, TT, P], ring + 28 * KB)
        TTm = at("TTm", [2, TT, P], ring + 32 * KB)
        WU = at("WU", [2, TT, P], ring + 36 * KB)
        wo = [top_of["raw"], x_off]
        GTt = [at(f"GT{i}", [NCH, HD], wo[i] + 10 * KB) for i in range(2)]
        STt = [at(f"ST{i}", [NCH, HD], wo[i] + 8 * KB) for i in range(2)]
        HSt = [at(f"HS{i}", [NCH, HD], wo[i] + 14 * KB) for i in range(2)]
        Fo = at("Fo", [KT, S], ar + 32 * KB)
        HH = at("HH", [KT, S], ar, F32R)
        HL = at("HL", [KT, S], ar + 16 * KB, F32R)
        gl = at("gl", [2, S], ar + 48 * KB)
        yv = at("yv", [2, S], ar + 52 * KB)
        cpar = at("cpar", [64], ar + 56 * KB)
        gateg = at("gateg", [4, TT, 4], ar + 56 * KB + 256)
        gcur = at("gcur", [TT, 4], ar + 56 * KB + 512)
        rt = at("rt", [24, 16], ar + 32 * KB)
        rt3 = at("rt3", [TT, 4, 4], ar + 34 * KB)
        lg = at("lg", [TT, 20], ar + 36 * KB)
        wrh = at("wrh", [KT, 20], ar + 37 * KB, F32R)
        wrl = at("wrl", [KT, 20], ar + 38 * KB, F32R)
        TXH = at("TXH", [TT, D], ar, F32R)
        TXL = at("TXL", [TT, D], ar + 16 * KB, F32R)
        GHH = at("GHH", [KT, P], ar + 32 * KB, F32R)
        GHL = at("GHL", [KT, P], ar + 36 * KB, F32R)
        YH = at("YH", [2, 4, 2 * P], ar + 40 * KB, F32R)
        YL = at("YL", [2, 4, 2 * P], ar + 48 * KB, F32R)
        G1 = at("G1", [TT, 4, P], top_of["cst"] + 4 * CO["alibi"][0], F32R)
        G2 = at("G2", [4, S], top_of["ev"], F32R)
        chosen = at("chosen", [4, TT, 4], ar + 56 * KB + 768)
        posn = at("posn", [4, TT, 4], ar + 57 * KB)
        pcur = at("pcur", [TT, 4], ar + 57 * KB + 256)
        gslot = at("gslot", [4], ar + 57 * KB + 320)
        most = at("most", [2], ar + 57 * KB + 384)
        flag = at("flag", [1], ar + 57 * KB + 448, mybir.dt.int32)
        identr = at("identr", [P], ar + 57 * KB + 512, F32R)
        gparts = at("gparts", [4, TT, 4, 2], ar + 58 * KB, F32R)
        gtwo = at("gtwo", [TT, 4, 2], ar + 58 * KB + 512, F32R)
        APAD = at("APAD", [4, S + CONV_A - 1], ar)
        AH = at("AH", [4, S], ar, F32R)
        AL = at("AL", [4, S], ar + 8 * KB, F32R)
        CH = at("CH", [4, S], ar + 16 * KB, F32R)
        CL = at("CL", [4, S], ar + 24 * KB, F32R)
        CA = at("CA", [4, S], ar + 32 * KB)
        cpad = at("cpad", [S + 2], ar + 40 * KB)
        upad = at("upad", [2, S + POOL_PAD], ar + 42 * KB + 256)
        MG = at("MG", [KT, S], ar + 32 * KB)
        PL = at("PL", [4, S], ar + 48 * KB)
        MH = at("MH", [KT, N_MEM], ar, F32R)
        ML = at("ML", [KT, N_MEM], ar + 8 * KB, F32R)
        KX = at("KX", [KT, N_MEM], ar + 16 * KB)
        VX = at("VX", [2, D], ar + 24 * KB)
        QX = at("QX", [KT, S], ar + 32 * KB)
        MT = at("MT", [KT, N_MEM], ar + 48 * KB)
        EXx = at("EXx", [2, N_MEM], ar + 48 * KB)
        PX = at("PX", [2, N_MEM], ar + 50 * KB)
        PTx = at("PTx", [2, S], ar + 52 * KB)

        acc = ctx.enter_context(nc.psum_tensor("acc", [P, 4, S], F32))
        mb = ctx.enter_context(nc.psum_tensor("mb", [P, 4, S], F32))

        def cs(name, a=0, b=None):
            o, w = CO[name]
            return cst[:, o + a:o + (w if b is None else b)]

        def pr(name, a, b=None):
            o, _ = PO[name]
            return par[:, o + a:o + (a + 1 if b is None else b)]

        ident, ones, blk = cs("ident"), cs("ones"), cs("blk")

        loaded = [sem(f"loaded{i}") for i in range(RING)]
        in_x, in_par, in_x2, in_mem = sem("in_x"), sem("in_par"), sem("in_x2"), sem("in_mem")
        hi_done, split_done = sem("hi_done"), sem("split_done")
        acc_ready, evac, ev_used = sem("acc_ready"), sem("evac"), sem("ev_used")
        sq_ready, sq_used = sem("sq_ready"), sem("sq_used")
        st_sum, sd_ready, rs_ready, rb_ready = sem("st_sum"), sem("sd_ready"), sem("rs_ready"), sem("rb_ready")
        xn_ready, x_ready = sem("xn_ready"), sem("x_ready")
        dchain, achain = sem("dchain"), sem("achain")
        names = ("lam_dot lam_exp lora_act at_sc at_mx at_e at_p at_t at_te at_o at_sq at_ss at_sd at_done "
                 "rk_up rk_upg rk_sig rk_g rk_kk rk_cum rk_ksq rk_kss rk_kmx rk_ksd rk_exp rk_hat rk_bon rk_bsum rk_bonus rk_tok "
                 "rk_toke rk_nr rk_nrm rk_ak rk_akm rk_q rk_qm rk_t rk_tm rk_tt rk_tte rk_x rk_xe rk_wu rk_wue rk_z rk_zs rk_gh "
                 "rk_gs rk_hs rk_s rk_st rk_y rk_ys rk_mu rk_d rk_dsq rk_var rk_sd rk_done mixed gelu_done hid_ready "
                 "acc_added la_in la_mu la_d la_sq la_sum la_var la_sd la_y la_act ac_ready p_mm mg_ready "
                 "mem_ready xs_sc xs_mx xs_e xs_p xs_t xs_te xs_o xs_hi xs_done wr_ready rt_lg rt_sub rt_exp "
                 "gate_ready gb_ready final_ready stored "
                 "low_dve fchain f_tok f_toke f_mask f_count f_flag f_g f_turn f_turned f_gate f_gath f_xh f_xl f_silu f_hid f_ht "
                 "f_hh f_hl f_y f_yh f_yl f_out f_add f_gslot").split()
        s = {n: sem(n) for n in names}

        def in_beats(main, side, pairs=4):
            for ct in range(pairs):
                for beat in BEATS:
                    if beat in main:
                        main[beat](ct)
                    for name in SIDE.get(beat, ()):
                        if name in side:
                            side[name](ct + 1)
                        elif name[:-1] in side and name[-1].isdigit():
                            side[name[:-1]](TT * ct + int(name[-1]))
                        elif "head_" + name in side:
                            side["head_" + name](ct)

        def x_bank(u):
            return (mb[:, 0, 0:N_MEM], mb[:, 1, 0:N_MEM], acc[:, 2, 0:N_MEM])[u % 3]

        def bank(hh, x):
            return (mb if hh else acc)[:, x if hh else 2 + x, :]

        block = ctx.enter_context(nc.Block())
        @block.sync
        def _(sp):
            sp.dma_start(XT[:, :, :], xT).then_inc(in_x, 16)
            sp.dma_start(cst[:, :], consts).then_inc(in_par, 16)
            sp.dma_start(par[:, :], params).then_inc(in_par, 16)
            for n in range(RING):
                sp.dma_start(raw[:, n, :], wstream[n]).then_inc(loaded[n], 16)
            sp.dma_start(lor[:, :, :], lora).then_inc(in_par, 16)
            sp.dma_start(pw[:, :, :], poolw).then_inc(in_par, 16)

            def load(n, slot, used=None):
                sp.wait_ge(acc_ready, TILES_TO[n - RING] if used is None else used)
                src = wstream[n] if isinstance(n, int) else wstream[bass.ds(n, 1)].rearrange("a p n -> p (a n)")
                sp.dma_start(raw[:, slot, :], src).then_inc(loaded[slot], 16)

            def load_range(a, b):
                assert (b - a) % RING == 0
                tiles = TILES_TO[a] - TILES_TO[a - RING]
                assert all(TILES_TO[n] - TILES_TO[n - RING] == tiles for n in range(a, b - RING))
                with sp.Fori(0, (b - a) // RING) as i:
                    for j in range(RING):
                        load(i * RING + (a + j), (a + j) % RING, i * tiles + TILES_TO[a + j - RING])

            load_range(RING, 12)
            load(12, 0)
            sp.wait_ge(s["rk_done"], 3)
            load(13, 1)
            sp.wait_ge(s["rk_y"], 4)
            load(14, 2)
            load(15, 3)
            sp.wait_ge(s["rk_done"], 4)
            sp.dma_start(XT[:, :, :], xT).then_inc(in_x2, 16)
            load_range(16, 68)
            load(68, 0)
            load(69, 1)
            load_range(70, 82)
            sp.wait_ge(s["p_mm"], KT)
            sp.dma_start(MT[:, :, :], memT).then_inc(in_mem, 16)
            load_range(82, 86)
            load_range(86, 146)
            load(146, 2)
            for m in range(KT):
                sp.wait_ge(s["final_ready"], m + 1)
                sp.dma_start(out[:, m, :], XT[:, m, :]).then_inc(s["stored"], 16)
            sp.wait_ge(s["stored"], 16 * KT)

        @block.gpsimd
        def _(pool):
            def lower(n, slot, kt=KT):
                pool.wait_ge(hi_done, n + 1)
                nc.gpsimd.tensor_tensor(wl[:, slot, 0:kt].rearrange("p a b c -> p (a b c)"),
                                        raw[:, slot, 0:kt * 2 * P],
                                        wh[:, slot, 0:kt].rearrange("p a b c -> p (a b c)").bitcast(F32),
                                        ALU.subtract).then_inc(split_done, 1)

            end = NBLK
            def lower_range(a, b, kt=KT):
                assert a % RING == 0
                with pool.Fori(0, (b - a) // RING) as i:
                    for j in range(RING):
                        lower(i * RING + (a + j), j, kt)
                for n in range(b - (b - a) % RING, b):
                    lower(n, n % RING, kt)

            lower_range(0, min(end, B0["moe"]))
            lower(B0["moe"], B0["moe"] % RING, KT - K_DVE)
            lower_range(B0["moe"] + 1, NBLK, KT - K_DVE)

        @block.tensor
        def _(pe):
            mm = nc.tensor.matmul

            def mm3(out_, a, b, start, stop):
                mm(out_, a[0], b[0], start=start, stop=False)
                mm(out_, a[0], b[1], start=False, stop=False)
                return mm(out_, a[1], b[0], start=False, stop=stop)

            def begin_block(n, t, tiles=2, moe=False):
                pe.wait_ge(split_done, n + 1)
                if moe:
                    pe.wait_ge(s["low_dve"], n + (1 - B0["moe"]))
                for j in range(tiles):
                    if not isinstance(t, int) or t + j >= 4:
                        pe.wait_ge(evac, t + (j - 3))

            def block_tiles(n, t, slot, bank, xs=(XH, XL), kt=KT, ns=S, need=None, moe=False):
                begin_block(n, t, moe=moe)
                for k in range(kt):
                    if need is not None:
                        pe.wait_ge(need[0], need[1] + k)
                    for j in range(2):
                        last = mm3(acc[:, (bank + j) % 4, 0:ns], (wh[:, slot, k, j, :], wl[:, slot, k, j, :]),
                                   (xs[0][:, k, 0:ns], xs[1][:, k, 0:ns]), k == 0, k == kt - 1)
                        if k == kt - 1:
                            last.then_inc(acc_ready, 1)

            def stage_blocks(name, count, need, xs=(XH, XL), ns=S, start=0):
                for b in range(start, start + count):
                    n, t = B0[name] + b, T0[name] + 2 * b
                    block_tiles(n, t, n % RING, t % 4, xs, ns=ns, need=need if b == start else None)

            def token_tiles(n, t, xs, lots):
                begin_block(n, t)
                for j, toks in enumerate(lots):
                    for c, tok in enumerate(toks):
                        for k in range(KT):
                            last = mm3(acc[:, (t + j) % 4, c * 256:(c + 1) * 256],
                                       (xs[0][:, k, tok * P:(tok + 1) * P], xs[1][:, k, tok * P:(tok + 1) * P]),
                                       (wh[:, n % RING, k].rearrange("p a b -> p (a b)"),
                                        wl[:, n % RING, k].rearrange("p a b -> p (a b)")), k == 0, k == KT - 1)
                    last.then_inc(acc_ready, 1)

            def norm_sums(r, nt=TT):
                pe.wait_ge(sq_used, KT * (r + 1))
                for t in range(nt):
                    last = mm(mb[:, 0, t:t + 1], sqa[:, t * P:(t + 1) * P], ones[:, 0:1], start=True, stop=True)
                last.then_inc(st_sum, 1)

            def norm_spread(r, nt=TT):
                pe.wait_ge(rs_ready, r + 1)
                for t in range(nt):
                    last = mm(mb[:, 1, t * P:(t + 1) * P], rs[:, t:t + 1].to_broadcast([P, P]), ident,
                              start=True, stop=True)
                last.then_inc(rb_ready, 1)

            def norm(r):
                norm_sums(r)
                norm_spread(r)

            pe.wait_ge(in_par, 64)
            norm(0)
            stage_blocks("in", 11, (xn_ready, 1))
            for b in (11, 12):
                token_tiles(B0["in"] + b, T0["in"] + 2 * b, (XH, XL), ((0, 1), (2, 3)))

            def scores(u):
                h, i = divmod(u, TT)
                if u == 0:
                    pe.wait_ge(evac, 26)
                else:
                    pe.wait_ge(s["at_te"], u)
                    if i == 0:
                        pe.wait_ge(s["at_done"], h)
                w = (i + 1) * P
                for c in range(2):
                    last = mm(mb[:, 2 + c, 0:w], QT[64 * c:64 * c + 64, h, i * P:(i + 1) * P],
                              KD[64 * c:64 * c + 64, h, 0:w], start=True, stop=True)
                last.then_inc(s["at_sc"], 1)

            def turn(u):
                pe.wait_ge(s["at_p"], u + 1)
                for j in range(u % TT + 1):
                    last = nc.tensor.transpose(mb[:, 2, j * P:(j + 1) * P], SC[:, u % 2, 0, j * P:(j + 1) * P], ident)
                last.then_inc(s["at_t"], 1)

            def head_out(h):
                pe.wait_ge(s["at_te"], TT * (h + 1))
                for j in range(TT):
                    last = mm(mb[:, 3, j * P:S], DV[:, j, h * P:(h + 1) * P], AT[:, j, j * P:S],
                              start=(j == 0), stop=(j == TT - 1))
                last.then_inc(s["at_o"], 1)

            def head_sums(h):
                pe.wait_ge(s["at_sq"], h + 1)
                mm(mb[:, 2, :], ones, SQO[:, 0, :], start=True, stop=True).then_inc(s["at_ss"], 1)

            def up(ct):
                if ct == 0:
                    pe.wait_ge(evac, 26)
                    pe.wait_ge(s["lora_act"], 1)
                elif ct == 4:
                    return
                else:
                    pe.wait_ge(s["rk_zs"], 2 * ct)
                c = slice(ct * P, (ct + 1) * P)
                mm(bank(0, 1), lor[0:64, 0, c], LO[0:64, :], start=True, stop=True)
                mm(bank(1, 1), lor[64:128, 0, c], LO[64:128, :], start=True, stop=True).then_inc(s["rk_up"], 1)

            def up_gate(ct):
                if ct < 4:
                    pe.wait_ge(s["rk_sig"], ct + 1)
                    mm(bank(0, 1), lor[:, 1, ct * P:(ct + 1) * P], GLO[:, :], start=True,
                       stop=True).then_inc(s["rk_upg"], 1)

            def keys(ct):
                if ct < 4:
                    pe.wait_ge(s["rk_ksq"], ct + 1)
                    mm(bank(1, 1), blk, Wt[ct % 2][:, 5, :], start=True, stop=True).then_inc(s["rk_kss"], 1)

            def tok(ct):
                pe.wait_ge(s["rk_hat"], ct + 1)
                pe.wait_ge(s["rk_g"], ct + 1)
                if ct:
                    pe.wait_ge(s["rk_sd"], ct)
                W = Wt[ct % 2]
                mm(acc[:, 0, :], blk, W[:, 3, :], start=True, stop=True).then_inc(s["rk_bsum"], 1)
                for t in range(TT):
                    o = slice(t * P, (t + 1) * P)
                    nc.tensor.transpose(acc[:, 1, o], AR[:, t, 0, :], ident)
                    nc.tensor.transpose(acc[:, 2, o], W[:, 0, o], ident)
                    nc.tensor.transpose(acc[:, 3, o], W[:, 2, o], ident)
                    last = nc.tensor.transpose(mb[:, 0, o], V[:, ct, o], ident)
                last.then_inc(s["rk_tok"], 1)

            def products(ct, left, done, ready, value):
                for hh in range(2):
                    pe.wait_ge(ready, value + hh)
                    ps = slice(HD * hh, HD * hh + HD)
                    for t in range(TT):
                        last = mm(bank(hh, t // 2)[:, 256 * (t % 2):256 * (t % 2) + 256], left[ps, t * P:(t + 1) * P],
                                  AR[ps, t].rearrange("p a b -> p (a b)"), start=True, stop=True)
                    last.then_inc(done, 1)

            def nr(ct):
                pe.wait_ge(s["rk_toke"], ct + 1)
                pe.wait_ge(s["rk_kmx"], ct + 1)
                products(ct, BT, s["rk_nr"], s["rk_toke"], ct)

            def ak(ct):
                products(ct, KH, s["rk_ak"], s["rk_nrm"], 2 * ct + 1)

            def l0(ct):
                for hh in range(2):
                    pe.wait_ge(s["rk_akm"], 2 * ct + hh + 1)
                    for t in range(TT):
                        last = nc.tensor.transpose(bank(hh, 0)[:, t * P:(t + 1) * P], NR[:, hh, t, 0, :], ident)
                    last.then_inc(s["rk_q"], 1)
                    for t in range(TT):
                        last = mm(bank(hh, 1)[:, t * HD:(t + 1) * HD], AKRK[:, hh, t, 0, :],
                                  Vtok[:, t, HD * hh:HD * hh + HD], start=True, stop=True)
                    last.then_inc(s["rk_x"], 1)

            def turn_t(u, hh, level):
                for t in range(TT):
                    last = nc.tensor.transpose(bank(hh, 1)[:, t * P:(t + 1) * P], Tm[:, hh, t, :], ident)
                last.then_inc(s["rk_tt"], 1)

            def level(l):
                def run(ct):
                    for hh in range(2):
                        pe.wait_ge(s["rk_tm"], 6 * ct * 2 + 2 * (l - 1) + hh + 1)
                        if l == 1:
                            pe.wait_ge(s["rk_xe"], 2 * ct + hh + 1)
                        for t in range(TT):
                            last = mm(bank(hh, 0)[:, t * P:(t + 1) * P], NR[:, hh, t, 0, :], Tm[:, hh, t, :],
                                      start=True, stop=True)
                        last.then_inc(s["rk_q"], 1)
                        turn_t(ct, hh, l)
                    for hh in range(2):
                        pe.wait_ge(s["rk_qm"], 10 * ct + 2 * (l - 1) + hh + 1)
                        pe.wait_ge(s["rk_tte"], 12 * ct + 2 * (l - 1) + hh + 1)
                        for t in range(TT):
                            last = mm(bank(hh, 1)[:, t * P:(t + 1) * P], TTm[:, hh, t, :], Qm[:, hh, t, :],
                                      start=True, stop=True)
                        last.then_inc(s["rk_t"], 1)
                return run

            def wu(ct):
                for hh in range(2):
                    pe.wait_ge(s["rk_tm"], 12 * ct + 10 + hh + 1)
                    turn_t(ct, hh, 6)
                for hh in range(2):
                    pe.wait_ge(s["rk_tte"], 12 * ct + 10 + hh + 1)
                    for t in range(TT):
                        last = mm(bank(hh, 0)[:, t * P:(t + 1) * P], TTm[:, hh, t, :],
                                  AXb[:, t, hh].rearrange("p a b -> p (a b)"), start=True, stop=True)
                    last.then_inc(s["rk_wu"], 1)

            def gh(ct):
                pe.wait_ge(s["rk_bonus"], ct + 1)
                for hh in range(2):
                    ps = slice(HD * hh, HD * hh + HD)
                    pe.wait_ge(s["rk_wue"], 2 * ct + hh + 1)
                    for t in range(TT):
                        last = mm(bank(hh, 1)[ps, t * P:(t + 1) * P], WU[:, hh, t, 0:HD], NR[:, hh, t, 1, :],
                                  start=True, stop=True)
                    last.then_inc(s["rk_z"], 1)
                    for c in range(NCH):
                        t, cp = c // 2, slice(HD * (c % 2), HD * (c % 2) + HD)
                        g, h = slice(t * HD, (t + 1) * HD), slice(256 + t * HD, 256 + (t + 1) * HD)
                        mm(acc[ps, c % 2, g], WU[cp, hh, t, 0:HD], Btok[cp, t, ps], start=True, stop=True)
                        mm(acc[ps, c % 2, h], Btok[cp, t, ps], WU[cp, hh, t, HD:P], start=True, stop=False)
                        last = mm(acc[ps, c % 2, h], Ktok[cp, t, ps], Vtok[cp, t, ps], start=False, stop=True)
                    last.then_inc(s["rk_gh"], 1)

            def enter(c):
                def run(ct):
                    pe.wait_ge(s["rk_st"], 7 * ct + c - 1)
                    if c == 2:
                        pe.wait_ge(s["rk_gs"], ct + 1)
                    for hh in range(2):
                        ps = slice(HD * hh, HD * hh + HD)
                        last = mm(mb[ps, 0, 0:HD], GTt[ct % 2][ps, c - 1, :], STt[ct % 2][ps, c - 1, :],
                                  start=True, stop=True)
                    last.then_inc(s["rk_s"], 1)
                return run

            def y(ct):
                pe.wait_ge(s["rk_st"], 7 * ct + 7)
                pe.wait_ge(s["rk_zs"], 2 * ct + 2)
                for hh in range(2):
                    ps = slice(HD * hh, HD * hh + HD)
                    for t in range(TT):
                        o = slice(t * P, (t + 1) * P)
                        mm(acc[ps, 2, o], WU[:, hh, t, HD:P], NR[:, hh, t, 1, :], start=True, stop=False)
                        mm(acc[ps, 2, o], Vtok[:, t, ps], AKRK[:, hh, t, 1, :], start=False, stop=False)
                        for c in (2 * t, 2 * t + 1):
                            if c:
                                last = mm(acc[ps, 2, c * HD:(c + 1) * HD], STt[ct % 2][ps, c, :],
                                          Z[ps, t, (c % 2) * HD:(c % 2 + 1) * HD], start=False, stop=(c % 2 == 1))
                last.then_inc(s["rk_y"], 1)

            def mu(ct):
                pe.wait_ge(s["rk_ys"], ct + 1)
                mm(mb[:, 0, :], blk, Wt[ct % 2][:, 0, :], start=True, stop=True).then_inc(s["rk_mu"], 1)

            def var(ct):
                pe.wait_ge(s["rk_dsq"], ct + 1)
                mm(acc[:, 2, :], blk, Wt[ct % 2][:, 2, :], start=True, stop=True).then_inc(s["rk_var"], 1)

            up(0)
            up_gate(0)
            keys(0)
            main = {"tok": tok, "nr": nr, "ak": ak, "l0": l0, "wu": wu, "gh": gh, "y": y, "mu": mu, "var": var}
            main |= {f"l{l}": level(l) for l in range(1, LEVELS)} | {f"s{c}": enter(c) for c in range(2, NCH)}
            in_beats(main, {"scores": scores, "turn": turn, "head_out": head_out, "head_sums": head_sums,
                            "up": up, "up_gate": up_gate, "keys": keys})

            stage_blocks("out", 4, (s["mixed"], 1))
            norm(1)

            def group(name, i, hidden, need=None, spread=None):
                n0, t0 = i * 12 + B0[name], i * 24 + T0[name]
                for b in range(hidden):
                    if spread is not None and b % 2 == 0:
                        spread(i, b // 2)
                    block_tiles(n0 + b, t0 + 2 * b, (B0[name] + b) % RING, (T0[name] + 2 * b) % 4,
                                need=need if b == 0 else None, moe=name == "moe")
                for b in range(4):
                    block_tiles(n0 + hidden + b, t0 + 2 * (hidden + b), (B0[name] + hidden + b) % RING,
                                (T0[name] + 2 * (hidden + b)) % 4, (HH, HL), kt=hidden,
                                need=(s["hid_ready"], i * 8 + (1 if name == "ffn" else 23)) if b == 0 else None,
                                moe=name == "moe")

            norm(2)
            pe.wait_ge(xn_ready, 16)
            with pe.Fori(0, 2) as i:
                group("ffn", i, 8)
            group("ffn", 2, 6)
            norm(3)

            norm(4)
            stage_blocks("mix", 12, (xn_ready, 17))

            def pooled(m):
                if m >= 2:
                    pe.wait_ge(s["mg_ready"], m - 1)
                mm(mb[:, 2 + m % 2, :], pw[:, m // 2, (m % 2) * P:(m % 2 + 1) * P], PL[:, m // 2, :],
                   start=True, stop=True).then_inc(s["p_mm"], 1)

            for m in range(KT):
                n, t = B0["gate"] + 2 * m, T0["gate"] + 5 * m
                block_tiles(n, t, n % RING, t % 4)
                if m == 0:
                    pe.wait_ge(s["la_in"], 1)
                    mm(mb[:, 0, :], ones, sqa[:, :], start=True, stop=True).then_inc(s["la_mu"], 1)
                    pe.wait_ge(s["la_sum"], 4)
                    mm(mb[:, 1, :], ones, sqa[:, :], start=True, stop=True).then_inc(s["la_var"], 1)
                pooled(m)
                begin_block(n + 1, t + 2, 3)
                slot = (n + 1) % RING
                for k in range(KT):
                    last = mm3(acc[:, (t + 2) % 4, :], (wh[:, slot, k, 0, :], wl[:, slot, k, 0, :]),
                               (XH[:, k, :], XL[:, k, :]), k == 0, k == KT - 1)
                last.then_inc(acc_ready, 1)
                for x, (xh, xl) in enumerate(((AH, AL), (CH, CL))):
                    for k in range(4):
                        if m == 0 and x == 0:
                            pe.wait_ge(s["ac_ready"], k + 1)
                        last = mm3(acc[:, (t + 3 + x) % 4, :],
                                   (wh[:, slot, 4 * x + k, 1, :], wl[:, slot, 4 * x + k, 1, :]),
                                   (xh[:, k, :], xl[:, k, :]), k == 0, k == 3)
                    last.then_inc(acc_ready, 1)

            stage_blocks("o", 1, (s["mg_ready"], KT + 1))
            norm_sums(5, 2)
            stage_blocks("o", 1, None, start=1)
            norm_spread(5, 2)
            stage_blocks("o", 2, None, start=2)
            stage_blocks("kv", 4, (s["mem_ready"], 1), (MH, ML), ns=N_MEM)
            for b in range(4, 8):
                token_tiles(B0["kv"] + b, T0["kv"] + 2 * b, (MH, ML), ((0,), (1,)))
            norm(6)
            stage_blocks("q", 4, (xn_ready, 25))

            def x_scores(u):
                h, i = divmod(u, TT)
                pe.wait_ge(evac, T0["q"] + 8)
                if u >= 3:
                    pe.wait_ge(s["xs_e"], u - 2)
                for k in range(2):
                    last = mm(x_bank(u), QX[:, 2 * h + k, i * P:(i + 1) * P], KX[:, 2 * h + k, :],
                              start=(k == 0), stop=(k == 1))
                last.then_inc(s["xs_sc"], 1)

            def x_turn(u):
                pe.wait_ge(s["xs_p"], u + 1)
                if u >= 2:
                    pe.wait_ge(s["xs_te"], u - 1)
                for j in range(2):
                    last = nc.tensor.transpose(mb[:, 2 + u % 2, j * P:(j + 1) * P], PX[:, u % 2, j * P:(j + 1) * P],
                                               ident)
                last.then_inc(s["xs_t"], 1)

            def x_out(h):
                pe.wait_ge(s["xs_te"], TT * (h + 1))
                if h:
                    pe.wait_ge(s["xs_done"], 2 * h)
                for v in range(2):
                    for j in range(2):
                        last = mm(acc[:, v, :], VX[:, j, h * 256 + v * P:h * 256 + (v + 1) * P], PTx[:, j, :],
                                  start=(j == 0), stop=(j == 1))
                    last.then_inc(s["xs_o"], 1)

            x_scores(0)
            x_scores(1)
            for u in range(4 * TT):
                if u + 2 < 4 * TT:
                    x_scores(u + 2)
                x_turn(u)
                if u % TT == TT - 1:
                    x_out(u // TT)
            stage_blocks("xo", 4, (s["xs_done"], 1))

            def spread_gate(i, e):
                pe.wait_ge(s["gate_ready"], i + 1)
                if not isinstance(i, int) or 4 * i + e >= 2:
                    if isinstance(i, int) or e >= 2:
                        pe.wait_ge(s["hid_ready"], i * 8 + (22 + 2 * (e - 1)))
                for t in range(TT):
                    last = mm(mb[:, 2 + e % 2, t * P:(t + 1) * P], gcur[:, t, e:e + 1].to_broadcast([P, P]), ident,
                              start=True, stop=True)
                last.then_inc(s["gb_ready"], 1)

            def turn_places(i):
                for e in range(4):
                    if e >= 2:
                        pe.wait_ge(s["f_turned"], i * 4 + (e - 1))
                    for t in range(TT):
                        last = mm(mb[:, 2 + e % 2, t * P:(t + 1) * P], G1[:, t, e, :], identr[:, :], start=True,
                                  stop=True)
                    last.then_inc(s["f_turn"], 1)

            def gather_gates(i):
                pe.wait_ge(s["f_g"], i + 1)
                for e in range(4):
                    for t in range(TT):
                        last = mm(mb[:, 0, 2 * e:2 * e + 2], G1[:, t, e, :], gtwo[:, t, e, :],
                                  start=(t == 0), stop=(t == TT - 1))
                last.then_inc(s["f_gate"], 1)

            def gather(i, k):
                if k >= 2:
                    pe.wait_ge(s["f_xl"], i * 8 + (k - 1))
                for t in range(TT):
                    for part in (TXH, TXL):
                        last = mm(acc[:, 2 + k % 2, :], part[:, t, k * P:(k + 1) * P],
                                  G1[:, t].rearrange("p a b -> p (a b)"),
                                  start=(t == 0 and part is TXH), stop=(t == TT - 1 and part is TXL))
                last.then_inc(s["f_gath"], 1)

            def gathered(i, last_group=False):
                n0, t0 = B0["moe"], T0["moe"]

                def turn_hidden(b):
                    pe.wait_ge(s["f_hid"], i * 8 + (b + 1))
                    if b >= 2:
                        pe.wait_ge(s["f_hl"], i * 8 + (b - 1))
                    else:
                        pe.wait_ge(s["f_turned"], i * 4 + (3 + b))
                    nc.tensor.transpose(mb[:, 2 + b % 2, 0:P], tmp[:, b % 2, P:2 * P], ident).then_inc(s["f_ht"], 1)

                for b in range(8):
                    pe.wait_ge(split_done, i * 12 + (n0 + b + 1))
                    pe.wait_ge(s["low_dve"], i * 12 + (b + 1))
                    if b >= 2:
                        pe.wait_ge(s["f_hid"], i * 8 + (b - 1))
                    e, slot = b // 2, (n0 + b) % RING
                    for k in range(KT):
                        if b == 0:
                            pe.wait_ge(s["f_xl"], i * 8 + (k + 1))
                        last = mm3(acc[:, b % 2, 0:2 * P],
                                   (XH[:, k, e * P:(e + 1) * P], XL[:, k, e * P:(e + 1) * P]),
                                   (wh[:, slot, k].rearrange("p a b -> p (a b)"),
                                    wl[:, slot, k].rearrange("p a b -> p (a b)")), k == 0, k == KT - 1)
                    last.then_inc(acc_ready, 2)
                    if b:
                        turn_hidden(b - 1)
                if last_group:
                    turn_hidden(7)
                else:
                    gather_gates(i + 1)
                    pe.wait_ge(s["f_add"], i * 8)
                    gather(i + 1, 0)
                    turn_hidden(7)
                    for k in range(1, KT):
                        gather(i + 1, k)
                    pe.wait_ge(s["f_gslot"], i + 2)

                def scatter(b):
                    pe.wait_ge(s["f_yl"], i * 8 + (2 * b + 2))
                    for j in range(2):
                        if b:
                            pe.wait_ge(s["f_add"], i * 8 + (2 * b + j - 1))
                        elif not last_group:
                            pe.wait_ge(s["f_xl"], i * 8 + (15 + j))
                        else:
                            pe.wait_ge(s["f_add"], i * 8)
                        if b == 0 and j == 0:
                            pe.wait_ge(s["f_turned"], i * 4 + 4)
                        for e in range(4):
                            for part in (YH, YL):
                                last = mm(acc[:, 2 + j, :], part[:, b % 2, e, j * P:(j + 1) * P], G2[:, e, :],
                                          start=(e == 0 and part is YH), stop=(e == 3 and part is YL))
                        last.then_inc(s["f_out"], 1)

                for b in range(4):
                    slot = (n0 + 8 + b) % RING
                    pe.wait_ge(split_done, i * 12 + (n0 + 8 + b + 1))
                    pe.wait_ge(s["low_dve"], i * 12 + (8 + b + 1))
                    for e in range(4):
                        if b and e % 2 == 0:
                            pe.wait_ge(s["f_yl"], i * 8 + (2 * b - 1 + e // 2))
                        for x in (2 * e, 2 * e + 1):
                            if b == 0:
                                pe.wait_ge(s["f_hl"], i * 8 + (x + 1))
                            last = mm3(mb[:, e // 2, (e % 2) * 2 * P:(e % 2 + 1) * 2 * P],
                                       (GHH[:, x, :], GHL[:, x, :]),
                                       (wh[:, slot, x].rearrange("p a b -> p (a b)"),
                                        wl[:, slot, x].rearrange("p a b -> p (a b)")), x % 2 == 0, x % 2 == 1)
                        if e == 1:
                            last.then_inc(s["f_y"], 1)
                    last.then_inc(acc_ready, 2)
                    if b:
                        scatter(b - 1)
                scatter(3)
                if not last_group:
                    turn_places(i + 1)

            norm(7)
            pe.wait_ge(xn_ready, 40)
            pe.wait_ge(s["wr_ready"], 1)
            for t in range(TT):
                for k in range(KT):
                    last = mm3(mb[:, 0, t * 20:(t + 1) * 20], (XH[:, k, t * P:(t + 1) * P],
                                                               XL[:, k, t * P:(t + 1) * P]),
                               (wrh[:, k, :], wrl[:, k, :]), k == 0, k == KT - 1)
            last.then_inc(s["rt_lg"], 1)
            for q in range(16):
                t, half, part = q // 4, q // 2 % 2, (XH, XL)[q % 2]
                if q >= 4:
                    pe.wait_ge(s["f_toke"], q - 3)
                for k in range(4):
                    last = mm(acc[:, q % 4, k * P:(k + 1) * P], part[:, 4 * half + k, t * P:(t + 1) * P],
                              identr[:, :], start=True, stop=True)
                last.then_inc(s["f_tok"], 1)
            pe.wait_ge(s["f_mask"], 1)
            for t in range(TT + 1):
                for j in range(min(t + 1, TT)):
                    last = mm(mb[:, 0, t * 16:(t + 1) * 16], cs("upto") if j == t else ones, chosen[:, :, j, :],
                              start=(j == 0), stop=(j == min(t, TT - 1)))
            last.then_inc(s["f_count"], 1)
            pe.wait_ge(s["f_toke"], 16)
            pe.wait_ge(s["f_flag"], 1)
            crowded = pe.value_load(flag[0:1, 0:1])
            with pe.If(crowded > 0):
                with pe.Fori(0, 3) as i:
                    group("moe", i, 8, spread=spread_gate)
                group("moe", 3, 8, spread=spread_gate)
            with pe.Else():
                gather_gates(0)
                for k in range(KT):
                    gather(0, k)
                turn_places(0)
                with pe.Fori(0, 3) as i:
                    gathered(i)
                gathered(3, last_group=True)
            norm(8)

        @block.scalar
        def _(act):
            actv = nc.scalar.activation
            chain_n = [0]

            def link(ins):
                chain_n[0] += 1
                ins.then_inc(achain, 1)
                act.wait_ge(achain, chain_n[0])

            def split_hi(n, value, tiles=None):
                act.wait_ge(loaded[n % RING], value)
                if tiles is not None:
                    act.wait_ge(acc_ready, tiles)
                actv(wh[:, n % RING].rearrange("p a b c -> p (a b c)"), raw[:, n % RING, :], ACT.Copy).then_inc(hi_done, 1)

            def ahead(n, i=None):
                n += 3
                if n >= NBLK:
                    return
                value, tiles = 16 * (n // RING + 1), TILES_TO[n - RING] if n >= RING else None
                if i is not None:
                    value, tiles = i * (16 * 12 // RING) + value, i * 24 + tiles
                split_hi(n, value, tiles)

            def take(t, e, func, bank, ring, scale=1.0):
                act.wait_ge(acc_ready, t + 1)
                if not isinstance(e, int) or e >= 4:
                    act.wait_ge(ev_used, e - 3)
                actv(ev[:, ring, 2:S + 2], acc[:, bank, :], func, scale=scale).then_inc(evac, 1)

            def take_s(t, e, func=ACT.Copy):
                take(t, e, func, t % 4, e % 4)

            def direct(t, dst, src, scale=1.0):
                act.wait_ge(acc_ready, t + 1)
                actv(dst, src, ACT.Copy, scale=scale).then_inc(evac, 1)

            def square(q, src):
                if q >= 2:
                    act.wait_ge(sq_used, q - 1)
                actv(sq[:, q % 2, 0:src.shape[-1]], src, ACT.Square).then_inc(sq_ready, 1)

            def norm_root(r, nt=TT):
                act.wait_ge(st_sum, r + 1)
                actv(sd[:, 0:nt], mb[:, 0, 0:nt], ACT.Sqrt, bias=cs("eps", 0, 1), scale=1.0 / D).then_inc(sd_ready, 1)

            act.wait_ge(in_x, 16)
            for k in range(KT):
                square(k, XT[:, k, :])
            act.wait_ge(in_par, 64)
            split_hi(0, 16)
            norm_root(0)
            for n in (1, 2):
                split_hi(n, 16)
            for b in range(13):
                if b < 10:
                    ahead(B0["in"] + b)
                for t in (2 * b, 2 * b + 1):
                    if t < 14:
                        take_s(t, t)
                    elif t < 18:
                        direct(t, QT[:, t - 14, :], acc[:, t % 4, :], 0.125)
                    elif t < 22:
                        direct(t, KD[:, t - 18, :], acc[:, t % 4, :])
                    else:
                        c, j = divmod(t - 22, 2)
                        direct(t, DV[:, 2 * j:2 * j + 2, c * 256:(c + 1) * 256],
                               acc[:, t % 4, :].rearrange("p (a b) -> p a b", a=2))
            act.wait_ge(s["lam_dot"], 1)
            actv(lam_e, lam_d, ACT.Exp).then_inc(s["lam_exp"], 1)

            def exp(u):
                w = (u % TT + 1) * P
                act.wait_ge(s["at_mx"], u + 1)
                for c in range(2):
                    x = 2 * (u % 2) + c
                    last = actv(SC[:, u % 2, c, 0:w], SC[:, u % 2, c, 0:w], ACT.Exp, bias=nmx[:, x:x + 1],
                                accum_out=den[:, x:x + 1])
                last.then_inc(s["at_e"], 1)

            def turned(u):
                h, i = divmod(u, TT)
                act.wait_ge(s["at_t"], u + 1)
                if i == 0 and h:
                    act.wait_ge(s["at_o"], h)
                actv(AT[:, 0:i + 1, i * P:(i + 1) * P], mb[:, 2, 0:(i + 1) * P].rearrange("p (a b) -> p a b", b=P),
                     ACT.Copy).then_inc(s["at_te"], 1)

            def head_square(h):
                act.wait_ge(s["at_o"], h + 1)
                actv(SQO[:, 0, :], mb[:, 3, :], ACT.Square).then_inc(s["at_sq"], 1)

            def head_norm(h):
                act.wait_ge(s["at_ss"], h + 1)
                actv(SQO[:, 1, :], mb[:, 2, :], ACT.Sqrt, bias=cs("eps", 1, 2), scale=1.0 / P).then_inc(s["at_sd"], 1)

            def gbuf(ct):
                return ev[:, ct % 2, 2:S + 2]

            def up(ct):
                if ct < 4:
                    W = Wt[ct % 2]
                    act.wait_ge(s["rk_up"], ct + 1)
                    actv(W[:, 0, :], bank(0, 1), ACT.Sigmoid, bias=pr("w_decay0", ct))
                    actv(W[:, 1, :], bank(1, 1), ACT.Sigmoid, bias=pr("w_iclr0", ct)).then_inc(s["rk_sig"], 1)

            def up_gate(ct):
                if ct < 4:
                    W = Wt[ct % 2]
                    act.wait_ge(s["rk_upg"], ct + 1)
                    actv(gbuf(ct), bank(0, 1), ACT.Copy).then_inc(s["rk_g"], 1)
                    act.wait_ge(s["rk_kk"], ct + 1)
                    actv(W[:, 5, :], W[:, 4, :], ACT.Square).then_inc(s["rk_ksq"], 1)

            def decays(ct):
                if ct < 4:
                    W = Wt[ct % 2]
                    act.wait_ge(s["rk_kmx"], ct + 1)
                    actv(W[:, 5, :], W[:, 5, :], ACT.Sqrt).then_inc(s["rk_ksd"], 1)
                    act.wait_ge(s["rk_cum"], ct + 1)
                    actv(W[:, 6, :], W[:, 2, :], ACT.Exp)
                    actv(W[:, 7, :], W[:, 2, :], ACT.Exp, scale=-1.0)
                    actv(W[:, 3, :], W[:, 3, :], ACT.Exp).then_inc(s["rk_exp"], 1)

            def flat(a):
                return a.rearrange("p a b -> p (a b)")

            def tok(ct):
                act.wait_ge(s["rk_tok"], ct + 1)
                actv(AXb[:, :, :, 0, :], acc[:, 1, :].rearrange("p (t h c) -> p t h c", t=TT, h=2), ACT.Copy)
                actv(flat(Btok[:, :, :]), acc[:, 2, :], ACT.Copy)
                actv(flat(Ktok[:, :, :]), acc[:, 3, :], ACT.Copy)
                actv(flat(Vtok[:, :, :]), mb[:, 0, :], ACT.Copy).then_inc(s["rk_toke"], 1)

            def l0(ct):
                for hh in range(2):
                    act.wait_ge(s["rk_x"], 2 * ct + hh + 1)
                    actv(AXb[:, :, hh, 1, :], bank(hh, 1)[:, 0:TT * HD].rearrange("p (t c) -> p t c", t=TT),
                         ACT.Copy).then_inc(s["rk_xe"], 1)

            def turned_t(l):
                def run(ct):
                    for hh in range(2):
                        act.wait_ge(s["rk_tt"], 12 * ct + 2 * (l - 1) + hh + 1)
                        actv(flat(TTm[:, hh]), bank(hh, 1), ACT.Copy).then_inc(s["rk_tte"], 1)
                return run

            def wu(ct):
                turned_t(LEVELS)(ct)
                for hh in range(2):
                    act.wait_ge(s["rk_wu"], 2 * ct + hh + 1)
                    actv(flat(WU[:, hh]), bank(hh, 0), ACT.Copy).then_inc(s["rk_wue"], 1)

            def gh(ct):
                act.wait_ge(s["rk_gh"], 2 * ct + 2)
                actv(HSt[ct % 2][:, :, :].rearrange("p (t a) j -> p a t j", a=2),
                     acc[:, 0:2, 256:512].rearrange("p a (t j) -> p a t j", t=TT), ACT.Copy).then_inc(s["rk_hs"], 1)

            def mu(ct):
                W = Wt[ct % 2]
                act.wait_ge(s["rk_d"], ct + 1)
                actv(W[:, 2, :], W[:, 1, :], ACT.Square).then_inc(s["rk_dsq"], 1)

            def var(ct):
                act.wait_ge(s["rk_var"], ct + 1)
                actv(Wt[ct % 2][:, 3, :], acc[:, 2, :], ACT.Sqrt, bias=cs("eps", 2, 3),
                     scale=1.0 / HD).then_inc(s["rk_sd"], 1)

            act.wait_ge(ev_used, 2)
            actv(LO[0:64, :], LO[0:64, :], ACT.Tanh)
            actv(GLO[:, :], GLO[:, :], ACT.Sigmoid).then_inc(s["lora_act"], 1)
            act.wait_ge(ev_used, 14)
            up(0)
            up_gate(0)
            decays(0)
            main = {"tok": tok, "l0": l0, "wu": wu, "gh": gh, "mu": mu, "var": var}
            main |= {f"l{l}": turned_t(l) for l in range(1, LEVELS)}
            in_beats(main, {"exp": exp, "turned": turned, "head_square": head_square, "head_norm": head_norm,
                            "up": up, "up_gate": up_gate, "decays": decays})

            def taken_out(t, dst, q):
                act.wait_ge(acc_ready, t + 1)
                if q >= 2:
                    act.wait_ge(sq_used, q - 1)
                actv(sq[:, q % 2, :], acc[:, t % 4, :], ACT.Square).then_inc(sq_ready, 1)
                actv(dst, acc[:, t % 4, :], ACT.Copy).then_inc(evac, 1)

            act.wait_ge(s["rk_y"], 4)
            for n in (13, 14, 15):
                split_hi(n, 16 * (n // RING + 1), TILES_TO[n - RING])
            for b in range(4):
                ahead(B0["out"] + b)
                for m in (2 * b, 2 * b + 1):
                    taken_out(T0["out"] + m, Fo[:, m, :], 8 + m)
            norm_root(1)

            for m in range(KT):
                act.wait_ge(x_ready, m + 1)
                square(16 + m, XT[:, m, :])
            norm_root(2)

            def group(name, i, hidden):
                loop = None if isinstance(i, int) else i
                k = i if loop is None else 0
                n0, t0, e0 = B0[name] + 12 * k, T0[name] + 24 * k, E0[name] + 24 * k
                add = (lambda v, per: v) if loop is None else (lambda v, per: loop * per + v)
                for b in range(hidden + 4):
                    ahead(n0 + b, loop)
                    for j in range(2):
                        func = ACT.Copy
                        if name == "moe" and b < hidden and j == 0:
                            func = ACT.Silu
                        take(add(t0 + 2 * b + j, 24), add(e0 + 2 * b + j, 24), func, (t0 + 2 * b + j) % 4,
                             (e0 + 2 * b + j) % 4)
                    if name == "ffn" and b < hidden:
                        act.wait_ge(ev_used, add(e0 + 2 * b + 1, 24))
                        actv(gl[:, b % 2, :], gl[:, b % 2, :], ACT.Gelu_apprx_tanh).then_inc(s["gelu_done"], 1)
                    if b >= hidden and loop is None and k == (2 if name == "ffn" else 3):
                        for m in (2 * (b - hidden), 2 * (b - hidden) + 1):
                            if name == "ffn":
                                act.wait_ge(s["acc_added"], m + 1)
                                square(24 + m, Fo[:, m, :])
                            else:
                                act.wait_ge(x_ready, 32 + m + 1)
                                square(64 + m, XT[:, m, :])

            with act.Fori(0, 2) as i:
                group("ffn", i, 8)
            group("ffn", 2, 6)
            norm_root(3)

            for m in range(KT):
                act.wait_ge(x_ready, 8 + m + 1)
                square(32 + m, XT[:, m, :])
            norm_root(4)
            for b in range(12):
                ahead(B0["mix"] + b)
                for t in (2 * b, 2 * b + 1):
                    take_s(T0["mix"] + t, E0["mix"] + t, ACT.Sigmoid if t < 8 and t % 2 else ACT.Copy)

            for m in range(KT):
                n, t, e = B0["gate"] + 2 * m, T0["gate"] + 5 * m, E0["gate"] + 5 * m
                ahead(n)
                take_s(t, e, ACT.Sigmoid)
                take_s(t + 1, e + 1, ACT.Sigmoid)
                ahead(n + 1)
                if m == 0:
                    for c in range(4):
                        act.wait_ge(s["la_d"], c + 1)
                        if c >= 2:
                            act.wait_ge(s["la_sum"], c - 1)
                        actv(sq[:, c % 2, :], CA[:, c, :], ACT.Square).then_inc(s["la_sq"], 1)
                    act.wait_ge(s["la_var"], 1)
                    actv(sq[:, 0, :], mb[:, 1, :], ACT.Sqrt, bias=cs("eps", 0, 1),
                         scale=2.0 / D).then_inc(s["la_sd"], 1)
                    for c in range(4):
                        act.wait_ge(s["la_y"], c + 1)
                        actv(CA[:, c, :], CA[:, c, :], ACT.Silu, bias=pr("ln_a_b", c),
                             scale=pr("ln_a_g", c)).then_inc(s["la_act"], 1)
                take_s(t + 2, e + 2, ACT.Sigmoid)
                take_s(t + 3, e + 3)
                take_s(t + 4, e + 4)

            act.wait_ge(in_mem, 16)
            for k in range(KT):
                square(40 + k, MT[:, k, :])
            for b in range(4):
                ahead(B0["o"] + b)
                for m in (2 * b, 2 * b + 1):
                    take_s(T0["o"] + m, E0["o"] + m)
                if b == 0:
                    norm_root(5, 2)
            for m in range(KT):
                act.wait_ge(x_ready, 16 + m + 1)
                square(48 + m, XT[:, m, :])

            for b in range(8):
                ahead(B0["kv"] + b)
                for j in range(2):
                    t = T0["kv"] + 2 * b + j
                    if b < 4:
                        direct(t, KX[:, 2 * b + j, :], acc[:, t % 4, 0:N_MEM])
                    else:
                        direct(t, VX[:, j, (b - 4) * 256:(b - 3) * 256], acc[:, t % 4, 0:256])
            norm_root(6)
            for b in range(4):
                ahead(B0["q"] + b)
                for j in range(2):
                    t = T0["q"] + 2 * b + j
                    direct(t, QX[:, 2 * b + j, :], acc[:, t % 4, :], 1.0 / 16.0)

            def x_exp(u):
                act.wait_ge(s["xs_mx"], u + 1)
                actv(EXx[:, u % 2, :], x_bank(u), ACT.Exp, bias=nmx[:, u % 4:u % 4 + 1],
                     accum_out=den[:, u % 4:u % 4 + 1]).then_inc(s["xs_e"], 1)

            def x_turned(u):
                h, i = divmod(u, TT)
                act.wait_ge(s["xs_t"], u + 1)
                if i == 0 and h:
                    act.wait_ge(s["xs_o"], 2 * h)
                actv(PTx[:, :, i * P:(i + 1) * P], mb[:, 2 + u % 2, 0:2 * P].rearrange("p (a b) -> p a b", a=2),
                     ACT.Copy).then_inc(s["xs_te"], 1)

            x_exp(0)
            for u in range(4 * TT):
                if u + 1 < 4 * TT:
                    x_exp(u + 1)
                x_turned(u)
                if u % TT == TT - 1:
                    h = u // TT
                    for v in range(2):
                        act.wait_ge(s["xs_o"], 2 * h + v + 1)
                        actv(XH[:, 2 * h + v, :], acc[:, v, :], ACT.Copy).then_inc(s["xs_hi"], 1)
            for b in range(4):
                ahead(B0["xo"] + b)
                for m in (2 * b, 2 * b + 1):
                    take_s(T0["xo"] + m, E0["xo"] + m)
            for m in range(KT):
                act.wait_ge(x_ready, 24 + m + 1)
                square(56 + m, XT[:, m, :])

            def places(i):
                for e in range(4):
                    act.wait_ge(s["f_turn"], i * 4 + (e + 1))
                    actv(G2[:, e, :], mb[:, 2 + e % 2, :], ACT.Copy).then_inc(s["f_turned"], 1)

            def gathered_upper(i, k):
                act.wait_ge(s["f_gath"], i * 8 + (k + 1))
                actv(XH[:, k, :], acc[:, 2 + k % 2, :], ACT.Copy).then_inc(s["f_xh"], 1)

            def gathered(i, last=False):
                n0, t0 = B0["moe"], T0["moe"]

                def next_block(b):
                    if last:
                        ahead(n0 + 36 + b)
                    else:
                        ahead(n0 + b, i)

                def hidden_upper(b):
                    act.wait_ge(s["f_ht"], i * 8 + (b + 1))
                    actv(GHH[:, b, :], mb[:, 2 + b % 2, 0:P], ACT.Copy).then_inc(s["f_hh"], 1)

                next_block(0)
                for b in range(8):
                    act.wait_ge(acc_ready, i * 24 + (t0 + 2 * b + 2))
                    actv(tmp[:, b % 2, 0:P], acc[:, b % 2, 0:P], ACT.Silu).then_inc(s["f_silu"], 1)
                    if b:
                        hidden_upper(b - 1)
                    next_block(b + 1)
                if last:
                    hidden_upper(7)
                else:
                    gathered_upper(i + 1, 0)
                    hidden_upper(7)
                    for k in range(1, KT):
                        gathered_upper(i + 1, k)
                for b in range(4):
                    if b:
                        next_block(8 + b)
                    act.wait_ge(s["f_y"], i * 4 + (b + 1))
                    actv(YH[:, b % 2, 0:2, :].rearrange("p a b -> p (a b)"), mb[:, 0, :],
                         ACT.Copy).then_inc(s["f_yh"], 1)
                    act.wait_ge(acc_ready, i * 24 + (t0 + 16 + 2 * b + 2))
                    actv(YH[:, b % 2, 2:4, :].rearrange("p a b -> p (a b)"), mb[:, 1, :],
                         ACT.Copy).then_inc(s["f_yh"], 1)
                    if last and b:
                        last_squares(b - 1)
                if last:
                    last_squares(3)
                else:
                    places(i + 1)

            def last_squares(b):
                for m in (2 * b, 2 * b + 1):
                    act.wait_ge(s["f_add"], 24 + m + 1)
                    square(64 + m, XT[:, m, :])

            norm_root(7)
            for q in range(16):
                t, half = q // 4, q // 2 % 2
                act.wait_ge(s["f_tok"], q + 1)
                actv((TXH, TXL)[q % 2][:, t, 512 * half:512 * half + 512], acc[:, q % 4, :],
                     ACT.Copy).then_inc(s["f_toke"], 1)
            act.wait_ge(s["rt_sub"], 1)
            actv(rt[:, 2, :], rt[:, 1, :], ACT.Exp).then_inc(s["rt_exp"], 1)
            act.wait_ge(s["rt_sub"], 2)
            actv(rt[:, 12, :], rt[:, 11, :], ACT.Exp).then_inc(s["rt_exp"], 1)
            act.wait_ge(s["f_flag"], 1)
            crowded = act.value_load(flag[0:1, 0:1])
            with act.If(crowded > 0):
                with act.Fori(0, 3) as i:
                    group("moe", i, 8)
                group("moe", 3, 8)
            with act.Else():
                for k in range(KT):
                    gathered_upper(0, k)
                places(0)
                with act.Fori(0, 3) as i:
                    gathered(i)
                gathered(3, last=True)
            norm_root(8)

        @block.vector
        def _(dve):
            v = nc.vector
            state = {"sem": dchain, "base": 0, "n": 0}

            def link(ins):
                state["n"] += 1
                ins.then_inc(state["sem"], 1)
                dve.wait_ge(state["sem"], state["base"] + state["n"])

            def loop(count, per, body):
                b, n = state["base"], state["n"]
                with dve.Fori(0, count) as i:
                    state["base"], state["n"] = i * per + (b + n), 0
                    body(i)
                    assert state["n"] == per, state["n"]
                state["base"], state["n"] = b, n + count * per

            def add_squares(q, w=S):
                dve.wait_ge(sq_ready, q + 1)
                if q % KT == 0:
                    v.tensor_copy(sqa[:, 0:w], sq[:, q % 2, 0:w]).then_inc(sq_used, 1)
                else:
                    dve.wait_ge(sq_used, q)
                    v.tensor_tensor(sqa[:, 0:w], sqa[:, 0:w], sq[:, q % 2, 0:w], ALU.add).then_inc(sq_used, 1)

            def norm_recip(r, nt=TT):
                dve.wait_ge(sd_ready, r + 1)
                v.reciprocal(rs[:, 0:nt], sd[:, 0:nt]).then_inc(rs_ready, 1)

            def split(src, hi, lo, done):
                link(v.tensor_copy(hi, src))
                v.tensor_tensor(lo, src, hi.bitcast(F32), ALU.subtract).then_inc(done, 1)

            def operand(r, gname):
                dve.wait_ge(rb_ready, r + 1)
                for k in range(KT):
                    link(v.scalar_tensor_tensor(out=tmp[:, k % 2, :], in0=XT[:, k, :], scalar=pr(gname, k),
                                                in1=mb[:, 1, :], op0=ALU.mult, op1=ALU.mult))
                    split(tmp[:, k % 2, :], XH[:, k, :], XL[:, k, :], xn_ready)

            def residual(r, gname, q):
                dve.wait_ge(rb_ready, r + 1)
                for m in range(KT):
                    link(v.scalar_tensor_tensor(out=tmp[:, m % 2, :], in0=Fo[:, m, :], scalar=pr(gname, m),
                                                in1=mb[:, 1, :], op0=ALU.mult, op1=ALU.mult))
                    v.tensor_tensor(XT[:, m, :], XT[:, m, :], tmp[:, m % 2, :], ALU.add).then_inc(x_ready, 1)
                    if m:
                        add_squares(q + m - 1)
                add_squares(q + KT - 1)

            link(v.memset(ev[:, :, 0:2], 0.0))

            for k in range(KT):
                add_squares(k)
            norm_recip(0)
            dve.wait_ge(in_par, 64)
            operand(0, "ln_attn_pre")
            dsts = [LO[:, :], GLO[:, :]] + [K[:, c, :] for c in range(4)] + [R[:, c, :] for c in range(4)] \
                + [V[:, c, :] for c in range(4)]
            for t, dst in enumerate(dsts):
                dve.wait_ge(evac, t + 1)
                e = ev[:, t % 4, :]
                link(v.tensor_tensor(tmp[:, t % 2, :], e[:, 1:S + 1], e[:, 2:S + 2], ALU.subtract))
                v.scalar_tensor_tensor(out=dst, in0=tmp[:, t % 2, :], scalar=pr("mu", t), in1=e[:, 2:S + 2],
                                       op0=ALU.mult, op1=ALU.add).then_inc(ev_used, 1)
            o = PO["lam"][0]
            for j in range(2):
                a, b = par[:, o + 128 * j:o + 128 * j + 64], par[:, o + 128 * j + 64:o + 128 * j + 128]
                link(v.tensor_tensor(tmp[:, 0, 64 * j:64 * j + 64], a, b, ALU.mult))
            v.tensor_reduce(lam_d, tmp[:, 0, 0:128].rearrange("p (a b) -> p a b", a=2), AX.X,
                            ALU.add).then_inc(s["lam_dot"], 1)
            dve.wait_ge(s["lam_exp"], 1)
            link(v.tensor_tensor(lam_n, lam_e[:, 1:2], lam_e[:, 0:1], ALU.subtract))
            link(v.tensor_scalar(lam_n, lam_n, -LAM_INIT, None, ALU.add))
            link(v.tensor_scalar(g08, pr("subln", 0), 1.0 - LAM_INIT, None, ALU.mult))

            def att_max(u):
                h, i = divmod(u, TT)
                w = (i + 1) * P
                slope = 2.0 ** (-8.0 * (h + 1) / 4)
                dve.wait_ge(s["at_sc"], u + 1)
                if u >= 2:
                    dve.wait_ge(s["at_t"], u - 1)
                for c in range(2):
                    link(v.scalar_tensor_tensor(out=SC[:, u % 2, c, 0:w], in0=cs("alibi", S - w, S), scalar=slope,
                                                in1=mb[:, 2 + c, 0:w], op0=ALU.mult, op1=ALU.add))
                x = slice(2 * (u % 2), 2 * (u % 2) + 2)
                link(v.tensor_reduce(mx[:, x], SC[:, u % 2, :, 0:w], AX.X, ALU.max))
                v.tensor_scalar(nmx[:, x], mx[:, x], -1.0, None, ALU.mult).then_inc(s["at_mx"], 1)

            def att_weights(u):
                w, x = (u % TT + 1) * P, 2 * (u % 2)
                a, b = SC[:, u % 2, 0, 0:w], SC[:, u % 2, 1, 0:w]
                dve.wait_ge(s["at_e"], u + 1)
                link(v.reciprocal(rden[:, x:x + 2], den[:, x:x + 2]))
                link(v.tensor_scalar(rden[:, x + 1:x + 2], rden[:, x + 1:x + 2], lam_n, None, ALU.mult))
                link(v.tensor_scalar(a, a, rden[:, x:x + 1], None, ALU.mult))
                v.scalar_tensor_tensor(out=a, in0=b, scalar=rden[:, x + 1:x + 2], in1=a, op0=ALU.mult,
                                       op1=ALU.add).then_inc(s["at_p"], 1)

            def head_norm(h):
                dve.wait_ge(s["at_sd"], h + 1)
                link(v.reciprocal(tmp[:, 0, :], SQO[:, 1, :]))
                v.scalar_tensor_tensor(out=OO[:, h, :], in0=mb[:, 3, :], scalar=g08, in1=tmp[:, 0, :],
                                       op0=ALU.mult, op1=ALU.mult).then_inc(s["at_done"], 1)

            def decay(ct):
                if ct < 4:
                    W = Wt[ct % 2]
                    v.tensor_scalar(W[:, 4, :], K[:, ct, :], pr("k_k", ct), None, ALU.mult).then_inc(s["rk_kk"], 1)
                    dve.wait_ge(s["rk_sig"], ct + 1)
                    link(v.tensor_scalar(W[:, 0, :], W[:, 0, :], -DECAY_SCALE, None, ALU.mult))
                    link(v.tensor_tensor_scan(W[:, 2, :], cs("reset"), W[:, 0, :], 0.0, ALU.mult, ALU.add))
                    v.tensor_tensor(W[:, 3, :], W[:, 2, :], W[:, 0, :], ALU.subtract).then_inc(s["rk_cum"], 1)

            def key_norm(ct):
                if ct < 4:
                    dve.wait_ge(s["rk_kss"], ct + 1)
                    v.tensor_scalar(Wt[ct % 2][:, 5, :], bank(1, 1), 1e-24, None, ALU.max).then_inc(s["rk_kmx"], 1)

            def pc_of(ct):
                a = Wt[ct % 2][:, 6, :].rearrange("p (c j) -> p c j", c=NCH)
                return a[:, :, HD - 1:HD].to_broadcast([P, NCH, HD])

            def scaled(ct):
                if ct < 4:
                    W = Wt[ct % 2]
                    Kc = K[:, ct, :]
                    dve.wait_ge(s["rk_cum"], ct + 1)
                    link(v.tensor_scalar(W[:, 0, :], W[:, 1, :], -1.0, pr("k_a", ct), ALU.add, ALU.mult))
                    link(v.scalar_tensor_tensor(out=Kc, in0=W[:, 0, :], scalar=1.0, in1=Kc, op0=ALU.add,
                                                op1=ALU.mult))

            def hats(ct):
                if ct < 4:
                    W = Wt[ct % 2]
                    dve.wait_ge(s["rk_ksd"], ct + 1)
                    link(v.reciprocal(W[:, 5, :], W[:, 5, :]))
                    link(v.tensor_tensor(W[:, 4, :], W[:, 4, :], W[:, 5, :], ALU.mult))
                    link(v.tensor_tensor(W[:, 1, :], W[:, 4, :], W[:, 1, :], ALU.mult))

            def hat(ct):
                if ct < 4:
                    W = Wt[ct % 2]
                    Kc, Rc = K[:, ct, :], R[:, ct, :]
                    dve.wait_ge(s["rk_exp"], ct + 1)
                    ch = lambda a: a.rearrange("p (t c) -> p t c", t=TT)
                    v.scalar_tensor_tensor(out=AR[:, :, 0, :], in0=ch(W[:, 4, :]), scalar=-1.0, in1=ch(W[:, 3, :]),
                                           op0=ALU.mult, op1=ALU.mult)
                    v.tensor_tensor(AR[:, :, 1, :], ch(Rc), ch(W[:, 6, :]), ALU.mult)
                    v.tensor_tensor(BT[:, :], W[:, 1, :], W[:, 7, :], ALU.mult)
                    link(v.tensor_tensor(KH[:, :], Kc, W[:, 7, :], ALU.mult))

            def ends(ct):
                if ct < 4:
                    W = Wt[ct % 2]
                    Kc, Rc = K[:, ct, :], R[:, ct, :]
                    cw = lambda a: a.rearrange("p (c j) -> p c j", c=NCH)
                    v.tensor_tensor(cw(W[:, 0, :]), cw(BT[:, :]), pc_of(ct), ALU.mult)
                    v.tensor_tensor(cw(W[:, 2, :]), cw(KH[:, :]), pc_of(ct), ALU.mult)
                    v.scalar_tensor_tensor(out=W[:, 3, :], in0=Rc, scalar=pr("r_k", ct), in1=Kc, op0=ALU.mult,
                                           op1=ALU.mult).then_inc(s["rk_hat"], 1)

            def tok(ct):
                dve.wait_ge(s["rk_bsum"], ct + 1)
                v.tensor_tensor(BON[:, :], acc[:, 0, :], V[:, ct, :], ALU.mult).then_inc(s["rk_bonus"], 1)

            def masked(dst, ready, done):
                def run(ct):
                    mask = cs("mask_nr").unsqueeze(1).to_broadcast([P, 2, 2 * P])
                    for hh in range(2):
                        dve.wait_ge(ready, 2 * ct + hh + 1)
                        for x in range(2):
                            last = v.tensor_tensor(dst[:, hh, 2 * x:2 * x + 2].rearrange("p t a b -> p t (a b)"),
                                                   bank(hh, x).rearrange("p (t c) -> p t c", t=2), mask, ALU.mult)
                        last.then_inc(done, 1)
                return run

            def by_tok(a):
                return a.rearrange("p (t c) -> p t c", t=TT)

            def lv(l):
                return cs("mask_lv", l * P, (l + 1) * P).unsqueeze(1).to_broadcast([P, TT, P])

            def l0(ct):
                for hh in range(2):
                    dve.wait_ge(s["rk_q"], 12 * ct + hh + 1)
                    link(v.tensor_tensor(Qm[:, hh], by_tok(bank(hh, 0)), lv(0), ALU.mult))
                    v.tensor_tensor(Tm[:, hh], Qm[:, hh], ident.unsqueeze(1).to_broadcast([P, TT, P]),
                                    ALU.add).then_inc(s["rk_tm"], 1)

            def level(l):
                def run(ct):
                    for hh in range(2):
                        dve.wait_ge(s["rk_q"], 12 * ct + 2 * l + hh + 1)
                        v.tensor_tensor(Qm[:, hh], by_tok(bank(hh, 0)), lv(l), ALU.mult).then_inc(s["rk_qm"], 1)
                    for hh in range(2):
                        dve.wait_ge(s["rk_t"], 10 * ct + 2 * (l - 1) + hh + 1)
                        v.tensor_tensor(Tm[:, hh], Tm[:, hh], by_tok(bank(hh, 1)), ALU.add).then_inc(s["rk_tm"], 1)
                return run

            def gh(ct):
                GT, ST, HS = GTt[ct % 2], STt[ct % 2], HSt[ct % 2]
                link(v.tensor_tensor(GT[:, :, :], cs("id64").unsqueeze(1).to_broadcast([P, NCH, HD]), pc_of(ct),
                                     ALU.mult))
                for hh in range(2):
                    ps = slice(HD * hh, HD * hh + HD)
                    dve.wait_ge(s["rk_z"], 2 * ct + hh + 1)
                    v.tensor_tensor(Z[ps, :, :], by_tok(bank(hh, 1)[ps]), AR[ps, :, 1, :],
                                    ALU.add).then_inc(s["rk_zs"], 1)
                dve.wait_ge(s["rk_hs"], ct + 1)
                g2 = GT[:, :, :].rearrange("p (t a) j -> p a t j", a=2)
                v.tensor_tensor(g2, g2, acc[:, 0:2, 0:256].rearrange("p a (t j) -> p a t j", t=TT),
                                ALU.add).then_inc(s["rk_gs"], 1)
                v.tensor_copy(ST[:, 1, :], HS[:, 0, :]).then_inc(s["rk_st"], 1)

            def enter(c):
                def run(ct):
                    dve.wait_ge(s["rk_s"], 6 * ct + c - 1)
                    v.tensor_tensor(STt[ct % 2][:, c, :], mb[:, 0, 0:HD], HSt[ct % 2][:, c - 1, :],
                                    ALU.add).then_inc(s["rk_st"], 1)
                return run

            def y(ct):
                dve.wait_ge(s["rk_y"], ct + 1)
                v.tensor_tensor(Wt[ct % 2][:, 0, :], acc[:, 2, :], BON[:, :], ALU.add).then_inc(s["rk_ys"], 1)

            def mu(ct):
                W = Wt[ct % 2]
                dve.wait_ge(s["rk_mu"], ct + 1)
                v.scalar_tensor_tensor(out=W[:, 1, :], in0=mb[:, 0, :], scalar=-1.0 / HD, in1=W[:, 0, :],
                                       op0=ALU.mult, op1=ALU.add).then_inc(s["rk_d"], 1)

            def var(ct):
                W = Wt[ct % 2]
                dve.wait_ge(s["rk_sd"], ct + 1)
                link(v.reciprocal(W[:, 3, :], W[:, 3, :]))
                link(v.tensor_tensor(W[:, 1, :], W[:, 1, :], W[:, 3, :], ALU.mult))
                link(v.tensor_scalar(W[:, 1, :], W[:, 1, :], pr("ln_x_w", ct), pr("ln_x_b", ct), ALU.mult, ALU.add))
                v.tensor_tensor(R[:, ct, :], W[:, 1, :], ev[:, ct % 2, 2:S + 2], ALU.mult).then_inc(s["rk_done"], 1)

            decay(0)
            key_norm(0)
            scaled(0)
            hats(0)
            hat(0)
            ends(0)
            main = {"tok": tok, "nr": masked(NR, s["rk_nr"], s["rk_nrm"]),
                    "ak": masked(AKRK, s["rk_ak"], s["rk_akm"]), "l0": l0, "gh": gh, "y": y, "mu": mu, "var": var}
            main |= {f"l{l}": level(l) for l in range(1, LEVELS)} | {f"s{c}": enter(c) for c in range(2, NCH)}
            in_beats(main, {"max": att_max, "weights": att_weights, "head_norm": head_norm, "decay": decay,
                            "key_norm": key_norm, "scaled": scaled, "hats": hats, "hat": hat, "ends": ends})

            dve.wait_ge(s["rk_done"], 4)
            for k in range(KT):
                src = R[:, k, :] if k < 4 else OO[:, k - 4, :]
                split(src, XH[:, k, :], XL[:, k, :], s["mixed"])
            for m in range(KT):
                add_squares(8 + m)
            norm_recip(1)
            dve.wait_ge(in_x2, 16)
            residual(1, "ln_attn_post", 16)

            def conv3(dst, e, w, b=None, done=None):
                if b is None:
                    link(v.tensor_scalar(dst, e[:, 2:S + 2], w[2], None, ALU.mult))
                else:
                    link(v.tensor_scalar(dst, e[:, 2:S + 2], w[2], b, ALU.mult, ALU.add))
                link(v.scalar_tensor_tensor(out=dst, in0=e[:, 1:S + 1], scalar=w[1], in1=dst, op0=ALU.mult,
                                            op1=ALU.add))
                return v.scalar_tensor_tensor(out=dst, in0=e[:, 0:S], scalar=w[0], in1=dst, op0=ALU.mult, op1=ALU.add)

            def lower_rest(b, i=0):
                if isinstance(i, int) and 12 * i + b >= 48:
                    return
                n = B0["moe"] + b
                dve.wait_ge(hi_done, i * 12 + (n + 1))
                v.tensor_tensor(wl[:, n % RING, KT - K_DVE:].rearrange("p a b c -> p (a b c)"),
                                raw[:, n % RING, (KT - K_DVE) * 2 * P:],
                                wh[:, n % RING, KT - K_DVE:].rearrange("p a b c -> p (a b c)").bitcast(F32),
                                ALU.subtract).then_inc(s["low_dve"], 1)

            def group(name, i, hidden, last=False):
                loop_i = not isinstance(i, int)
                k = 0 if loop_i else i
                t0, e0 = T0[name] + 24 * k, E0[name] + 24 * k
                add = (lambda x, per: i * per + x) if loop_i else (lambda x, per: x)
                h0 = {"ffn": 0, "moe": 22}[name] + 8 * k
                if name == "ffn":
                    src = par[:, PO["conv"][0] + 64 * i:PO["conv"][0] + 64 * i + 64] if not loop_i else \
                        par[:, bass.ds(i * 64 + PO["conv"][0], 64)]
                    link(v.tensor_copy(cpar[:, :], src))
                else:
                    gsrc = gateg[:, :, :, :].rearrange("p g t e -> p (g t e)")
                    src = gsrc[:, 16 * i:16 * i + 16] if not loop_i else gsrc[:, bass.ds(i * 16, 16)]
                    v.tensor_copy(gcur[:, :, :].rearrange("p t e -> p (t e)"), src).then_inc(s["gate_ready"], 1)
                for b in range(hidden):
                    dve.wait_ge(evac, add(t0 + 2 * b + 1, 24))
                    ea, eb = ev[:, (e0 + 2 * b) % 4, :], ev[:, (e0 + 2 * b + 1) % 4, :]
                    if name == "ffn":
                        c = [cpar[:, 8 * b + x:8 * b + x + 1] for x in range(8)]
                        conv3(gl[:, b % 2, :], ea, c[0:3], c[3]).then_inc(ev_used, 1)
                        dve.wait_ge(evac, add(t0 + 2 * b + 2, 24))
                        conv3(yv[:, b % 2, :], eb, c[4:7], c[7]).then_inc(ev_used, 1)
                        dve.wait_ge(ev_used, add(e0 + 2 * b + 2, 24))
                        dve.wait_ge(s["gelu_done"], add(8 * k + b + 1, 8))
                        link(v.tensor_tensor(tmp[:, b % 2, :], gl[:, b % 2, :], yv[:, b % 2, :], ALU.mult))
                    else:
                        dve.wait_ge(evac, add(t0 + 2 * b + 2, 24))
                        v.tensor_tensor(gl[:, b % 2, :], ea[:, 2:S + 2], eb[:, 2:S + 2],
                                        ALU.mult).then_inc(ev_used, 2)
                        dve.wait_ge(ev_used, add(e0 + 2 * b + 2, 24))
                        dve.wait_ge(s["gb_ready"], add(4 * k + b // 2 + 1, 4))
                        link(v.tensor_tensor(tmp[:, b % 2, :], gl[:, b % 2, :], mb[:, 2 + b // 2 % 2, :], ALU.mult))
                    split(tmp[:, b % 2, :], HH[:, b, :], HL[:, b, :], s["hid_ready"])
                    if name == "moe":
                        lower_rest(b + 2, i)
                dst = Fo if name == "ffn" else XT
                for m in range(KT):
                    dve.wait_ge(evac, add(t0 + 2 * hidden + m + 1, 24))
                    e = ev[:, (e0 + 2 * hidden + m) % 4, 2:S + 2]
                    link(v.tensor_tensor(dst[:, m, :], dst[:, m, :], e, ALU.add))
                    v.nop().then_inc(ev_used, 1)
                    if name == "moe" and m % 2:
                        lower_rest(8 + m // 2 + 2, i)
                    if last:
                        v.nop().then_inc(s["acc_added"] if name == "ffn" else x_ready, 1)
                        if m:
                            add_squares((24 if name == "ffn" else 64) + m - 1)
                if last:
                    add_squares((24 if name == "ffn" else 64) + KT - 1)

            norm_recip(2)
            operand(2, "ln_ffn_pre")
            link(v.memset(Fo[:, :, :], 0.0))
            loop(2, 1 + 8 * 6 + 8, lambda i: group("ffn", i, 8))
            group("ffn", 2, 6, last=True)
            norm_recip(3)
            residual(3, "ln_ffn_post", 32)
            norm_recip(4)
            operand(4, "norm_mix")
            link(v.memset(APAD[:, :, 0:CONV_A - 1], 0.0))
            link(v.memset(cpad[:, 0:2], 0.0))
            link(v.memset(upad[:, :, 0:POOL_PAD], 0.0))
            t0, e0 = T0["mix"], E0["mix"]
            taps = [(c, j) for c in range(4) for j in range(TAPS)] \
                + [(c, j) for j in range(TAPS, CONV_A) for c in range(4)]

            def tap():
                c, j = taps.pop(0)
                x, w = APAD[:, c, j:j + S], pr("conv_a_w", c * CONV_A + j)
                if j == 0:
                    link(v.tensor_scalar(CA[:, c, :], x, w, pr("conv_a_b", c), ALU.mult, ALU.add))
                else:
                    link(v.scalar_tensor_tensor(out=CA[:, c, :], in0=x, scalar=w, in1=CA[:, c, :],
                                                op0=ALU.mult, op1=ALU.add))

            for c in range(4):
                dve.wait_ge(evac, t0 + 2 * c + 2)
                v.tensor_tensor(APAD[:, c, CONV_A - 1:], ev[:, (e0 + 2 * c) % 4, 2:S + 2],
                                ev[:, (e0 + 2 * c + 1) % 4, 2:S + 2], ALU.mult).then_inc(ev_used, 2)
                dve.wait_ge(ev_used, e0 + 2 * c + 2)
                for _ in range(TAPS):
                    tap()
            for c in range(4):
                t, e = t0 + 8 + 3 * c, e0 + 8 + 3 * c
                for _ in range(9):
                    tap()
                dve.wait_ge(evac, t + 2)
                v.tensor_tensor(cpad[:, 2:], ev[:, e % 4, 2:S + 2], ev[:, (e + 1) % 4, 2:S + 2],
                                ALU.mult).then_inc(ev_used, 2)
                dve.wait_ge(ev_used, e + 2)
                link(conv3(tmp[:, 0, :], cpad, [pr("conv_c", 3 * c + x) for x in range(3)]))
                dve.wait_ge(evac, t + 3)
                v.tensor_tensor(tmp[:, 1, :], tmp[:, 0, :], ev[:, (e + 2) % 4, 2:S + 2],
                                ALU.mult).then_inc(ev_used, 1)
                dve.wait_ge(ev_used, e + 3)
                split(tmp[:, 1, :], CH[:, c, :], CL[:, c, :], dchain)
                state["n"] += 1
                for _ in range(6):
                    tap()
            for g in range(4):
                t, e = t0 + 20 + g, e0 + 20 + g
                for _ in range(5):
                    if taps:
                        tap()
                dve.wait_ge(evac, t + 1)
                x = ev[:, e % 4, :]
                cur, oth = upad[:, 0, :], upad[:, 1, :]
                link(v.tensor_tensor(cur[:, POOL_PAD:], x[:, 2:S + 2], x[:, 1:S + 1], ALU.add))
                for step in [2, 4, 8][:g]:
                    link(v.tensor_tensor(oth[:, POOL_PAD:], cur[:, POOL_PAD:],
                                         cur[:, POOL_PAD - step:POOL_PAD - step + S], ALU.add))
                    cur, oth = oth, cur
                link(v.scalar_tensor_tensor(out=PL[:, g, :], in0=cur[:, POOL_PAD:], scalar=0.5 ** (g + 1),
                                            in1=x[:, 2:S + 2], op0=ALU.mult, op1=ALU.subtract))
                link(v.tensor_tensor(tmp[:, 0, 0:POOL_PAD], cur[:, POOL_PAD:2 * POOL_PAD],
                                     cs("invcnt", g * POOL_PAD, (g + 1) * POOL_PAD), ALU.mult))
                v.tensor_tensor(PL[:, g, 0:POOL_PAD], tmp[:, 0, 0:POOL_PAD], x[:, 2:POOL_PAD + 2],
                                ALU.subtract).then_inc(ev_used, 1)
                dve.wait_ge(ev_used, e + 1)
            while taps:
                tap()

            link(v.tensor_tensor(sqa[:, :], CA[:, 0, :], CA[:, 1, :], ALU.add))
            link(v.tensor_tensor(sqa[:, :], sqa[:, :], CA[:, 2, :], ALU.add))
            v.tensor_tensor(sqa[:, :], sqa[:, :], CA[:, 3, :], ALU.add).then_inc(s["la_in"], 1)
            dve.wait_ge(s["la_mu"], 1)
            for c in range(4):
                v.scalar_tensor_tensor(out=CA[:, c, :], in0=mb[:, 0, :], scalar=-2.0 / D, in1=CA[:, c, :],
                                       op0=ALU.mult, op1=ALU.add).then_inc(s["la_d"], 1)
            for c in range(4):
                dve.wait_ge(s["la_sq"], c + 1)
                if c == 0:
                    v.tensor_copy(sqa[:, :], sq[:, 0, :]).then_inc(s["la_sum"], 1)
                else:
                    dve.wait_ge(s["la_sum"], c)
                    v.tensor_tensor(sqa[:, :], sqa[:, :], sq[:, c % 2, :], ALU.add).then_inc(s["la_sum"], 1)
            dve.wait_ge(s["la_sd"], 1)
            link(v.reciprocal(tmp[:, 0, :], sq[:, 0, :]))
            for c in range(4):
                v.tensor_tensor(CA[:, c, :], CA[:, c, :], tmp[:, 0, :], ALU.mult).then_inc(s["la_y"], 1)
            for c in range(4):
                dve.wait_ge(s["la_act"], c + 1)
                split(CA[:, c, :], AH[:, c, :], AL[:, c, :], s["ac_ready"])
            dve.wait_ge(s["ac_ready"], 4)
            for m in range(KT):
                t, e = T0["gate"] + 5 * m, E0["gate"] + 5 * m
                tile = lambda x: ev[:, (e + x) % 4, 2:S + 2]
                dve.wait_ge(s["p_mm"], m + 1)
                dve.wait_ge(evac, t + 2)
                link(v.scalar_tensor_tensor(out=tmp[:, 0, :], in0=mb[:, 2 + m % 2, :], scalar=pr("pool_scale", m),
                                            in1=tile(1), op0=ALU.mult, op1=ALU.mult))
                dve.wait_ge(evac, t + 4)
                v.tensor_tensor(tmp[:, 1, :], tile(0), tile(3), ALU.mult).then_inc(ev_used, 2)
                dve.wait_ge(ev_used, e + 2)
                link(v.tensor_tensor(MG[:, m, :], tmp[:, 0, :], tmp[:, 1, :], ALU.add))
                dve.wait_ge(evac, t + 5)
                v.tensor_tensor(tmp[:, 1, :], tile(2), tile(4), ALU.mult).then_inc(ev_used, 3)
                dve.wait_ge(ev_used, e + 5)
                v.tensor_tensor(MG[:, m, :], MG[:, m, :], tmp[:, 1, :], ALU.add).then_inc(s["mg_ready"], 1)

            def add_tile(name, m):
                dve.wait_ge(evac, T0[name] + m + 1)
                link(v.tensor_tensor(XT[:, m, :], XT[:, m, :], ev[:, (E0[name] + m) % 4, 2:S + 2], ALU.add))
                v.nop().then_inc(ev_used, 1)
                v.nop().then_inc(x_ready, 1)

            dve.wait_ge(s["mg_ready"], KT)
            for k in range(KT):
                split(MG[:, k, :], XH[:, k, :], XL[:, k, :], s["mg_ready"])
            for k in range(KT):
                add_squares(40 + k, N_MEM)
            add_tile("o", 0)
            add_tile("o", 1)
            norm_recip(5, 2)
            add_tile("o", 2)
            add_tile("o", 3)
            dve.wait_ge(rb_ready, 6)
            for k in range(KT):
                link(v.scalar_tensor_tensor(out=tmp[:, k % 2, 0:N_MEM], in0=MT[:, k, :], scalar=pr("norm_mem", k),
                                            in1=mb[:, 1, 0:N_MEM], op0=ALU.mult, op1=ALU.mult))
                split(tmp[:, k % 2, 0:N_MEM], MH[:, k, :], ML[:, k, :], s["mem_ready"])
            for m in range(4, KT):
                add_tile("o", m)
            for m in range(KT):
                add_squares(48 + m)

            def x_max(u):
                dve.wait_ge(s["xs_sc"], u + 1)
                link(v.tensor_reduce(mx[:, u % 4:u % 4 + 1], x_bank(u), AX.X, ALU.max))
                v.tensor_scalar(nmx[:, u % 4:u % 4 + 1], mx[:, u % 4:u % 4 + 1], -1.0, None,
                                ALU.mult).then_inc(s["xs_mx"], 1)

            def x_weights(u):
                dve.wait_ge(s["xs_e"], u + 1)
                link(v.reciprocal(rden[:, u % 4:u % 4 + 1], den[:, u % 4:u % 4 + 1]))
                if u >= 2:
                    dve.wait_ge(s["xs_t"], u - 1)
                v.tensor_scalar(PX[:, u % 2, :], EXx[:, u % 2, :], rden[:, u % 4:u % 4 + 1], None,
                                ALU.mult).then_inc(s["xs_p"], 1)

            norm_recip(6)
            operand(6, "norm_x")
            x_max(0)
            x_max(1)
            for u in range(4 * TT):
                x_weights(u)
                if u + 2 < 4 * TT:
                    x_max(u + 2)
                if u % TT == TT - 1:
                    h = u // TT
                    for j in range(2):
                        dve.wait_ge(s["xs_hi"], 2 * h + j + 1)
                        v.tensor_tensor(XL[:, 2 * h + j, :], acc[:, j, :], XH[:, 2 * h + j, :].bitcast(F32),
                                        ALU.subtract).then_inc(s["xs_done"], 1)
            for m in range(KT):
                add_tile("xo", m)
            for m in range(KT):
                add_squares(56 + m)

            def route():
                r = lambda j: rt[:, j, :].rearrange("p (t c) -> p t c", t=TT)
                red = lambda j: rt[:, j, 0:TT]
                wide = lambda j: rt[:, j, 0:TT].unsqueeze(2).to_broadcast([P, TT, 4])
                rank = cs("rank").unsqueeze(1).to_broadcast([P, TT, 4])

                def best(p, eq, top, hot):
                    link(v.tensor_reduce(red(top), r(p), AX.X, ALU.max))
                    link(v.tensor_tensor(r(eq), r(p), wide(top), ALU.is_equal))
                    link(v.tensor_tensor(r(eq), r(eq), rank, ALU.mult))
                    link(v.tensor_reduce(red(23), r(eq), AX.X, ALU.max))
                    link(v.tensor_tensor(r(hot), r(eq), wide(23), ALU.is_equal))

                def softmax_in(src, to):
                    link(v.tensor_reduce(red(0), src, AX.X, ALU.max))
                    v.tensor_tensor(r(to), src, wide(0), ALU.subtract).then_inc(s["rt_sub"], 1)

                def softmax_out(p):
                    link(v.tensor_reduce(red(0), r(p), AX.X, ALU.add))
                    link(v.reciprocal(red(22), red(0)))
                    link(v.tensor_tensor(r(p), r(p), wide(22), ALU.mult))

                dve.wait_ge(s["rt_lg"], 1)
                link(v.tensor_tensor(lg[:, :, :], mb[:, 0, 0:TT * 20].rearrange("p (t c) -> p t c", t=TT),
                                     pr("b_router", 0, 20).unsqueeze(1).to_broadcast([P, TT, 20]), ALU.add))
                softmax_in(lg[:, :, 0:4], 1)
                dve.wait_ge(s["rt_exp"], 1)
                softmax_out(2)
                best(2, 3, 4, 5)
                for t in range(TT):
                    link(v.tensor_tensor(rt3[:, t], lg[:, t, 4:20].rearrange("p (g e) -> p g e", g=4),
                                         rt[:, 5, 4 * t:4 * t + 4].unsqueeze(2).to_broadcast([P, 4, 4]), ALU.mult))
                link(v.tensor_reduce(r(10), rt3[:, :, :, :].rearrange("p t g e -> p t e g"), AX.X, ALU.add))
                softmax_in(r(10), 11)
                dve.wait_ge(s["rt_exp"], 2)
                softmax_out(12)
                best(12, 13, 14, 15)
                link(v.scalar_tensor_tensor(out=r(16), in0=r(15), scalar=-2.0, in1=r(12), op0=ALU.mult, op1=ALU.add))
                best(16, 13, 17, 18)
                link(v.tensor_tensor(red(19), red(14), red(17), ALU.add))
                link(v.reciprocal(red(20), red(19)))
                link(v.tensor_tensor(red(20), red(20), red(4), ALU.mult))
                link(v.tensor_tensor(r(15), r(15), r(18), ALU.add))
                v.tensor_tensor(chosen[:, :, :, :], r(15).unsqueeze(1).to_broadcast([P, 4, TT, 4]),
                                r(5).rearrange("p t g -> p g t").unsqueeze(3).to_broadcast([P, 4, TT, 4]),
                                ALU.mult).then_inc(s["f_mask"], 1)
                dve.wait_ge(s["f_mask"], 1)
                link(v.tensor_tensor(r(15), r(15), r(12), ALU.mult))
                link(v.tensor_tensor(r(15), r(15), wide(20), ALU.mult))
                for g in range(4):
                    link(v.tensor_tensor(gateg[:, g], r(15), r(5)[:, :, g:g + 1].to_broadcast([P, TT, 4]), ALU.mult))

            def place(i):
                for src, dst, w in ((posn, pcur, 16), (gparts, gtwo, 32)):
                    src = src[:, :, :, :] if w == 16 else src[:, :, :, :, :]
                    src = src.rearrange("p g t e -> p (g t e)" if w == 16 else "p g t e x -> p (g t e x)")
                    src = src[:, w * i:w * i + w] if isinstance(i, int) else src[:, bass.ds(i * w, w)]
                    dst = dst[:, :, :].rearrange("p t e -> p (t e)") if w == 16 else \
                        dst[:, :, :, :].rearrange("p t e x -> p (t e x)")
                    done = v.tensor_copy(dst, src)
                link(done)
                v.tensor_tensor(G1[:, :, :, :].rearrange("p t e c -> p (t e) c"),
                                cs("count").unsqueeze(1).to_broadcast([P, 16, P]),
                                pcur[:, :, :].rearrange("p t e -> p (t e)").unsqueeze(2).to_broadcast([P, 16, P]),
                                ALU.is_equal).then_inc(s["f_g"], 1)

            def slot_gates(i):
                dve.wait_ge(s["f_gate"], i + 1)
                dve.wait_ge(s["f_hid"], i * 8)
                v.tensor_reduce(gslot[:, :], mb[:, 0, 0:8].rearrange("p (e x) -> p e x", x=2), AX.X,
                                ALU.add).then_inc(s["f_gslot"], 1)

            def gathered_lower(i, k):
                dve.wait_ge(s["f_xh"], i * 8 + (k + 1))
                v.tensor_tensor(XL[:, k, :], acc[:, 2 + k % 2, :], XH[:, k, :].bitcast(F32),
                                ALU.subtract).then_inc(s["f_xl"], 1)

            def gathered(i, last=False):
                if not last:
                    dve.wait_ge(s["f_turn"], i * 4 + 4)
                    place(i + 1)
                dve.wait_ge(s["f_gslot"], i + 1)

                def hidden_lower(b):
                    dve.wait_ge(s["f_hh"], i * 8 + (b + 1))
                    v.tensor_tensor(GHL[:, b, :], mb[:, 2 + b % 2, 0:P], GHH[:, b, :].bitcast(F32),
                                    ALU.subtract).then_inc(s["f_hl"], 1)

                for b in range(8):
                    dve.wait_ge(s["f_silu"], i * 8 + (b + 1))
                    v.scalar_tensor_tensor(out=tmp[:, b % 2, P:2 * P], in0=acc[:, b % 2, P:2 * P],
                                           scalar=gslot[:, b // 2:b // 2 + 1], in1=tmp[:, b % 2, 0:P],
                                           op0=ALU.mult, op1=ALU.mult).then_inc(s["f_hid"], 1)
                    lower_rest(b + 2, i)
                    if b:
                        hidden_lower(b - 1)
                lower_rest(10, i)
                if last:
                    hidden_lower(7)
                else:
                    slot_gates(i + 1)
                    gathered_lower(i + 1, 0)
                    hidden_lower(7)
                    for k in range(1, KT):
                        gathered_lower(i + 1, k)

                def added(b):
                    for j in range(2):
                        m = 2 * b + j
                        dve.wait_ge(s["f_out"], i * 8 + (m + 1))
                        if m == 0:
                            dve.wait_ge(s["f_add"], i * 8)
                        v.tensor_tensor(XT[:, m, :], XT[:, m, :], acc[:, 2 + j, :], ALU.add).then_inc(s["f_add"], 1)
                    if last:
                        for m in (2 * b, 2 * b + 1):
                            add_squares(64 + m)

                for b in range(4):
                    for x in range(2):
                        dve.wait_ge(s["f_yh"], i * 8 + (2 * b + x + 1))
                        v.tensor_tensor(YL[:, b % 2, 2 * x:2 * x + 2, :].rearrange("p a b -> p (a b)"), mb[:, x, :],
                                        YH[:, b % 2, 2 * x:2 * x + 2, :].rearrange("p a b -> p (a b)").bitcast(F32),
                                        ALU.subtract).then_inc(s["f_yl"], 1)
                    if b < 3:
                        lower_rest(11 + b, i)
                    if b:
                        added(b - 1)
                added(3)

            link(v.tensor_copy(identr[:, :], ident))
            o = PO["w_router"][0]
            wr = par[:, o:o + KT * 20].rearrange("p (k c) -> p k c", k=KT)
            split(wr, wrh[:, :, :], wrl[:, :, :], s["wr_ready"])
            norm_recip(7)
            operand(7, "norm_ffn")
            lower_rest(0)
            lower_rest(1)
            route()
            gp = gateg[:, :, :, :].rearrange("p g t e -> p (g t e)")
            gq = gparts[:, :, :, :, :].rearrange("p g t e x -> p (g t e) x")
            link(v.tensor_copy(gq[:, :, 0], gp))
            v.tensor_tensor(gq[:, :, 1], gp, gq[:, :, 0].bitcast(F32), ALU.subtract)
            dve.wait_ge(s["f_count"], 1)
            v.tensor_tensor(posn[:, :, :, :], mb[:, 0, 0:TT * 16].rearrange("p (t g e) -> p g t e", t=TT, g=4),
                            chosen[:, :, :, :], ALU.mult)
            link(v.tensor_reduce(most[:, 0:1], mb[:, 0, TT * 16:TT * 16 + 16], AX.X, ALU.max))
            link(v.tensor_scalar(most[:, 1:2], most[:, 0:1], P + 0.5, None, ALU.is_gt))
            v.tensor_copy(flag[:, :], most[:, 1:2]).then_inc(s["f_flag"], 1)
            dve.wait_ge(s["f_flag"], 1)
            crowded = dve.value_load(flag[0:1, 0:1])
            with dve.If(crowded > 0):
                loop(3, 16 + 8, lambda i: group("moe", i, 8))
                group("moe", 3, 8, last=True)
            with dve.Else():
                before = dict(state)
                state.update(sem=s["fchain"], base=0, n=0)
                place(0)
                slot_gates(0)
                for k in range(KT):
                    gathered_lower(0, k)
                loop(3, 1, gathered)
                gathered(3, last=True)
                state.update(before)
            norm_recip(8)
            dve.wait_ge(rb_ready, 9)
            for m in range(KT):
                v.scalar_tensor_tensor(out=XT[:, m, :], in0=XT[:, m, :], scalar=pr("norm_f", m), in1=mb[:, 1, :],
                                       op0=ALU.mult, op1=ALU.mult).then_inc(s["final_ready"], 1)



def pack(inputs):
    import numpy as np

    g = {n: np.asarray(a) for n, a in inputs.items()}
    W = {n: g[n][0] for n in ("w_in", "w_out", "w_up", "w_down", "w_in_2", "w_a_out_2", "w_c_out_2", "w_o_2",
                              "w_xq_2", "w_xkv_2", "w_xo_2", "w_e_gate_2", "w_e_up_2", "w_e_down_2")}

    def tile(w, c):
        t = w[:, c:c + P].reshape(-1, P, P).transpose(1, 0, 2)
        if t.shape[1] < KT:
            t = np.concatenate([t, np.zeros((P, KT - t.shape[1], P), t.dtype)], axis=1)
        return t

    tiles = []
    order = [12 * P, 13 * P] + [c * P for c in (4, 5, 6, 7, 0, 1, 2, 3, 8, 9, 10, 11)] \
        + [c * P for c in range(14, 26)]
    tiles += [tile(W["w_in"], c) for c in order]
    tiles += [tile(W["w_out"], m * P) for m in range(KT)]
    for a, b in ((0, 8), (8, 16), (16, 22)):
        for h in range(a, b):
            tiles += [tile(W["w_up"], h * P), tile(W["w_up"], D_FF + h * P)]
        tiles += [tile(W["w_down"][a * P:b * P], m * P) for m in range(KT)]
    w2 = W["w_in_2"]
    for c in range(4):
        tiles += [tile(w2, c * P), tile(w2, 512 + c * P)]
    for c in range(4):
        tiles += [tile(w2, o + c * P) for o in (2560, 1536, 2048)]
    tiles += [tile(w2, 1024 + c * P) for c in range(4)]
    for m in range(KT):
        tiles += [tile(w2, 3072 + x * D + m * P) for x in range(3)]
        tiles.append(np.concatenate([tile(W["w_a_out_2"], m * P)[:, :4], tile(W["w_c_out_2"], m * P)[:, :4]], axis=1))
    tiles += [tile(W["w_o_2"], m * P) for m in range(KT)]
    tiles += [tile(W["w_xkv_2"], m * P) for m in range(2 * KT)]
    tiles += [tile(W["w_xq_2"], m * P) for m in range(KT)]
    tiles += [tile(W["w_xo_2"], m * P) for m in range(KT)]
    down = W["w_e_down_2"].reshape(-1, D)
    for q in range(4):
        for e in range(4 * q, 4 * q + 4):
            for c in range(2):
                tiles += [tile(W["w_e_gate_2"][e], c * P), tile(W["w_e_up_2"][e], c * P)]
        tiles += [tile(down[q * D:(q + 1) * D], m * P) for m in range(KT)]
    ws = np.stack(tiles).reshape(NBLK, 2, P, KT, P).transpose(0, 2, 3, 1, 4)
    ws = np.ascontiguousarray(ws).reshape(NBLK, P, BLK)

    def cols(a):
        return np.asarray(a).reshape(-1, P).T

    def rows(a):
        return np.broadcast_to(np.asarray(a).reshape(1, -1), (P, np.asarray(a).size))

    mu = cols(g["mu_shift"][0])
    cw, cb = g["conv_w"][0], g["conv_b"][0]
    conv = []
    for h in range(22):
        for o in (0, D_FF):
            conv += [cw[x, o + h * P:o + (h + 1) * P] for x in range(3)] + [cb[o + h * P:o + (h + 1) * P]]
    conv = np.stack(conv + [np.zeros(P, cw.dtype)] * 16, axis=1)
    ca = np.concatenate([g["conv_a_w_2"][0][:, c * P:(c + 1) * P].T for c in range(4)], axis=1)
    cc = np.concatenate([g["conv_c_w_2"][0][:, c * P:(c + 1) * P].T for c in range(4)], axis=1)
    router = np.concatenate([g["w_rg_2"][0], g["w_re_2"][0]], axis=1)
    router = router.reshape(KT, P, 20).transpose(1, 0, 2).reshape(P, KT * 20)
    par = {
        "ln_attn_pre": cols(g["ln_attn_pre"]), "mu": mu[:, [12, 13, 4, 5, 6, 7, 0, 1, 2, 3, 8, 9, 10, 11]],
        "w_decay0": cols(g["w_decay0"]), "w_iclr0": cols(g["w_iclr0"]), "k_k": cols(g["k_k"]),
        "k_a": cols(g["k_a"]), "r_k": cols(g["r_k"]), "ln_x_w": cols(g["ln_x_w"]), "ln_x_b": cols(g["ln_x_b"]),
        "subln": cols(g["diff_subln"]), "ln_attn_post": cols(g["ln_attn_post"]),
        "ln_ffn_pre": cols(g["ln_ffn_pre"]), "conv": conv, "ln_ffn_post": cols(g["ln_ffn_post"]),
        "norm_mix": cols(g["norm_mix_g_2"]), "conv_a_w": ca, "conv_a_b": cols(g["conv_a_b_2"]),
        "ln_a_g": cols(g["ln_a_g_2"]), "ln_a_b": cols(g["ln_a_b_2"]), "pool_scale": cols(g["pool_scale_2"]),
        "conv_c": cc, "norm_x": cols(g["norm_x_g_2"]), "norm_mem": cols(g["norm_mem_g_2"]),
        "norm_ffn": cols(g["norm_ffn_g_2"]), "norm_f": cols(g["norm_f_g_2"]), "w_router": router,
        "b_router": np.concatenate([rows(g["b_rg_2"]), rows(g["b_re_2"])], axis=1),
        "lam": np.concatenate([rows(g[n]) for n in ("lambda_q1", "lambda_k1", "lambda_q2", "lambda_k2")], axis=1),
    }
    params = np.ascontiguousarray(np.concatenate([par[n] for n, _ in PCOLS], axis=1))
    lora = np.stack([np.concatenate([g["w_decay_up"][0], g["w_iclr_up"][0]], axis=0), g["w_gate_up"][0]], axis=1)
    xT = g["x"][0].T.reshape(KT, P, S).transpose(1, 0, 2)
    memT = g["mem_2"][0].T.reshape(KT, P, N_MEM).transpose(1, 0, 2)
    poolw = g["w_pool_grp_2"][0].transpose(1, 0, 2)
    return {k: np.ascontiguousarray(a) for k, a in
            dict(xT=xT, memT=memT, wstream=ws, params=params, consts=constants(), lora=lora, poolw=poolw).items()}


def constants():
    import numpy as np

    i, j = np.arange(P)[:, None], np.arange(P)[None, :]
    c = np.arange(S)[None, :] - (S - P)
    same = i // HD == j // HD
    lv = [((i >> l) % 2 == 1) & ((j >> l) % 2 == 0) & (i >> (l + 1) == j >> (l + 1)) for l in range(LEVELS)]
    cnt = [np.minimum(np.arange(POOL_PAD) + 1, 2 ** (g + 1)) for g in range(4)]
    eps = np.broadcast_to(np.array([[1e-6, 1e-5, 64e-5, 0.0]]), (P, 4))
    tab = {
        "ident": i == j, "ones": np.ones((P, P)), "blk": same, "alibi": np.where(c <= i, c - i, -1e30),
        "mask_nr": np.concatenate([same & (i < j), same & (i <= j)], axis=1),
        "mask_lv": np.concatenate(lv, axis=1), "reset": np.broadcast_to(np.arange(S)[None] % HD != 0, (P, S)),
        "id64": i % HD == np.arange(HD)[None], "invcnt": np.broadcast_to(1.0 / np.concatenate(cnt)[None], (P, 64)),
        "rank": np.broadcast_to(np.array([[4, 3, 2, 1]]), (P, 4)), "eps": eps,
        "upto": i <= j, "count": np.broadcast_to(np.arange(P)[None] + 1, (P, P)),
    }
    return np.concatenate([tab[n].astype(np.float32) for n, _ in CCOLS], axis=1)


def kernel(**inputs):
    import numpy as np
    import concourse.bacc as bacc
    from concourse.bass_utils import run_bass_kernel_spmd

    arrays = pack(inputs)
    nc = bacc.Bacc("TRN2", target_bir_lowering=False, num_devices=1)
    aps = {n: nc.dram_tensor(n, a.shape, F32, kind="ExternalInput").ap() for n, a in arrays.items()}
    out = nc.dram_tensor("out", (P, KT, S), F32, kind="ExternalOutput").ap()
    build(nc, out=out, **aps)
    r = run_bass_kernel_spmd(nc, [arrays], core_ids=[0])
    got = r.results[0]["out"]
    return np.ascontiguousarray(got.transpose(2, 1, 0)).reshape(1, S, D)
```

```python
import math
from contextlib import ExitStack

import concourse.bass as bass
from concourse import mybir

F32 = mybir.dt.float32
F32R = mybir.dt.float32r
ALU = mybir.AluOpType
ACT = mybir.ActivationFunctionType
AX = mybir.AxisListType

P = 128
D = 1024
S = 512
KT = D // P
TT = S // P
HD = 64
NCH = S // HD
LEVELS = 6
D_FF = 2816
N_MEM = 256
DECAY_SCALE = math.exp(-0.5)
LAM_INIT = 0.8 - 0.6 * math.exp(-0.3 * 0)
CONV_A = 31
TAPS = 14
POOL_PAD = 16
RING = 4
K_DVE = 3
BLK = KT * 2 * P

STAGES = [("in", 13, 26, 14), ("out", 4, 8, 0), ("ffn", 34, 68, 68), ("mix", 12, 24, 24), ("gate", 16, 40, 40),
          ("o", 4, 8, 8), ("kv", 8, 16, 0), ("q", 4, 8, 0), ("xo", 4, 8, 8), ("moe", 48, 96, 96)]
B0, T0, E0, TILES_TO = {}, {}, {}, []
_b = _t = _e = 0
for _name, _nb, _nt, _ne in STAGES:
    B0[_name], T0[_name], E0[_name] = _b, _t, _e
    for _i in range(_nb):
        _per = (2 if _i % 2 == 0 else 3) if _name == "gate" else 2
        _t += _per
        TILES_TO.append(_t)
    _b, _e = _b + _nb, _e + _ne
    assert _t == T0[_name] + _nt
NBLK, NTILE = _b, _t

OPERANDS = {0: 0, 2: 8, 4: 16, 6: 24, 7: 32}
SUMMED = (2, 4)
OTHERS = {r: sum(x not in SUMMED for x in range(r + 1)) for r in range(9)}

PCOLS = [("ln_attn_pre", 8), ("mu", 14), ("w_decay0", 4), ("w_iclr0", 4), ("k_k", 4), ("k_a", 4), ("r_k", 4),
         ("ln_x_w", 4), ("ln_x_b", 4), ("subln", 1), ("ln_attn_post", 8), ("ln_ffn_pre", 8), ("conv", 8 * 24),
         ("ln_ffn_post", 8), ("norm_mix", 8), ("conv_a_w", 4 * CONV_A), ("conv_a_b", 4), ("ln_a_g", 4),
         ("ln_a_b", 4), ("pool_scale", 8), ("conv_c", 12), ("norm_x", 8), ("norm_mem", 8), ("norm_ffn", 8),
         ("norm_f", 8), ("w_router", KT * 20), ("b_router", 20), ("lam", 4 * HD)]
CCOLS = [("ident", P), ("ones", P), ("blk", P), ("eps", 8), ("alibi", S), ("mask_nr", 2 * P), ("mask_lv", LEVELS * P),
         ("reset", S), ("id64", HD), ("invcnt", 4 * POOL_PAD), ("rank", 4),
         ("upto", P), ("count", P)]


BEATS = ["tok", "nr", "ak", "l0", "l1", "l2", "l3", "l4", "l5", "wu", "gh", "s2", "s3", "s4", "s5", "s6", "s7",
         "y", "mu", "var"]
SIDE = {"tok": ["scores0", "max0"], "nr": ["exp0", "weights0"], "ak": ["turn0", "turned0", "scores1"],
        "l0": ["max1"], "l1": ["exp1", "weights1"], "l2": ["turn1", "turned1", "scores2"], "l3": ["max2"],
        "l4": ["exp2", "weights2"], "l5": ["turn2", "turned2", "scores3"], "wu": ["max3", "exp3"],
        "gh": ["weights3"], "s2": ["up", "turn3"], "s3": ["decay", "up_gate", "turned3"],
        "s4": ["out", "square", "sums", "exps", "keys", "scaled"], "s5": ["root", "key_norm", "roots", "hat_r"],
        "s6": ["spread", "norm", "key_spread"], "s7": ["hats", "hat", "ends"]}


def offsets(cols):
    at, out = 0, {}
    for name, w in cols:
        out[name] = (at, w)
        at += w
    return out, at


PO, NPAR = offsets(PCOLS)
CO, NCST = offsets(CCOLS)


def build(nc, xT, memT, wstream, params, consts, lora, poolw, out):
    with ExitStack() as ctx:
        def sem(name):
            return ctx.enter_context(nc.semaphore(name))

        top = [nc.sbuf_base + (-nc.sbuf_base) % 64]
        KB = 1024

        def at(name, shape, offset, dt=F32):
            assert offset + 4 * math.prod(shape) <= nc.sbuf_usable_end, name
            return nc.alloc_sbuf_tensor_at(name, [P, *shape], dt, offset=offset)

        top_of = {}

        def sb(name, shape, dt=F32):
            top_of[name] = top[0]
            t = at(name, shape, top[0], dt)
            top[0] += -(-4 * math.prod(shape) // 64) * 64
            return t

        raw = sb("raw", [RING, BLK])
        wh = sb("wh", [RING, KT, 2, P], F32R)
        wl = at("wl", [RING, KT, 2, P], top_of["raw"], F32R)
        cst = sb("cst", [NCST])
        par = sb("par", [NPAR])
        pw = sb("pw", [4, 2 * P])
        ev = sb("ev", [4, S + 2])
        tmp = sb("tmp", [2, S])
        sq = sb("sq", [2, S])
        sqa = sb("sqa", [S])
        sml = sb("sml", [64])
        rs, sd = sml[:, 0:4], sml[:, 4:8]
        lam_d, lam_e, lam_n, g08 = sml[:, 8:10], sml[:, 10:12], sml[:, 12:13], sml[:, 13:14]
        kn = sml[:, 32:40].rearrange("p (t h) -> p t h", h=2)
        vn = sml[:, 40:48].rearrange("p (t h) -> p t h", h=2)
        hn = sml[:, 48:52]
        mx = sml[:, 16:20]
        nmx = sml[:, 20:24]
        den = sml[:, 24:28]
        rden = sml[:, 28:32]
        xt_off = top[0]
        XT = sb("XT", [KT, S])
        x_off = top[0]
        XH = sb("XH", [KT, S], F32R)
        XL = sb("XL", [KT, S], F32R)
        ar = top[0]

        R = at("R", [4, S], ar)
        K = at("K", [4, S], ar + 8 * KB)
        V = at("V", [4, S], ar + 16 * KB)
        LO = at("LO", [S], ar + 24 * KB)
        GLO = at("GLO", [S], ar + 26 * KB)
        OO = at("OO", [4, S], ar + 28 * KB)
        lor = at("lor", [2, S], ar + 36 * KB)
        QT = at("QT", [4, S], ar + 40 * KB)
        KD = at("KD", [4, S], xt_off)
        DV = at("DV", [TT, S], xt_off + 8 * KB)
        SC = at("SC", [2, 2, S], ar + 48 * KB)
        SQO = sq
        ring = top_of["raw"] + 16 * KB
        AT = at("AT", [TT, S], ring + 40 * KB)
        Wt = [at("Wr", [8, S], top_of["raw"]), at("Wx", [8, S], x_off)]
        AR = at("AR", [TT, 2, P], x_off + 16 * KB)
        BT = at("BT", [S], x_off + 20 * KB)
        KH = at("KH", [S], x_off + 22 * KB)
        BON = at("BON", [S], x_off + 24 * KB)
        AXb = at("AXb", [TT, 2, 2, HD], x_off + 28 * KB)
        Btok = at("Btok", [TT, P], ring)
        Ktok = at("Ktok", [TT, P], ring + 2 * KB)
        Vtok = at("Vtok", [TT, P], ring + 4 * KB)
        Z = at("Z", [TT, P], ring + 6 * KB)
        NR = at("NR", [2, TT, 2, P], ring + 8 * KB)
        AKRK = at("AKRK", [2, TT, 2, P], ring + 16 * KB)
        Qm = at("Qm", [2, TT, P], ring + 24 * KB)
        Tm = at("Tm", [2, TT, P], ring + 28 * KB)
        TTm = at("TTm", [2, TT, P], ring + 32 * KB)
        WU = at("WU", [2, TT, P], ring + 36 * KB)
        wo = [top_of["raw"], x_off]
        GTt = [at(f"GT{i}", [NCH, HD], wo[i] + 10 * KB) for i in range(2)]
        STt = [at(f"ST{i}", [NCH, HD], wo[i] + 8 * KB) for i in range(2)]
        HSt = [at(f"HS{i}", [NCH, HD], wo[i] + 14 * KB) for i in range(2)]
        Fo = at("Fo", [KT, S], ar + 32 * KB)
        HH = at("HH", [KT, S], ar, F32R)
        HL = at("HL", [KT, S], ar + 16 * KB, F32R)
        gl = at("gl", [2, S], ar + 48 * KB)
        yv = at("yv", [2, S], ar + 52 * KB)
        cpar = at("cpar", [64], ar + 56 * KB)
        gateg = at("gateg", [4, TT, 4], ar + 56 * KB + 256)
        gcur = at("gcur", [TT, 4], ar + 56 * KB + 512)
        rt = at("rt", [24, 16], ar + 32 * KB)
        rt3 = at("rt3", [TT, 4, 4], ar + 34 * KB)
        lg = at("lg", [TT, 20], ar + 36 * KB)
        wrh = at("wrh", [KT, 20], ar + 37 * KB, F32R)
        wrl = at("wrl", [KT, 20], ar + 38 * KB, F32R)
        TXH = at("TXH", [TT, D], ar, F32R)
        TXL = at("TXL", [TT, D], ar + 16 * KB, F32R)
        GHH = at("GHH", [KT, P], ar + 32 * KB, F32R)
        GHL = at("GHL", [KT, P], ar + 36 * KB, F32R)
        YH = at("YH", [2, 4, 2 * P], ar + 40 * KB, F32R)
        YL = at("YL", [2, 4, 2 * P], ar + 48 * KB, F32R)
        G1 = at("G1", [TT, 4, P], top_of["cst"] + 4 * CO["alibi"][0], F32R)
        G2 = at("G2", [4, S], top_of["ev"], F32R)
        chosen = at("chosen", [4, TT, 4], ar + 56 * KB + 768, F32R)
        posn = at("posn", [4, TT, 4], ar + 57 * KB)
        pcur = at("pcur", [TT, 4], ar + 57 * KB + 256)
        gslot = at("gslot", [4], ar + 57 * KB + 320)
        most = at("most", [2], ar + 57 * KB + 384)
        flag = at("flag", [1], ar + 57 * KB + 448, mybir.dt.int32)
        uptor = at("uptor", [P], ar + 34 * KB + 512, F32R)
        onesr = at("onesr", [P], ar + 35 * KB, F32R)
        identr = at("identr", [P], ar + 57 * KB + 512, F32R)
        gparts = at("gparts", [4, TT, 4, 2], ar + 58 * KB, F32R)
        gtwo = at("gtwo", [TT, 4, 2], ar + 58 * KB + 512, F32R)
        APAD = at("APAD", [4, S + CONV_A - 1], ar)
        AH = at("AH", [4, S], ar, F32R)
        AL = at("AL", [4, S], ar + 8 * KB, F32R)
        CH = at("CH", [4, S], ar + 16 * KB, F32R)
        CL = at("CL", [4, S], ar + 24 * KB, F32R)
        CA = at("CA", [4, S], ar + 32 * KB)
        cpad = at("cpad", [S + 2], ar + 40 * KB)
        upad = at("upad", [2, S + POOL_PAD], ar + 42 * KB + 256)
        MG = at("MG", [KT, S], ar + 32 * KB)
        PL = at("PL", [4, S], ar + 48 * KB)
        MH = at("MH", [KT, N_MEM], ar, F32R)
        ML = at("ML", [KT, N_MEM], ar + 8 * KB, F32R)
        KX = at("KX", [KT, N_MEM], ar + 16 * KB)
        VX = at("VX", [2, D], ar + 24 * KB)
        QX = at("QX", [KT, S], ar + 32 * KB)
        MT = at("MT", [KT, N_MEM], ar + 48 * KB)
        EXx = at("EXx", [2, N_MEM], ar + 48 * KB)
        PX = at("PX", [2, N_MEM], ar + 50 * KB)
        PTx = at("PTx", [2, S], ar + 52 * KB)

        acc = ctx.enter_context(nc.psum_tensor("acc", [P, 4, S], F32))
        mb = ctx.enter_context(nc.psum_tensor("mb", [P, 4, S], F32))

        def cs(name, a=0, b=None):
            o, w = CO[name]
            return cst[:, o + a:o + (w if b is None else b)]

        def pr(name, a, b=None):
            o, _ = PO[name]
            return par[:, o + a:o + (a + 1 if b is None else b)]

        ident, ones, blk = cs("ident"), cs("ones"), cs("blk")

        loaded = [sem(f"loaded{i}") for i in range(RING)]
        in_x, in_xb, in_x2, in_mem = sem("in_x"), sem("in_xb"), sem("in_x2"), sem("in_mem")
        in_par, in_rest = sem("in_par"), sem("in_rest")
        hi_done, split_done = sem("hi_done"), sem("split_done")
        acc_ready, evac, ev_used = sem("acc_ready"), sem("evac"), sem("ev_used")
        sq_ready, sq_used = sem("sq_ready"), sem("sq_used")
        st_sum, sd_ready, rs_ready, rb_ready = sem("st_sum"), sem("sd_ready"), sem("rs_ready"), sem("rb_ready")
        xn_ready, x_ready = sem("xn_ready"), sem("x_ready")
        dchain = sem("dchain")
        names = []
        names += ("lam_dot lam_exp lora_act at_sc at_mx at_e at_p at_t at_te at_o at_sq at_ss at_sd at_done rk_up "
                  "rk_upg rk_sig rk_g rk_kk rk_cum rk_ksq rk_kss rk_kmx rk_ksd rk_exp rk_hat rk_bsum rk_bonus rk_tok "
                  "rk_toke rk_nr rk_nrm rk_ak rk_akm rk_q rk_qm rk_t rk_tm rk_tt rk_tte rk_x rk_xe rk_wu rk_wue rk_z "
                  "rk_zs rk_gh rk_gs rk_hs rk_s rk_st rk_y rk_ys rk_mu rk_d rk_dsq rk_var rk_sd rk_vr rk_vs rk_kr rk_ks "
                  "at_rr at_sp rk_done mixed").split()
        names += ("op_n op_hi la_rr la_sp gelu_done hid_ready acc_added la_in la_mu la_d la_sq la_sum la_var la_sd la_y "
                  "la_act ac_ready p_mm mg_ready").split()
        names += ("mem_ready xs_sc xs_mx xs_e xs_p xs_t xs_te xs_o xs_hi xs_done").split()
        names += ("wr_ready rt_lg rt_sub rt_exp gate_ready gb_ready final_ready stored low_dve fchain f_tok f_toke "
                  "f_mask f_count f_flag f_g f_turn f_turned f_gate f_gath f_xh f_xl f_silu f_hid f_ht f_hh f_hl f_y "
                  "f_yh f_yl f_out f_add f_gslot").split()
        s = {n: sem(n) for n in names}

        def in_beats(main, side, pairs=4):
            for ct in range(pairs):
                for beat in BEATS:
                    if beat in main:
                        main[beat](ct)
                    for name in SIDE.get(beat, ()):
                        if name in side:
                            side[name](ct + 1)
                        elif name[:-1] in side and name[-1].isdigit():
                            side[name[:-1]](TT * ct + int(name[-1]))
                        elif "head_" + name in side:
                            side["head_" + name](ct)

        def g_bank(k, banks):
            return 2 + k % 2 if banks == 2 else k % 4

        def x_bank(u):
            return (mb[:, 0, 0:N_MEM], mb[:, 1, 0:N_MEM], acc[:, 2, 0:N_MEM])[u % 3]

        def bank(hh, x):
            return (mb if hh else acc)[:, x if hh else 2 + x, :]

        block = ctx.enter_context(nc.Block())
        @block.sync
        def _(sp):
            first = CO["alibi"][0]
            sp.dma_start(XT[:, 0:4, :], xT[:, 0:4, :]).then_inc(in_x, 16)
            sp.dma_start(XT[:, 4:8, :], xT[:, 4:8, :]).then_inc(in_xb, 16)
            sp.dma_start(cst[:, 0:first], consts[:, 0:first]).then_inc(in_par, 16)
            sp.dma_start(par[:, :], params).then_inc(in_par, 16)
            for n in range(RING):
                sp.dma_start(raw[:, n, :], wstream[n]).then_inc(loaded[n], 16)
            sp.dma_start(cst[:, first:], consts[:, first:]).then_inc(in_rest, 16)
            sp.dma_start(lor[:, :, :], lora).then_inc(in_rest, 16)
            sp.dma_start(pw[:, :, :], poolw).then_inc(in_rest, 16)

            def load(n, slot, used=None):
                sp.wait_ge(acc_ready, TILES_TO[n - RING] if used is None else used)
                src = wstream[n] if isinstance(n, int) else wstream[bass.ds(n, 1)].rearrange("a p n -> p (a n)")
                sp.dma_start(raw[:, slot, :], src).then_inc(loaded[slot], 16)

            def load_range(a, b):
                assert (b - a) % RING == 0
                tiles = TILES_TO[a] - TILES_TO[a - RING]
                assert all(TILES_TO[n] - TILES_TO[n - RING] == tiles for n in range(a, b - RING))
                with sp.Fori(0, (b - a) // RING) as i:
                    for j in range(RING):
                        load(i * RING + (a + j), (a + j) % RING, i * tiles + TILES_TO[a + j - RING])

            load_range(RING, 12)
            load(12, 0)
            sp.wait_ge(s["rk_done"], 3)
            load(13, 1)
            sp.wait_ge(s["rk_y"], 4)
            load(14, 2)
            load(15, 3)
            sp.wait_ge(s["rk_done"], 4)
            sp.dma_start(XT[:, :, :], xT).then_inc(in_x2, 16)
            load_range(16, 68)
            load(68, 0)
            load(69, 1)
            load_range(70, 82)
            sp.wait_ge(s["p_mm"], KT)
            sp.dma_start(MT[:, :, :], memT).then_inc(in_mem, 16)
            load_range(82, 86)
            load_range(86, 146)
            load(146, 2)
            for m in range(KT):
                sp.wait_ge(s["final_ready"], m + 1)
                sp.dma_start(out[:, m, :], XT[:, m, :]).then_inc(s["stored"], 16)
            sp.wait_ge(s["stored"], 16 * KT)

        @block.gpsimd
        def _(pool):
            def lower(n, slot, kt=KT):
                pool.wait_ge(hi_done, n + 1)
                nc.gpsimd.tensor_tensor(wl[:, slot, 0:kt].rearrange("p a b c -> p (a b c)"),
                                        raw[:, slot, 0:kt * 2 * P],
                                        wh[:, slot, 0:kt].rearrange("p a b c -> p (a b c)").bitcast(F32),
                                        ALU.subtract).then_inc(split_done, 1)

            end = NBLK
            def lower_range(a, b, kt=KT):
                assert a % RING == 0
                with pool.Fori(0, (b - a) // RING) as i:
                    for j in range(RING):
                        lower(i * RING + (a + j), j, kt)
                for n in range(b - (b - a) % RING, b):
                    lower(n, n % RING, kt)

            lower_range(0, min(end, B0["moe"]))
            lower(B0["moe"], B0["moe"] % RING, KT - K_DVE)
            lower_range(B0["moe"] + 1, NBLK, KT - K_DVE)

        @block.tensor
        def _(pe):
            mm = nc.tensor.matmul

            def mm3(out_, a, b, start, stop):
                mm(out_, a[0], b[0], start=start, stop=False)
                mm(out_, a[0], b[1], start=False, stop=False)
                return mm(out_, a[1], b[0], start=False, stop=stop)

            def begin_block(n, t, tiles=2, moe=False):
                pe.wait_ge(split_done, n + 1)
                if moe:
                    pe.wait_ge(s["low_dve"], n + (1 - B0["moe"]))
                for j in range(tiles):
                    if not isinstance(t, int) or t + j >= 4:
                        pe.wait_ge(evac, t + (j - 3))

            def block_tiles(n, t, slot, bank, xs=(XH, XL), kt=KT, ns=S, need=None, moe=False):
                begin_block(n, t, moe=moe)
                for k in range(kt):
                    if need is not None:
                        pe.wait_ge(need[0], need[1] + k)
                    for j in range(2):
                        last = mm3(acc[:, (bank + j) % 4, 0:ns], (wh[:, slot, k, j, :], wl[:, slot, k, j, :]),
                                   (xs[0][:, k, 0:ns], xs[1][:, k, 0:ns]), k == 0, k == kt - 1)
                        if k == kt - 1:
                            last.then_inc(acc_ready, 1)

            def stage_blocks(name, count, need, xs=(XH, XL), ns=S, start=0):
                for b in range(start, start + count):
                    n, t = B0[name] + b, T0[name] + 2 * b
                    block_tiles(n, t, n % RING, t % 4, xs, ns=ns, need=need if b == start else None)

            def token_tiles(n, t, xs, lots):
                begin_block(n, t)
                for j, toks in enumerate(lots):
                    for c, tok in enumerate(toks):
                        for k in range(KT):
                            last = mm3(acc[:, (t + j) % 4, c * 256:(c + 1) * 256],
                                       (xs[0][:, k, tok * P:(tok + 1) * P], xs[1][:, k, tok * P:(tok + 1) * P]),
                                       (wh[:, n % RING, k].rearrange("p a b -> p (a b)"),
                                        wl[:, n % RING, k].rearrange("p a b -> p (a b)")), k == 0, k == KT - 1)
                    last.then_inc(acc_ready, 1)

            def norm_sums(r, nt=TT):
                pe.wait_ge(sq_used, KT * (r + 1))
                for t in range(nt):
                    last = mm(mb[:, 0, t:t + 1], sqa[:, t * P:(t + 1) * P], ones[:, 0:1], start=True, stop=True)
                last.then_inc(st_sum, 1)

            def norm_spread(r, nt=TT):
                pe.wait_ge(rs_ready, r + 1)
                for t in range(nt):
                    last = mm(mb[:, 1, t * P:(t + 1) * P], rs[:, t:t + 1].to_broadcast([P, P]), ident,
                              start=True, stop=True)
                last.then_inc(rb_ready, 1)

            def norm(r):
                if r in SUMMED:
                    pe.wait_ge(evac, {2: T0["ffn"], 4: T0["mix"]}[r])
                    for m in range(KT):
                        pe.wait_ge(sq_ready, KT * r + m + 1)
                        for t in range(TT):
                            last = mm(acc[:, t, 0:1], sq[:, m % 2, t * P:(t + 1) * P], ones[:, 0:1],
                                      start=(m == 0), stop=(m == KT - 1))
                        last.then_inc(sq_used, 1)
                else:
                    norm_sums(r)
                norm_spread(r)

            pe.wait_ge(in_par, 32)
            norm(0)
            stage_blocks("in", 11, (xn_ready, 1))
            for b in (11, 12):
                token_tiles(B0["in"] + b, T0["in"] + 2 * b, (XH, XL), ((0, 1), (2, 3)))

            def scores(u):
                h, i = divmod(u, TT)
                if u == 0:
                    pe.wait_ge(evac, 26)
                else:
                    pe.wait_ge(s["at_te"], u)
                    if i == 0:
                        pe.wait_ge(s["at_done"], h)
                w = (i + 1) * P
                for c in range(2):
                    last = mm(mb[:, 2 + c, 0:w], QT[64 * c:64 * c + 64, h, i * P:(i + 1) * P],
                              KD[64 * c:64 * c + 64, h, 0:w], start=True, stop=True)
                last.then_inc(s["at_sc"], 1)

            def turn(u):
                pe.wait_ge(s["at_p"], u + 1)
                for j in range(u % TT + 1):
                    last = nc.tensor.transpose(mb[:, 2, j * P:(j + 1) * P], SC[:, u % 2, 0, j * P:(j + 1) * P], ident)
                last.then_inc(s["at_t"], 1)

            def head_out(h):
                pe.wait_ge(s["at_te"], TT * (h + 1))
                for j in range(TT):
                    last = mm(mb[:, 3, j * P:S], DV[:, j, h * P:(h + 1) * P], AT[:, j, j * P:S],
                              start=(j == 0), stop=(j == TT - 1))
                last.then_inc(s["at_o"], 1)

            def head_sums(h):
                pe.wait_ge(s["at_sq"], h + 1)
                for t in range(TT):
                    last = mm(mb[:, 2, t:t + 1], SQO[:, 0, t * P:(t + 1) * P], ones[:, 0:1], start=True, stop=True)
                last.then_inc(s["at_ss"], 1)

            def head_spread(h):
                pe.wait_ge(s["at_rr"], h + 1)
                for t in range(TT):
                    last = mm(mb[:, 2, t * P:(t + 1) * P], hn[:, t:t + 1].to_broadcast([P, P]), ident,
                              start=True, stop=True)
                last.then_inc(s["at_sp"], 1)

            def pair_sums(dst, src):
                for t in range(TT):
                    last = mm(dst[:, 2 * t:2 * t + 2], src[:, t * P:(t + 1) * P],
                              blk.rearrange("p (h c) -> p h c", h=2)[:, :, 0], start=True, stop=True)
                return last

            def pair_spread(dst, src):
                for t in range(TT):
                    for hh in range(2):
                        last = mm(dst[HD * hh:HD * hh + HD, t * P:(t + 1) * P],
                                  src[:, t, hh:hh + 1].to_broadcast([P, HD]), ident, start=True, stop=True)
                return last

            def up(ct):
                if ct == 0:
                    pe.wait_ge(evac, 26)
                    pe.wait_ge(in_rest, 48)
                    pe.wait_ge(s["lora_act"], 1)
                elif ct == 4:
                    return
                else:
                    pe.wait_ge(s["rk_zs"], 2 * ct)
                c = slice(ct * P, (ct + 1) * P)
                mm(bank(0, 1), lor[0:64, 0, c], LO[0:64, :], start=True, stop=True)
                mm(bank(1, 1), lor[64:128, 0, c], LO[64:128, :], start=True, stop=True).then_inc(s["rk_up"], 1)

            def up_gate(ct):
                if ct < 4:
                    pe.wait_ge(s["rk_sig"], ct + 1)
                    mm(bank(0, 1), lor[:, 1, ct * P:(ct + 1) * P], GLO[:, :], start=True,
                       stop=True).then_inc(s["rk_upg"], 1)

            def keys(ct):
                if ct < 4:
                    pe.wait_ge(s["rk_ksq"], ct + 1)
                    pair_sums(bank(1, 1), Wt[ct % 2][:, 5, :]).then_inc(s["rk_kss"], 1)

            def key_spread(ct):
                if ct < 4:
                    pe.wait_ge(s["rk_kr"], ct + 1)
                    pair_spread(bank(1, 1), kn).then_inc(s["rk_ks"], 1)

            def var_spread(ct):
                pe.wait_ge(s["rk_vr"], ct + 1)
                pair_spread(mb[:, 1, :], vn).then_inc(s["rk_vs"], 1)

            def tok(ct):
                pe.wait_ge(s["rk_hat"], ct + 1)
                pe.wait_ge(s["rk_g"], ct + 1)
                if ct:
                    pe.wait_ge(s["rk_sd"], ct)
                W = Wt[ct % 2]
                mm(acc[:, 0, :], blk, W[:, 3, :], start=True, stop=True).then_inc(s["rk_bsum"], 1)
                for t in range(TT):
                    o = slice(t * P, (t + 1) * P)
                    nc.tensor.transpose(acc[:, 1, o], AR[:, t, 0, :], ident)
                    nc.tensor.transpose(acc[:, 2, o], W[:, 0, o], ident)
                    nc.tensor.transpose(acc[:, 3, o], W[:, 2, o], ident)
                    last = nc.tensor.transpose(mb[:, 0, o], V[:, ct, o], ident)
                last.then_inc(s["rk_tok"], 1)
                if ct:
                    var_spread(ct - 1)

            def products(ct, left, done, ready, value):
                for hh in range(2):
                    pe.wait_ge(ready, value + hh)
                    ps = slice(HD * hh, HD * hh + HD)
                    for t in range(TT):
                        last = mm(bank(hh, t // 2)[:, 256 * (t % 2):256 * (t % 2) + 256], left[ps, t * P:(t + 1) * P],
                                  AR[ps, t].rearrange("p a b -> p (a b)"), start=True, stop=True)
                    last.then_inc(done, 1)

            def nr(ct):
                pe.wait_ge(s["rk_toke"], ct + 1)
                if ct:
                    pe.wait_ge(s["rk_done"], ct)
                products(ct, BT, s["rk_nr"], s["rk_toke"], ct)

            def ak(ct):
                products(ct, KH, s["rk_ak"], s["rk_nrm"], 2 * ct + 1)

            def l0(ct):
                for hh in range(2):
                    pe.wait_ge(s["rk_akm"], 2 * ct + hh + 1)
                    for t in range(TT):
                        last = nc.tensor.transpose(bank(hh, 0)[:, t * P:(t + 1) * P], NR[:, hh, t, 0, :], ident)
                    last.then_inc(s["rk_q"], 1)
                    for t in range(TT):
                        last = mm(bank(hh, 1)[:, t * HD:(t + 1) * HD], AKRK[:, hh, t, 0, :],
                                  Vtok[:, t, HD * hh:HD * hh + HD], start=True, stop=True)
                    last.then_inc(s["rk_x"], 1)

            def turn_t(u, hh, level):
                for t in range(TT):
                    last = nc.tensor.transpose(bank(hh, 1)[:, t * P:(t + 1) * P], Tm[:, hh, t, :], ident)
                last.then_inc(s["rk_tt"], 1)

            def level(l):
                def run(ct):
                    for hh in range(2):
                        pe.wait_ge(s["rk_tm"], 6 * ct * 2 + 2 * (l - 1) + hh + 1)
                        if l == 1:
                            pe.wait_ge(s["rk_xe"], 2 * ct + hh + 1)
                        for t in range(TT):
                            last = mm(bank(hh, 0)[:, t * P:(t + 1) * P], NR[:, hh, t, 0, :], Tm[:, hh, t, :],
                                      start=True, stop=True)
                        last.then_inc(s["rk_q"], 1)
                        turn_t(ct, hh, l)
                    for hh in range(2):
                        pe.wait_ge(s["rk_qm"], 10 * ct + 2 * (l - 1) + hh + 1)
                        pe.wait_ge(s["rk_tte"], 12 * ct + 2 * (l - 1) + hh + 1)
                        for t in range(TT):
                            last = mm(bank(hh, 1)[:, t * P:(t + 1) * P], TTm[:, hh, t, :], Qm[:, hh, t, :],
                                      start=True, stop=True)
                        last.then_inc(s["rk_t"], 1)
                return run

            def wu(ct):
                for hh in range(2):
                    pe.wait_ge(s["rk_tm"], 12 * ct + 10 + hh + 1)
                    turn_t(ct, hh, 6)
                for hh in range(2):
                    pe.wait_ge(s["rk_tte"], 12 * ct + 10 + hh + 1)
                    for t in range(TT):
                        last = mm(bank(hh, 0)[:, t * P:(t + 1) * P], TTm[:, hh, t, :],
                                  AXb[:, t, hh].rearrange("p a b -> p (a b)"), start=True, stop=True)
                    last.then_inc(s["rk_wu"], 1)

            def gh(ct):
                pe.wait_ge(s["rk_bonus"], ct + 1)
                for hh in range(2):
                    ps = slice(HD * hh, HD * hh + HD)
                    pe.wait_ge(s["rk_wue"], 2 * ct + hh + 1)
                    for t in range(TT):
                        last = mm(bank(hh, 1)[ps, t * P:(t + 1) * P], WU[:, hh, t, 0:HD], NR[:, hh, t, 1, :],
                                  start=True, stop=True)
                    last.then_inc(s["rk_z"], 1)
                    for c in range(NCH):
                        t, cp = c // 2, slice(HD * (c % 2), HD * (c % 2) + HD)
                        g, h = slice(t * HD, (t + 1) * HD), slice(256 + t * HD, 256 + (t + 1) * HD)
                        mm(acc[ps, c % 2, g], WU[cp, hh, t, 0:HD], Btok[cp, t, ps], start=True, stop=True)
                        mm(acc[ps, c % 2, h], Btok[cp, t, ps], WU[cp, hh, t, HD:P], start=True, stop=False)
                        last = mm(acc[ps, c % 2, h], Ktok[cp, t, ps], Vtok[cp, t, ps], start=False, stop=True)
                    last.then_inc(s["rk_gh"], 1)

            def enter(c):
                def run(ct):
                    pe.wait_ge(s["rk_st"], 7 * ct + c - 1)
                    if c == 2:
                        pe.wait_ge(s["rk_gs"], ct + 1)
                    for hh in range(2):
                        ps = slice(HD * hh, HD * hh + HD)
                        last = mm(mb[ps, 0, 0:HD], GTt[ct % 2][ps, c - 1, :], STt[ct % 2][ps, c - 1, :],
                                  start=True, stop=True)
                    last.then_inc(s["rk_s"], 1)
                return run

            def y(ct):
                pe.wait_ge(s["rk_st"], 7 * ct + 7)
                pe.wait_ge(s["rk_zs"], 2 * ct + 2)
                for hh in range(2):
                    ps = slice(HD * hh, HD * hh + HD)
                    for t in range(TT):
                        o = slice(t * P, (t + 1) * P)
                        mm(acc[ps, 2, o], WU[:, hh, t, HD:P], NR[:, hh, t, 1, :], start=True, stop=False)
                        mm(acc[ps, 2, o], Vtok[:, t, ps], AKRK[:, hh, t, 1, :], start=False, stop=False)
                        for c in (2 * t, 2 * t + 1):
                            if c:
                                last = mm(acc[ps, 2, c * HD:(c + 1) * HD], STt[ct % 2][ps, c, :],
                                          Z[ps, t, (c % 2) * HD:(c % 2 + 1) * HD], start=False, stop=(c % 2 == 1))
                last.then_inc(s["rk_y"], 1)

            def mu(ct):
                pe.wait_ge(s["rk_ys"], ct + 1)
                mm(mb[:, 0, :], blk, Wt[ct % 2][:, 0, :], start=True, stop=True).then_inc(s["rk_mu"], 1)

            def var(ct):
                pe.wait_ge(s["rk_dsq"], ct + 1)
                pair_sums(acc[:, 2, :], Wt[ct % 2][:, 2, :]).then_inc(s["rk_var"], 1)

            up(0)
            up_gate(0)
            keys(0)
            key_spread(0)
            main = {"tok": tok, "nr": nr, "ak": ak, "l0": l0, "wu": wu, "gh": gh, "y": y, "mu": mu, "var": var}
            main |= {f"l{l}": level(l) for l in range(1, LEVELS)} | {f"s{c}": enter(c) for c in range(2, NCH)}
            in_beats(main, {"scores": scores, "turn": turn, "head_out": head_out, "head_sums": head_sums,
                            "head_spread": head_spread, "up": up, "up_gate": up_gate, "keys": keys,
                            "key_spread": key_spread})
            var_spread(3)

            stage_blocks("out", 4, (s["mixed"], 1))
            norm(1)

            def group(name, i, hidden, need=None, spread=None):
                n0, t0 = i * 12 + B0[name], i * 24 + T0[name]
                for b in range(hidden):
                    if spread is not None and b % 2 == 0:
                        spread(i, b // 2)
                    block_tiles(n0 + b, t0 + 2 * b, (B0[name] + b) % RING, (T0[name] + 2 * b) % 4,
                                need=need if b == 0 else None, moe=name == "moe")
                for b in range(4):
                    block_tiles(n0 + hidden + b, t0 + 2 * (hidden + b), (B0[name] + hidden + b) % RING,
                                (T0[name] + 2 * (hidden + b)) % 4, (HH, HL), kt=hidden,
                                need=(s["hid_ready"], i * 8 + (1 if name == "ffn" else 23)) if b == 0 else None,
                                moe=name == "moe")

            norm(2)
            with pe.Fori(0, 2) as i:
                group("ffn", i, 8, need=(xn_ready, 9))
            group("ffn", 2, 6)
            norm(3)

            norm(4)
            stage_blocks("mix", 12, (xn_ready, 17))

            def pooled(m):
                if m >= 2:
                    pe.wait_ge(s["mg_ready"], m - 1)
                mm(mb[:, 2 + m % 2, :], pw[:, m // 2, (m % 2) * P:(m % 2 + 1) * P], PL[:, m // 2, :],
                   start=True, stop=True).then_inc(s["p_mm"], 1)

            for m in range(KT):
                n, t = B0["gate"] + 2 * m, T0["gate"] + 5 * m
                block_tiles(n, t, n % RING, t % 4)
                if m == 0:
                    pe.wait_ge(s["la_in"], 1)
                    mm(mb[:, 0, :], ones, sqa[:, :], start=True, stop=True).then_inc(s["la_mu"], 1)
                pooled(m)
                begin_block(n + 1, t + 2, 3)
                slot = (n + 1) % RING
                for k in range(KT):
                    last = mm3(acc[:, (t + 2) % 4, :], (wh[:, slot, k, 0, :], wl[:, slot, k, 0, :]),
                               (XH[:, k, :], XL[:, k, :]), k == 0, k == KT - 1)
                last.then_inc(acc_ready, 1)
                if m == 0:
                    pe.wait_ge(s["la_sum"], 4)
                    for x in range(TT):
                        last = mm(mb[:, 1, x:x + 1], sqa[:, x * P:(x + 1) * P], ones[:, 0:1], start=True,
                                  stop=True)
                    last.then_inc(s["la_var"], 1)
                for x, (xh, xl) in enumerate(((CH, CL), (AH, AL))):
                    if m == 0 and x == 1:
                        pe.wait_ge(s["la_rr"], 1)
                        for y in range(TT):
                            last = mm(mb[:, 1, y * P:(y + 1) * P], hn[:, y:y + 1].to_broadcast([P, P]), ident,
                                      start=True, stop=True)
                        last.then_inc(s["la_sp"], 1)
                    for k in range(4):
                        if m == 0 and x == 1:
                            pe.wait_ge(s["ac_ready"], k + 1)
                        last = mm3(acc[:, (t + 3 + x) % 4, :],
                                   (wh[:, slot, 4 * (1 - x) + k, 1, :], wl[:, slot, 4 * (1 - x) + k, 1, :]),
                                   (xh[:, k, :], xl[:, k, :]), k == 0, k == 3)
                    last.then_inc(acc_ready, 1)

            stage_blocks("o", 1, (s["mg_ready"], KT + 1))
            norm_sums(5, 2)
            stage_blocks("o", 1, None, start=1)
            norm_spread(5, 2)
            stage_blocks("o", 2, None, start=2)
            stage_blocks("kv", 4, (s["mem_ready"], 1), (MH, ML), ns=N_MEM)
            for b in range(4, 8):
                token_tiles(B0["kv"] + b, T0["kv"] + 2 * b, (MH, ML), ((0,), (1,)))
            norm(6)
            stage_blocks("q", 4, (xn_ready, 25))

            def x_scores(u):
                h, i = divmod(u, TT)
                pe.wait_ge(evac, T0["q"] + 8)
                if u >= 3:
                    pe.wait_ge(s["xs_e"], u - 2)
                for k in range(2):
                    last = mm(x_bank(u), QX[:, 2 * h + k, i * P:(i + 1) * P], KX[:, 2 * h + k, :],
                              start=(k == 0), stop=(k == 1))
                last.then_inc(s["xs_sc"], 1)

            def x_turn(u):
                pe.wait_ge(s["xs_p"], u + 1)
                if u >= 2:
                    pe.wait_ge(s["xs_te"], u - 1)
                for j in range(2):
                    last = nc.tensor.transpose(mb[:, 2 + u % 2, j * P:(j + 1) * P], PX[:, u % 2, j * P:(j + 1) * P],
                                               ident)
                last.then_inc(s["xs_t"], 1)

            def x_out(h):
                pe.wait_ge(s["xs_te"], TT * (h + 1))
                if h:
                    pe.wait_ge(s["xs_done"], 2 * h)
                for v in range(2):
                    for j in range(2):
                        last = mm(acc[:, v, :], VX[:, j, h * 256 + v * P:h * 256 + (v + 1) * P], PTx[:, j, :],
                                  start=(j == 0), stop=(j == 1))
                    last.then_inc(s["xs_o"], 1)

            x_scores(0)
            x_scores(1)
            for u in range(4 * TT):
                if u + 2 < 4 * TT:
                    x_scores(u + 2)
                x_turn(u)
                if u % TT == TT - 1:
                    x_out(u // TT)
            stage_blocks("xo", 4, (s["xs_done"], 1))

            def spread_gate(i, e):
                pe.wait_ge(s["gate_ready"], i + 1)
                if not isinstance(i, int) or 4 * i + e >= 2:
                    if isinstance(i, int) or e >= 2:
                        pe.wait_ge(s["hid_ready"], i * 8 + (22 + 2 * (e - 1)))
                for t in range(TT):
                    last = mm(mb[:, 2 + e % 2, t * P:(t + 1) * P], gcur[:, t, e:e + 1].to_broadcast([P, P]), ident,
                              start=True, stop=True)
                last.then_inc(s["gb_ready"], 1)

            def turn_places(i):
                for e in range(4):
                    if e >= 2:
                        pe.wait_ge(s["f_turned"], i * 4 + (e - 1))
                    for t in range(TT):
                        last = mm(mb[:, 2 + e % 2, t * P:(t + 1) * P], G1[:, t, e, :], identr[:, :], start=True,
                                  stop=True)
                    last.then_inc(s["f_turn"], 1)

            def gather_gates(i):
                pe.wait_ge(s["f_g"], i + 1)
                for e in range(4):
                    for t in range(TT):
                        last = mm(mb[:, 0, 2 * e:2 * e + 2], G1[:, t, e, :], gtwo[:, t, e, :],
                                  start=(t == 0), stop=(t == TT - 1))
                last.then_inc(s["f_gate"], 1)

            def gather(i, h, k, banks=2):
                if 8 * h + k >= banks:
                    pe.wait_ge(s["f_xl"], i * 16 + (8 * h + k - banks + 1))
                for t in range(TT):
                    for part in (TXH, TXL):
                        last = mm(acc[:, g_bank(k, banks), 0:2 * P], part[:, t, k * P:(k + 1) * P],
                                  G1[:, t, 2 * h:2 * h + 2].rearrange("p a b -> p (a b)"),
                                  start=(t == 0 and part is TXH), stop=(t == TT - 1 and part is TXL))
                last.then_inc(s["f_gath"], 1)

            def gathered(i, last_group=False):
                n0, t0 = B0["moe"], T0["moe"]

                def turn_hidden(b):
                    pe.wait_ge(s["f_hid"], i * 8 + (b + 1))
                    if b >= 2:
                        pe.wait_ge(s["f_hl"], i * 8 + (b - 1))
                    else:
                        pe.wait_ge(s["f_turned"], i * 4 + (3 + b))
                    nc.tensor.transpose(mb[:, 2 + b % 2, 0:P], tmp[:, b % 2, P:2 * P], ident).then_inc(s["f_ht"], 1)

                for b in range(8):
                    pe.wait_ge(split_done, i * 12 + (n0 + b + 1))
                    pe.wait_ge(s["low_dve"], i * 12 + (b + 1))
                    if b >= 2:
                        pe.wait_ge(s["f_hid"], i * 8 + (b - 1))
                    e, slot = b // 2, (n0 + b) % RING
                    for k in range(KT):
                        if b % 4 == 0:
                            pe.wait_ge(s["f_xl"], i * 16 + (2 * b + k + 1))
                        last = mm3(acc[:, b % 2, 0:2 * P],
                                   (XH[:, k, e * P:(e + 1) * P], XL[:, k, e * P:(e + 1) * P]),
                                   (wh[:, slot, k].rearrange("p a b -> p (a b)"),
                                    wl[:, slot, k].rearrange("p a b -> p (a b)")), k == 0, k == KT - 1)
                    last.then_inc(acc_ready, 2)
                    if b:
                        turn_hidden(b - 1)
                    if b == 4 and not last_group:
                        pe.wait_ge(s["f_g"], i + 2)
                        pe.wait_ge(s["f_add"], i * 8)
                    if b >= 4 and not last_group:
                        gather(i + 1, 0, 2 * (b - 4))
                        gather(i + 1, 0, 2 * (b - 4) + 1)
                if last_group:
                    turn_hidden(7)
                else:
                    gather_gates(i + 1)
                    gather(i + 1, 1, 0)
                    turn_hidden(7)
                    for k in range(1, KT):
                        gather(i + 1, 1, k)
                    pe.wait_ge(s["f_gslot"], i + 2)

                def scatter(b):
                    pe.wait_ge(s["f_yl"], i * 8 + (2 * b + 2))
                    for j in range(2):
                        if b:
                            pe.wait_ge(s["f_add"], i * 8 + (2 * b + j - 1))
                        elif not last_group:
                            pe.wait_ge(s["f_xl"], i * 16 + (31 + j))
                        else:
                            pe.wait_ge(s["f_add"], i * 8)
                        if b == 0 and j == 0:
                            pe.wait_ge(s["f_turned"], i * 4 + 4)
                        for e in range(4):
                            for part in (YH, YL):
                                last = mm(acc[:, 2 + j, :], part[:, b % 2, e, j * P:(j + 1) * P], G2[:, e, :],
                                          start=(e == 0 and part is YH), stop=(e == 3 and part is YL))
                        last.then_inc(s["f_out"], 1)

                for b in range(4):
                    slot = (n0 + 8 + b) % RING
                    pe.wait_ge(split_done, i * 12 + (n0 + 8 + b + 1))
                    pe.wait_ge(s["low_dve"], i * 12 + (8 + b + 1))
                    for e in range(4):
                        if b and e % 2 == 0:
                            pe.wait_ge(s["f_yl"], i * 8 + (2 * b - 1 + e // 2))
                        for x in (2 * e, 2 * e + 1):
                            if b == 0:
                                pe.wait_ge(s["f_hl"], i * 8 + (x + 1))
                            last = mm3(mb[:, e // 2, (e % 2) * 2 * P:(e % 2 + 1) * 2 * P],
                                       (GHH[:, x, :], GHL[:, x, :]),
                                       (wh[:, slot, x].rearrange("p a b -> p (a b)"),
                                        wl[:, slot, x].rearrange("p a b -> p (a b)")), x % 2 == 0, x % 2 == 1)
                        if e == 1:
                            last.then_inc(s["f_y"], 1)
                    last.then_inc(acc_ready, 2)
                    if b:
                        scatter(b - 1)
                scatter(3)
                if not last_group:
                    turn_places(i + 1)

            norm(7)
            pe.wait_ge(s["wr_ready"], 1)
            for k in range(KT):
                pe.wait_ge(xn_ready, 32 + k + 1)
                for t in range(TT):
                    last = mm3(acc[:, t, 0:20], (XH[:, k, t * P:(t + 1) * P], XL[:, k, t * P:(t + 1) * P]),
                               (wrh[:, k, :], wrl[:, k, :]), k == 0, k == KT - 1)
            last.then_inc(s["rt_lg"], 1)
            for q in range(16):
                if q == 12:
                    pe.wait_ge(s["f_mask"], 1)
                    for t in range(TT + 1):
                        for j in range(min(t + 1, TT)):
                            last = mm(mb[:, 0, t * 16:(t + 1) * 16], (uptor if j == t else onesr)[:, :],
                                      chosen[:, :, j, :], start=(j == 0), stop=(j == min(t, TT - 1)))
                    last.then_inc(s["f_count"], 1)
                t, half, part = q // 4, q // 2 % 2, (XH, XL)[q % 2]
                if q >= 4:
                    pe.wait_ge(s["f_toke"], q - 3)
                elif q == 0:
                    pe.wait_ge(s["rt_sub"], 1)
                for k in range(4):
                    last = mm(acc[:, q % 4, k * P:(k + 1) * P], part[:, 4 * half + k, t * P:(t + 1) * P],
                              identr[:, :], start=True, stop=True)
                last.then_inc(s["f_tok"], 1)
            pe.wait_ge(s["f_toke"], 16)
            pe.wait_ge(s["f_flag"], 1)
            crowded = pe.value_load(flag[0:1, 0:1])
            with pe.If(crowded > 0):
                with pe.Fori(0, 3) as i:
                    group("moe", i, 8, spread=spread_gate)
                group("moe", 3, 8, spread=spread_gate)
            with pe.Else():
                pe.wait_ge(s["f_g"], 1)
                for h in range(2):
                    for k in range(KT):
                        gather(0, h, k, banks=4)
                gather_gates(0)
                turn_places(0)
                pe.wait_ge(s["f_xl"], 16)
                with pe.Fori(0, 3) as i:
                    gathered(i)
                gathered(3, last_group=True)
            norm(8)

        @block.scalar
        def _(act):
            actv = nc.scalar.activation

            def split_hi(n, value, tiles=None):
                act.wait_ge(loaded[n % RING], value)
                if tiles is not None:
                    act.wait_ge(acc_ready, tiles)
                actv(wh[:, n % RING].rearrange("p a b c -> p (a b c)"), raw[:, n % RING, :],
                     ACT.Copy).then_inc(hi_done, 1)

            def ahead(n, i=None):
                n += 3
                if n >= NBLK:
                    return
                value, tiles = 16 * (n // RING + 1), TILES_TO[n - RING] if n >= RING else None
                if i is not None:
                    value, tiles = i * (16 * 12 // RING) + value, i * 24 + tiles
                split_hi(n, value, tiles)

            def take(t, e, func, bank, ring, scale=1.0):
                act.wait_ge(acc_ready, t + 1)
                if not isinstance(e, int) or e >= 4:
                    act.wait_ge(ev_used, e - 3)
                actv(ev[:, ring, 2:S + 2], acc[:, bank, :], func, scale=scale).then_inc(evac, 1)

            def take_s(t, e, func=ACT.Copy):
                take(t, e, func, t % 4, e % 4)

            def direct(t, dst, src, scale=1.0):
                act.wait_ge(acc_ready, t + 1)
                actv(dst, src, ACT.Copy, scale=scale).then_inc(evac, 1)

            def square(q, src):
                if q >= 2:
                    act.wait_ge(sq_used, q - 1)
                actv(sq[:, q % 2, 0:src.shape[-1]], src, ACT.Square).then_inc(sq_ready, 1)

            def norm_root(r, nt=TT):
                actv(sml[:, 60:61], cs("eps", 0, 1), ACT.Sqrt)
                if r in SUMMED:
                    act.wait_ge(sq_used, KT * (r + 1))
                    sums = acc[:, :, 0]
                else:
                    act.wait_ge(st_sum, OTHERS[r])
                    sums = mb[:, 0, 0:nt]
                actv(sd[:, 0:nt], sums, ACT.Sqrt, bias=cs("eps", 0, 1), scale=1.0 / D).then_inc(sd_ready, 1)

            def operand_upper(r, k):
                act.wait_ge(s["op_n"], OPERANDS[r] + k + 1)
                actv(XH[:, k, :], tmp[:, k % 2, :], ACT.Copy).then_inc(s["op_hi"], 1)

            act.wait_ge(in_x, 16)
            for k in range(KT):
                if k == 4:
                    act.wait_ge(in_xb, 16)
                square(k, XT[:, k, :])
            act.wait_ge(in_par, 32)
            split_hi(0, 16)
            norm_root(0)
            for k in range(KT):
                operand_upper(0, k)
                if k in (1, 4):
                    split_hi(1 + k // 3, 16)
            for b in range(13):
                if b < 10:
                    ahead(B0["in"] + b)
                if b == 10:
                    act.wait_ge(ev_used, 14)
                    actv(GLO[:, :], GLO[:, :], ACT.Sigmoid)
                    actv(LO[0:64, :], LO[0:64, :], ACT.Tanh).then_inc(s["lora_act"], 1)
                    act.wait_ge(s["lam_dot"], 1)
                    actv(lam_e, lam_d, ACT.Exp).then_inc(s["lam_exp"], 1)
                for t in (2 * b, 2 * b + 1):
                    if t < 14:
                        take_s(t, t)
                    elif t < 18:
                        direct(t, QT[:, t - 14, :], acc[:, t % 4, :], 0.125)
                    elif t < 22:
                        direct(t, KD[:, t - 18, :], acc[:, t % 4, :])
                    else:
                        c, j = divmod(t - 22, 2)
                        direct(t, DV[:, 2 * j:2 * j + 2, c * 256:(c + 1) * 256],
                               acc[:, t % 4, :].rearrange("p (a b) -> p a b", a=2))

            def exp(u):
                w = (u % TT + 1) * P
                act.wait_ge(s["at_mx"], u + 1)
                for c in range(2):
                    x = 2 * (u % 2) + c
                    last = actv(SC[:, u % 2, c, 0:w], SC[:, u % 2, c, 0:w], ACT.Exp, bias=nmx[:, x:x + 1],
                                accum_out=den[:, x:x + 1])
                last.then_inc(s["at_e"], 1)

            def turned(u):
                h, i = divmod(u, TT)
                act.wait_ge(s["at_t"], u + 1)
                if i == 0 and h:
                    act.wait_ge(s["at_o"], h)
                actv(AT[:, 0:i + 1, i * P:(i + 1) * P], mb[:, 2, 0:(i + 1) * P].rearrange("p (a b) -> p a b", b=P),
                     ACT.Copy).then_inc(s["at_te"], 1)

            def head_square(h):
                act.wait_ge(s["at_o"], h + 1)
                actv(SQO[:, 0, :], mb[:, 3, :], ACT.Square).then_inc(s["at_sq"], 1)

            def head_root(h):
                act.wait_ge(s["at_ss"], h + 1)
                actv(hn, mb[:, 2, 0:TT], ACT.Sqrt, bias=cs("eps", 1, 2), scale=1.0 / P).then_inc(s["at_sd"], 1)

            def gbuf(ct):
                return ev[:, ct % 2, 2:S + 2]

            def up(ct):
                if ct < 4:
                    W = Wt[ct % 2]
                    act.wait_ge(s["rk_up"], ct + 1)
                    actv(W[:, 0, :], bank(0, 1), ACT.Sigmoid, bias=pr("w_decay0", ct))
                    actv(W[:, 1, :], bank(1, 1), ACT.Sigmoid, bias=pr("w_iclr0", ct)).then_inc(s["rk_sig"], 1)

            def up_gate(ct):
                if ct < 4:
                    W = Wt[ct % 2]
                    act.wait_ge(s["rk_upg"], ct + 1)
                    actv(gbuf(ct), bank(0, 1), ACT.Copy).then_inc(s["rk_g"], 1)
                    act.wait_ge(s["rk_kk"], ct + 1)
                    actv(W[:, 5, :], W[:, 4, :], ACT.Square).then_inc(s["rk_ksq"], 1)

            def exps(ct):
                if ct < 4:
                    W = Wt[ct % 2]
                    act.wait_ge(s["rk_cum"], ct + 1)
                    actv(W[:, 6, :], W[:, 2, :], ACT.Exp)
                    actv(W[:, 7, :], W[:, 2, :], ACT.Exp, scale=-1.0)
                    actv(W[:, 3, :], W[:, 3, :], ACT.Exp).then_inc(s["rk_exp"], 1)

            def roots(ct):
                if ct < 4:
                    act.wait_ge(s["rk_kmx"], ct + 1)
                    actv(kn, kn, ACT.Sqrt).then_inc(s["rk_ksd"], 1)

            def flat(a):
                return a.rearrange("p a b -> p (a b)")

            def tok(ct):
                act.wait_ge(s["rk_tok"], ct + 1)
                actv(AXb[:, :, :, 0, :], acc[:, 1, :].rearrange("p (t h c) -> p t h c", t=TT, h=2), ACT.Copy)
                actv(flat(Btok[:, :, :]), acc[:, 2, :], ACT.Copy)
                actv(flat(Ktok[:, :, :]), acc[:, 3, :], ACT.Copy)
                actv(flat(Vtok[:, :, :]), mb[:, 0, :], ACT.Copy).then_inc(s["rk_toke"], 1)

            def l0(ct):
                for hh in range(2):
                    act.wait_ge(s["rk_x"], 2 * ct + hh + 1)
                    actv(AXb[:, :, hh, 1, :], bank(hh, 1)[:, 0:TT * HD].rearrange("p (t c) -> p t c", t=TT),
                         ACT.Copy).then_inc(s["rk_xe"], 1)

            def turned_t(l):
                def run(ct):
                    for hh in range(2):
                        act.wait_ge(s["rk_tt"], 12 * ct + 2 * (l - 1) + hh + 1)
                        actv(flat(TTm[:, hh]), bank(hh, 1), ACT.Copy).then_inc(s["rk_tte"], 1)
                return run

            def wu(ct):
                turned_t(LEVELS)(ct)
                for hh in range(2):
                    act.wait_ge(s["rk_wu"], 2 * ct + hh + 1)
                    actv(flat(WU[:, hh]), bank(hh, 0), ACT.Copy).then_inc(s["rk_wue"], 1)

            def gh(ct):
                act.wait_ge(s["rk_gh"], 2 * ct + 2)
                actv(HSt[ct % 2][:, :, :].rearrange("p (t a) j -> p a t j", a=2),
                     acc[:, 0:2, 256:512].rearrange("p a (t j) -> p a t j", t=TT), ACT.Copy).then_inc(s["rk_hs"], 1)

            def mu(ct):
                W = Wt[ct % 2]
                act.wait_ge(s["rk_d"], ct + 1)
                actv(W[:, 2, :], W[:, 1, :], ACT.Square).then_inc(s["rk_dsq"], 1)

            def var(ct):
                act.wait_ge(s["rk_var"], ct + 1)
                actv(vn, acc[:, 2, 0:2 * TT].rearrange("p (t h) -> p t h", h=2), ACT.Sqrt, bias=cs("eps", 2, 3),
                     scale=1.0 / HD).then_inc(s["rk_sd"], 1)

            up(0)
            up_gate(0)
            exps(0)
            roots(0)
            main = {"tok": tok, "l0": l0, "wu": wu, "gh": gh, "mu": mu, "var": var}
            main |= {f"l{l}": turned_t(l) for l in range(1, LEVELS)}
            in_beats(main, {"exp": exp, "turned": turned, "head_square": head_square, "head_root": head_root,
                            "up": up, "up_gate": up_gate, "exps": exps, "roots": roots})

            def taken_out(t, dst, q):
                act.wait_ge(acc_ready, t + 1)
                if q >= 2:
                    act.wait_ge(sq_used, q - 1)
                actv(sq[:, q % 2, :], acc[:, t % 4, :], ACT.Square).then_inc(sq_ready, 1)
                actv(dst, acc[:, t % 4, :], ACT.Copy).then_inc(evac, 1)

            act.wait_ge(s["rk_y"], 4)
            for n in (13, 14, 15):
                split_hi(n, 16 * (n // RING + 1), TILES_TO[n - RING])
            for b in range(4):
                ahead(B0["out"] + b)
                for m in (2 * b, 2 * b + 1):
                    taken_out(T0["out"] + m, Fo[:, m, :], 8 + m)
            norm_root(1)

            for m in range(KT):
                act.wait_ge(x_ready, m + 1)
                square(16 + m, XT[:, m, :])
            norm_root(2)
            for k in range(KT):
                operand_upper(2, k)

            def group(name, i, hidden):
                loop = None if isinstance(i, int) else i
                k = i if loop is None else 0
                n0, t0, e0 = B0[name] + 12 * k, T0[name] + 24 * k, E0[name] + 24 * k
                add = (lambda v, per: v) if loop is None else (lambda v, per: loop * per + v)
                for b in range(hidden + 4):
                    ahead(n0 + b, loop)
                    for j in range(2):
                        func = ACT.Copy
                        if name == "moe" and b < hidden and j == 0:
                            func = ACT.Silu
                        take(add(t0 + 2 * b + j, 24), add(e0 + 2 * b + j, 24), func, (t0 + 2 * b + j) % 4,
                             (e0 + 2 * b + j) % 4)
                    if name == "ffn" and b < hidden:
                        act.wait_ge(ev_used, add(e0 + 2 * b + 1, 24))
                        actv(gl[:, b % 2, :], gl[:, b % 2, :], ACT.Gelu_apprx_tanh).then_inc(s["gelu_done"], 1)
                    if b >= hidden and loop is None and k == (2 if name == "ffn" else 3):
                        for m in (2 * (b - hidden), 2 * (b - hidden) + 1):
                            if name == "ffn":
                                act.wait_ge(s["acc_added"], m + 1)
                                square(24 + m, Fo[:, m, :])
                            else:
                                act.wait_ge(x_ready, 32 + m + 1)
                                square(64 + m, XT[:, m, :])

            with act.Fori(0, 2) as i:
                group("ffn", i, 8)
            group("ffn", 2, 6)
            norm_root(3)

            for m in range(KT):
                act.wait_ge(x_ready, 8 + m + 1)
                square(32 + m, XT[:, m, :])
            norm_root(4)
            for k in range(KT):
                operand_upper(4, k)
            for b in range(12):
                ahead(B0["mix"] + b)
                for t in (2 * b, 2 * b + 1):
                    take_s(T0["mix"] + t, E0["mix"] + t, ACT.Sigmoid if t < 8 and t % 2 else ACT.Copy)

            for m in range(KT):
                n, t, e = B0["gate"] + 2 * m, T0["gate"] + 5 * m, E0["gate"] + 5 * m
                ahead(n)
                take_s(t, e, ACT.Sigmoid)
                take_s(t + 1, e + 1, ACT.Sigmoid)
                ahead(n + 1)
                if m == 0:
                    for c in range(4):
                        act.wait_ge(s["la_d"], c + 1)
                        if c >= 2:
                            act.wait_ge(s["la_sum"], c - 1)
                        actv(sq[:, c % 2, :], CA[:, c, :], ACT.Square).then_inc(s["la_sq"], 1)
                    actv(sml[:, 60:61], cs("eps", 0, 1), ACT.Sqrt)
                    act.wait_ge(s["la_var"], 1)
                    actv(hn, mb[:, 1, 0:TT], ACT.Sqrt, bias=cs("eps", 0, 1),
                         scale=2.0 / D).then_inc(s["la_sd"], 1)
                    for c in range(4):
                        act.wait_ge(s["la_y"], c + 1)
                        actv(CA[:, c, :], CA[:, c, :], ACT.Silu, bias=pr("ln_a_b", c),
                             scale=pr("ln_a_g", c)).then_inc(s["la_act"], 1)
                take_s(t + 2, e + 2, ACT.Sigmoid)
                take_s(t + 3, e + 3)
                take_s(t + 4, e + 4)

            act.wait_ge(in_mem, 16)
            for k in range(KT):
                square(40 + k, MT[:, k, :])
            for b in range(4):
                ahead(B0["o"] + b)
                for m in (2 * b, 2 * b + 1):
                    take_s(T0["o"] + m, E0["o"] + m)
                if b == 0:
                    norm_root(5, 2)
            for m in range(KT):
                act.wait_ge(x_ready, 16 + m + 1)
                square(48 + m, XT[:, m, :])

            for b in range(8):
                ahead(B0["kv"] + b)
                for j in range(2):
                    t = T0["kv"] + 2 * b + j
                    if b < 4:
                        direct(t, KX[:, 2 * b + j, :], acc[:, t % 4, 0:N_MEM])
                    else:
                        direct(t, VX[:, j, (b - 4) * 256:(b - 3) * 256], acc[:, t % 4, 0:256])
            norm_root(6)
            for k in range(KT):
                operand_upper(6, k)
            for b in range(4):
                ahead(B0["q"] + b)
                for j in range(2):
                    t = T0["q"] + 2 * b + j
                    direct(t, QX[:, 2 * b + j, :], acc[:, t % 4, :], 1.0 / 16.0)

            def x_exp(u):
                act.wait_ge(s["xs_mx"], u + 1)
                actv(EXx[:, u % 2, :], x_bank(u), ACT.Exp, bias=nmx[:, u % 4:u % 4 + 1],
                     accum_out=den[:, u % 4:u % 4 + 1]).then_inc(s["xs_e"], 1)

            def x_squares(b):
                for m in (2 * b, 2 * b + 1):
                    act.wait_ge(x_ready, 24 + m + 1)
                    square(56 + m, XT[:, m, :])

            def x_turned(u):
                h, i = divmod(u, TT)
                act.wait_ge(s["xs_t"], u + 1)
                if i == 0 and h:
                    act.wait_ge(s["xs_o"], 2 * h)
                actv(PTx[:, :, i * P:(i + 1) * P], mb[:, 2 + u % 2, 0:2 * P].rearrange("p (a b) -> p a b", a=2),
                     ACT.Copy).then_inc(s["xs_te"], 1)

            x_exp(0)
            for u in range(4 * TT):
                if u + 1 < 4 * TT:
                    x_exp(u + 1)
                x_turned(u)
                if u % TT == TT - 1:
                    h = u // TT
                    for v in range(2):
                        act.wait_ge(s["xs_o"], 2 * h + v + 1)
                        actv(XH[:, 2 * h + v, :], acc[:, v, :], ACT.Copy).then_inc(s["xs_hi"], 1)
            for b in range(4):
                ahead(B0["xo"] + b)
                for m in (2 * b, 2 * b + 1):
                    take_s(T0["xo"] + m, E0["xo"] + m)
                if b:
                    x_squares(b - 1)
            x_squares(3)

            def places(i):
                for e in range(4):
                    act.wait_ge(s["f_turn"], i * 4 + (e + 1))
                    actv(G2[:, e, :], mb[:, 2 + e % 2, :], ACT.Copy).then_inc(s["f_turned"], 1)

            def gathered_upper(i, h, k, banks=2):
                act.wait_ge(s["f_gath"], i * 16 + (8 * h + k + 1))
                actv(XH[:, k, 256 * h:256 * h + 256], acc[:, g_bank(k, banks), 0:2 * P],
                     ACT.Copy).then_inc(s["f_xh"], 1)

            def gathered(i, last=False):
                n0, t0 = B0["moe"], T0["moe"]

                def next_block(b):
                    if last:
                        ahead(n0 + 36 + b)
                    else:
                        ahead(n0 + b, i)

                def hidden_upper(b):
                    act.wait_ge(s["f_ht"], i * 8 + (b + 1))
                    actv(GHH[:, b, :], mb[:, 2 + b % 2, 0:P], ACT.Copy).then_inc(s["f_hh"], 1)

                actv(sml[:, 60:61], cs("eps", 0, 1), ACT.Silu)
                for b in range(8):
                    act.wait_ge(acc_ready, i * 24 + (t0 + 2 * b + 2))
                    actv(tmp[:, b % 2, 0:P], acc[:, b % 2, 0:P], ACT.Silu).then_inc(s["f_silu"], 1)
                    if b:
                        hidden_upper(b - 1)
                    if b >= 4 and not last:
                        gathered_upper(i + 1, 0, 2 * (b - 4))
                        gathered_upper(i + 1, 0, 2 * (b - 4) + 1)
                    next_block(b + 1)
                if last:
                    hidden_upper(7)
                else:
                    gathered_upper(i + 1, 1, 0)
                    hidden_upper(7)
                    for k in range(1, KT):
                        gathered_upper(i + 1, 1, k)
                for b in range(4):
                    if b:
                        next_block(8 + b)
                    act.wait_ge(s["f_y"], i * 4 + (b + 1))
                    actv(YH[:, b % 2, 0:2, :].rearrange("p a b -> p (a b)"), mb[:, 0, :],
                         ACT.Copy).then_inc(s["f_yh"], 1)
                    act.wait_ge(acc_ready, i * 24 + (t0 + 16 + 2 * b + 2))
                    actv(YH[:, b % 2, 2:4, :].rearrange("p a b -> p (a b)"), mb[:, 1, :],
                         ACT.Copy).then_inc(s["f_yh"], 1)
                    if b == 3:
                        next_block(12)
                    if last and b:
                        last_squares(b - 1)
                if last:
                    last_squares(3)
                else:
                    places(i + 1)

            def last_squares(b):
                for m in (2 * b, 2 * b + 1):
                    act.wait_ge(s["f_add"], 24 + m + 1)
                    square(64 + m, XT[:, m, :])

            norm_root(7)
            for k in range(KT):
                operand_upper(7, k)
            for q in range(16):
                if q in (0, 5):
                    x, e = ((1, 2), (11, 12))[q // 5]
                    act.wait_ge(s["rt_sub"], 1 + q // 5)
                    actv(rt[:, e, :], rt[:, x, :], ACT.Exp).then_inc(s["rt_exp"], 1)
                t, half = q // 4, q // 2 % 2
                act.wait_ge(s["f_tok"], q + 1)
                actv((TXH, TXL)[q % 2][:, t, 512 * half:512 * half + 512], acc[:, q % 4, :],
                     ACT.Copy).then_inc(s["f_toke"], 1)
            act.wait_ge(s["f_flag"], 1)
            crowded = act.value_load(flag[0:1, 0:1])
            with act.If(crowded > 0):
                with act.Fori(0, 3) as i:
                    group("moe", i, 8)
                group("moe", 3, 8)
            with act.Else():
                for h in range(2):
                    for k in range(KT):
                        gathered_upper(0, h, k, banks=4)
                places(0)
                ahead(B0["moe"])
                with act.Fori(0, 3) as i:
                    gathered(i)
                gathered(3, last=True)
            norm_root(8)

        @block.vector
        def _(dve):
            v = nc.vector
            state = {"sem": dchain, "base": 0, "n": 0}

            def link(ins):
                state["n"] += 1
                ins.then_inc(state["sem"], 1)
                dve.wait_ge(state["sem"], state["base"] + state["n"])

            def loop(count, per, body):
                b, n = state["base"], state["n"]
                with dve.Fori(0, count) as i:
                    state["base"], state["n"] = i * per + (b + n), 0
                    body(i)
                    assert state["n"] == per, state["n"]
                state["base"], state["n"] = b, n + count * per

            def add_squares(q, w=S):
                dve.wait_ge(sq_ready, q + 1)
                if q % KT == 0:
                    v.tensor_copy(sqa[:, 0:w], sq[:, q % 2, 0:w]).then_inc(sq_used, 1)
                else:
                    dve.wait_ge(sq_used, q)
                    v.tensor_tensor(sqa[:, 0:w], sqa[:, 0:w], sq[:, q % 2, 0:w], ALU.add).then_inc(sq_used, 1)

            def norm_recip(r, nt=TT):
                dve.wait_ge(sd_ready, r + 1)
                v.reciprocal(rs[:, 0:nt], sd[:, 0:nt]).then_inc(rs_ready, 1)

            def split(src, hi, lo, done):
                link(v.tensor_copy(hi, src))
                v.tensor_tensor(lo, src, hi.bitcast(F32), ALU.subtract).then_inc(done, 1)

            def operand(r, gname):
                dve.wait_ge(rb_ready, r + 1)
                if r:
                    dve.wait_ge(xn_ready, OPERANDS[r])
                for k in range(KT + 1):
                    if k < KT:
                        if k >= 2:
                            dve.wait_ge(xn_ready, OPERANDS[r] + k - 1)
                        v.scalar_tensor_tensor(out=tmp[:, k % 2, :], in0=XT[:, k, :], scalar=pr(gname, k),
                                               in1=mb[:, 1, :], op0=ALU.mult, op1=ALU.mult).then_inc(s["op_n"], 1)
                    if k:
                        dve.wait_ge(s["op_hi"], OPERANDS[r] + k)
                        v.tensor_tensor(XL[:, k - 1, :], tmp[:, (k - 1) % 2, :], XH[:, k - 1, :].bitcast(F32),
                                        ALU.subtract).then_inc(xn_ready, 1)

            def residual(r, gname):
                dve.wait_ge(rb_ready, r + 1)
                for m in range(KT):
                    link(v.scalar_tensor_tensor(out=tmp[:, m % 2, :], in0=Fo[:, m, :], scalar=pr(gname, m),
                                                in1=mb[:, 1, :], op0=ALU.mult, op1=ALU.mult))
                    v.tensor_tensor(XT[:, m, :], XT[:, m, :], tmp[:, m % 2, :], ALU.add).then_inc(x_ready, 1)

            link(v.memset(ev[:, :, 0:2], 0.0))

            for k in range(KT):
                add_squares(k)
            norm_recip(0)
            dve.wait_ge(in_par, 32)
            operand(0, "ln_attn_pre")
            dsts = [LO[:, :], GLO[:, :]] + [K[:, c, :] for c in range(4)] + [R[:, c, :] for c in range(4)] \
                + [V[:, c, :] for c in range(4)]
            for t, dst in enumerate(dsts):
                dve.wait_ge(evac, t + 1)
                e = ev[:, t % 4, :]
                link(v.tensor_tensor(tmp[:, t % 2, :], e[:, 1:S + 1], e[:, 2:S + 2], ALU.subtract))
                v.scalar_tensor_tensor(out=dst, in0=tmp[:, t % 2, :], scalar=pr("mu", t), in1=e[:, 2:S + 2],
                                       op0=ALU.mult, op1=ALU.add).then_inc(ev_used, 1)
            dve.wait_ge(in_rest, 48)
            o = PO["lam"][0]
            for j in range(2):
                a, b = par[:, o + 128 * j:o + 128 * j + 64], par[:, o + 128 * j + 64:o + 128 * j + 128]
                link(v.tensor_tensor(tmp[:, 0, 64 * j:64 * j + 64], a, b, ALU.mult))
            v.tensor_reduce(lam_d, tmp[:, 0, 0:128].rearrange("p (a b) -> p a b", a=2), AX.X,
                            ALU.add).then_inc(s["lam_dot"], 1)
            dve.wait_ge(s["lam_exp"], 1)
            link(v.tensor_tensor(lam_n, lam_e[:, 1:2], lam_e[:, 0:1], ALU.subtract))
            link(v.tensor_scalar(lam_n, lam_n, -LAM_INIT, None, ALU.add))
            link(v.tensor_scalar(g08, pr("subln", 0), 1.0 - LAM_INIT, None, ALU.mult))

            def att_max(u):
                h, i = divmod(u, TT)
                w = (i + 1) * P
                slope = 2.0 ** (-8.0 * (h + 1) / 4)
                dve.wait_ge(s["at_sc"], u + 1)
                if u >= 2:
                    dve.wait_ge(s["at_t"], u - 1)
                for c in range(2):
                    link(v.scalar_tensor_tensor(out=SC[:, u % 2, c, 0:w], in0=cs("alibi", S - w, S), scalar=slope,
                                                in1=mb[:, 2 + c, 0:w], op0=ALU.mult, op1=ALU.add))
                x = slice(2 * (u % 2), 2 * (u % 2) + 2)
                link(v.tensor_reduce(mx[:, x], SC[:, u % 2, :, 0:w], AX.X, ALU.max))
                v.tensor_scalar(nmx[:, x], mx[:, x], -1.0, None, ALU.mult).then_inc(s["at_mx"], 1)

            def att_weights(u):
                w, x = (u % TT + 1) * P, 2 * (u % 2)
                a, b = SC[:, u % 2, 0, 0:w], SC[:, u % 2, 1, 0:w]
                dve.wait_ge(s["at_e"], u + 1)
                link(v.reciprocal(rden[:, x:x + 2], den[:, x:x + 2]))
                link(v.tensor_scalar(rden[:, x + 1:x + 2], rden[:, x + 1:x + 2], lam_n, None, ALU.mult))
                link(v.tensor_scalar(a, a, rden[:, x:x + 1], None, ALU.mult))
                v.scalar_tensor_tensor(out=a, in0=b, scalar=rden[:, x + 1:x + 2], in1=a, op0=ALU.mult,
                                       op1=ALU.add).then_inc(s["at_p"], 1)

            def head_norm(h):
                dve.wait_ge(s["at_sp"], h + 1)
                link(v.tensor_scalar(tmp[:, 0, :], mb[:, 2, :], g08, None, ALU.mult))
                v.tensor_tensor(OO[:, h, :], mb[:, 3, :], tmp[:, 0, :], ALU.mult).then_inc(s["at_done"], 1)

            def head_root(h):
                dve.wait_ge(s["at_sd"], h + 1)
                v.reciprocal(hn, hn).then_inc(s["at_rr"], 1)

            def decay(ct):
                if ct < 4:
                    W = Wt[ct % 2]
                    v.tensor_scalar(W[:, 4, :], K[:, ct, :], pr("k_k", ct), None, ALU.mult).then_inc(s["rk_kk"], 1)
                    dve.wait_ge(s["rk_sig"], ct + 1)
                    link(v.tensor_scalar(W[:, 0, :], W[:, 0, :], -DECAY_SCALE, None, ALU.mult))
                    link(v.tensor_tensor_scan(W[:, 2, :], cs("reset"), W[:, 0, :], 0.0, ALU.mult, ALU.add))
                    v.tensor_tensor(W[:, 3, :], W[:, 2, :], W[:, 0, :], ALU.subtract).then_inc(s["rk_cum"], 1)

            def key_norm(ct):
                if ct < 4:
                    dve.wait_ge(s["rk_kss"], ct + 1)
                    v.tensor_scalar(kn, bank(1, 1)[:, 0:2 * TT].rearrange("p (t h) -> p t h", h=2), 1e-24, None,
                                    ALU.max).then_inc(s["rk_kmx"], 1)

            def pc_of(ct):
                a = Wt[ct % 2][:, 6, :].rearrange("p (c j) -> p c j", c=NCH)
                return a[:, :, HD - 1:HD].to_broadcast([P, NCH, HD])

            def scaled(ct):
                if ct < 4:
                    W = Wt[ct % 2]
                    Kc = K[:, ct, :]
                    dve.wait_ge(s["rk_cum"], ct + 1)
                    link(v.tensor_scalar(W[:, 0, :], W[:, 1, :], -1.0, pr("k_a", ct), ALU.add, ALU.mult))
                    link(v.scalar_tensor_tensor(out=Kc, in0=W[:, 0, :], scalar=1.0, in1=Kc, op0=ALU.add,
                                                op1=ALU.mult))

            def key_root(ct):
                if ct < 4:
                    dve.wait_ge(s["rk_ksd"], ct + 1)
                    v.reciprocal(kn, kn).then_inc(s["rk_kr"], 1)

            def hats(ct):
                if ct < 4:
                    W = Wt[ct % 2]
                    dve.wait_ge(s["rk_ks"], ct + 1)
                    link(v.tensor_tensor(W[:, 4, :], W[:, 4, :], bank(1, 1), ALU.mult))
                    link(v.tensor_tensor(W[:, 1, :], W[:, 4, :], W[:, 1, :], ALU.mult))

            def by_chunk(a):
                return a.rearrange("p (c j) -> p c j", c=NCH)

            def hat_r(ct):
                if ct < 4:
                    W = Wt[ct % 2]
                    dve.wait_ge(s["rk_exp"], ct + 1)
                    v.tensor_tensor(AR[:, :, 1, :], by_tok(R[:, ct, :]), by_tok(W[:, 6, :]), ALU.mult)
                    link(v.tensor_tensor(KH[:, :], K[:, ct, :], W[:, 7, :], ALU.mult))
                    v.tensor_tensor(by_chunk(W[:, 2, :]), by_chunk(KH[:, :]), pc_of(ct), ALU.mult)

            def hat(ct):
                if ct < 4:
                    W = Wt[ct % 2]
                    v.scalar_tensor_tensor(out=AR[:, :, 0, :], in0=by_tok(W[:, 4, :]), scalar=-1.0,
                                           in1=by_tok(W[:, 3, :]), op0=ALU.mult, op1=ALU.mult)
                    link(v.tensor_tensor(BT[:, :], W[:, 1, :], W[:, 7, :], ALU.mult))

            def ends(ct):
                if ct < 4:
                    W = Wt[ct % 2]
                    v.tensor_tensor(by_chunk(W[:, 0, :]), by_chunk(BT[:, :]), pc_of(ct), ALU.mult)
                    v.scalar_tensor_tensor(out=W[:, 3, :], in0=R[:, ct, :], scalar=pr("r_k", ct), in1=K[:, ct, :],
                                           op0=ALU.mult, op1=ALU.mult).then_inc(s["rk_hat"], 1)

            def tok(ct):
                dve.wait_ge(s["rk_bsum"], ct + 1)
                v.tensor_tensor(BON[:, :], acc[:, 0, :], V[:, ct, :], ALU.mult).then_inc(s["rk_bonus"], 1)
                if ct:
                    normed(ct - 1)

            def masked(dst, ready, done):
                def run(ct):
                    mask = cs("mask_nr").unsqueeze(1).to_broadcast([P, 2, 2 * P])
                    for hh in range(2):
                        dve.wait_ge(ready, 2 * ct + hh + 1)
                        for x in range(2):
                            last = v.tensor_tensor(dst[:, hh, 2 * x:2 * x + 2].rearrange("p t a b -> p t (a b)"),
                                                   bank(hh, x).rearrange("p (t c) -> p t c", t=2), mask, ALU.mult)
                        last.then_inc(done, 1)
                return run

            def by_tok(a):
                return a.rearrange("p (t c) -> p t c", t=TT)

            def lv(l):
                return cs("mask_lv", l * P, (l + 1) * P).unsqueeze(1).to_broadcast([P, TT, P])

            def l0(ct):
                for hh in range(2):
                    dve.wait_ge(s["rk_q"], 12 * ct + hh + 1)
                    link(v.tensor_tensor(Qm[:, hh], by_tok(bank(hh, 0)), lv(0), ALU.mult))
                    v.tensor_tensor(Tm[:, hh], Qm[:, hh], ident.unsqueeze(1).to_broadcast([P, TT, P]),
                                    ALU.add).then_inc(s["rk_tm"], 1)

            def level(l):
                def run(ct):
                    for hh in range(2):
                        dve.wait_ge(s["rk_q"], 12 * ct + 2 * l + hh + 1)
                        v.tensor_tensor(Qm[:, hh], by_tok(bank(hh, 0)), lv(l), ALU.mult).then_inc(s["rk_qm"], 1)
                    for hh in range(2):
                        dve.wait_ge(s["rk_t"], 10 * ct + 2 * (l - 1) + hh + 1)
                        v.tensor_tensor(Tm[:, hh], Tm[:, hh], by_tok(bank(hh, 1)), ALU.add).then_inc(s["rk_tm"], 1)
                return run

            def gh(ct):
                GT, ST, HS = GTt[ct % 2], STt[ct % 2], HSt[ct % 2]
                link(v.tensor_tensor(GT[:, :, :], cs("id64").unsqueeze(1).to_broadcast([P, NCH, HD]), pc_of(ct),
                                     ALU.mult))
                for hh in range(2):
                    ps = slice(HD * hh, HD * hh + HD)
                    dve.wait_ge(s["rk_z"], 2 * ct + hh + 1)
                    v.tensor_tensor(Z[ps, :, :], by_tok(bank(hh, 1)[ps]), AR[ps, :, 1, :],
                                    ALU.add).then_inc(s["rk_zs"], 1)
                dve.wait_ge(s["rk_hs"], ct + 1)
                g2 = GT[:, :, :].rearrange("p (t a) j -> p a t j", a=2)
                v.tensor_tensor(g2, g2, acc[:, 0:2, 0:256].rearrange("p a (t j) -> p a t j", t=TT),
                                ALU.add).then_inc(s["rk_gs"], 1)
                v.tensor_copy(ST[:, 1, :], HS[:, 0, :]).then_inc(s["rk_st"], 1)

            def enter(c):
                def run(ct):
                    dve.wait_ge(s["rk_s"], 6 * ct + c - 1)
                    v.tensor_tensor(STt[ct % 2][:, c, :], mb[:, 0, 0:HD], HSt[ct % 2][:, c - 1, :],
                                    ALU.add).then_inc(s["rk_st"], 1)
                return run

            def y(ct):
                dve.wait_ge(s["rk_y"], ct + 1)
                v.tensor_tensor(Wt[ct % 2][:, 0, :], acc[:, 2, :], BON[:, :], ALU.add).then_inc(s["rk_ys"], 1)

            def mu(ct):
                W = Wt[ct % 2]
                dve.wait_ge(s["rk_mu"], ct + 1)
                v.scalar_tensor_tensor(out=W[:, 1, :], in0=mb[:, 0, :], scalar=-1.0 / HD, in1=W[:, 0, :],
                                       op0=ALU.mult, op1=ALU.add).then_inc(s["rk_d"], 1)

            def var(ct):
                dve.wait_ge(s["rk_sd"], ct + 1)
                v.reciprocal(vn, vn).then_inc(s["rk_vr"], 1)

            def normed(ct):
                W = Wt[ct % 2]
                dve.wait_ge(s["rk_vs"], ct + 1)
                link(v.tensor_tensor(W[:, 1, :], W[:, 1, :], mb[:, 1, :], ALU.mult))
                link(v.tensor_scalar(W[:, 1, :], W[:, 1, :], pr("ln_x_w", ct), pr("ln_x_b", ct), ALU.mult, ALU.add))
                v.tensor_tensor(R[:, ct, :], W[:, 1, :], ev[:, ct % 2, 2:S + 2], ALU.mult).then_inc(s["rk_done"], 1)

            decay(0)
            key_norm(0)
            scaled(0)
            key_root(0)
            hat_r(0)
            hats(0)
            hat(0)
            ends(0)
            main = {"tok": tok, "nr": masked(NR, s["rk_nr"], s["rk_nrm"]),
                    "ak": masked(AKRK, s["rk_ak"], s["rk_akm"]), "l0": l0, "gh": gh, "y": y, "mu": mu, "var": var}
            main |= {f"l{l}": level(l) for l in range(1, LEVELS)} | {f"s{c}": enter(c) for c in range(2, NCH)}
            in_beats(main, {"max": att_max, "weights": att_weights, "head_norm": head_norm, "head_root": head_root,
                            "decay": decay, "key_norm": key_norm, "roots": key_root, "hat_r": hat_r,
                            "scaled": scaled, "hats": hats, "hat": hat, "ends": ends})
            normed(3)

            dve.wait_ge(s["rk_done"], 4)
            for k in range(KT):
                src = R[:, k, :] if k < 4 else OO[:, k - 4, :]
                split(src, XH[:, k, :], XL[:, k, :], s["mixed"])
            for m in range(KT):
                add_squares(8 + m)
            norm_recip(1)
            dve.wait_ge(in_x2, 16)
            residual(1, "ln_attn_post")

            def conv3(dst, e, w, b=None, done=None):
                if b is None:
                    link(v.tensor_scalar(dst, e[:, 2:S + 2], w[2], None, ALU.mult))
                else:
                    link(v.tensor_scalar(dst, e[:, 2:S + 2], w[2], b, ALU.mult, ALU.add))
                link(v.scalar_tensor_tensor(out=dst, in0=e[:, 1:S + 1], scalar=w[1], in1=dst, op0=ALU.mult,
                                            op1=ALU.add))
                return v.scalar_tensor_tensor(out=dst, in0=e[:, 0:S], scalar=w[0], in1=dst, op0=ALU.mult, op1=ALU.add)

            def lower_rest(b, i=0):
                if isinstance(i, int) and 12 * i + b >= 48:
                    return
                n = B0["moe"] + b
                dve.wait_ge(hi_done, i * 12 + (n + 1))
                v.tensor_tensor(wl[:, n % RING, KT - K_DVE:].rearrange("p a b c -> p (a b c)"),
                                raw[:, n % RING, (KT - K_DVE) * 2 * P:],
                                wh[:, n % RING, KT - K_DVE:].rearrange("p a b c -> p (a b c)").bitcast(F32),
                                ALU.subtract).then_inc(s["low_dve"], 1)

            def group(name, i, hidden, last=False):
                loop_i = not isinstance(i, int)
                k = 0 if loop_i else i
                t0, e0 = T0[name] + 24 * k, E0[name] + 24 * k
                add = (lambda x, per: i * per + x) if loop_i else (lambda x, per: x)
                h0 = {"ffn": 0, "moe": 22}[name] + 8 * k
                if name == "ffn":
                    src = par[:, PO["conv"][0] + 64 * i:PO["conv"][0] + 64 * i + 64] if not loop_i else \
                        par[:, bass.ds(i * 64 + PO["conv"][0], 64)]
                    link(v.tensor_copy(cpar[:, :], src))
                else:
                    gsrc = gateg[:, :, :, :].rearrange("p g t e -> p (g t e)")
                    src = gsrc[:, 16 * i:16 * i + 16] if not loop_i else gsrc[:, bass.ds(i * 16, 16)]
                    v.tensor_copy(gcur[:, :, :].rearrange("p t e -> p (t e)"), src).then_inc(s["gate_ready"], 1)
                for b in range(hidden):
                    dve.wait_ge(evac, add(t0 + 2 * b + 1, 24))
                    ea, eb = ev[:, (e0 + 2 * b) % 4, :], ev[:, (e0 + 2 * b + 1) % 4, :]
                    if name == "ffn":
                        c = [cpar[:, 8 * b + x:8 * b + x + 1] for x in range(8)]
                        conv3(gl[:, b % 2, :], ea, c[0:3], c[3]).then_inc(ev_used, 1)
                        dve.wait_ge(evac, add(t0 + 2 * b + 2, 24))
                        conv3(yv[:, b % 2, :], eb, c[4:7], c[7]).then_inc(ev_used, 1)
                        dve.wait_ge(ev_used, add(e0 + 2 * b + 2, 24))
                        dve.wait_ge(s["gelu_done"], add(8 * k + b + 1, 8))
                        link(v.tensor_tensor(tmp[:, b % 2, :], gl[:, b % 2, :], yv[:, b % 2, :], ALU.mult))
                    else:
                        dve.wait_ge(evac, add(t0 + 2 * b + 2, 24))
                        v.tensor_tensor(gl[:, b % 2, :], ea[:, 2:S + 2], eb[:, 2:S + 2],
                                        ALU.mult).then_inc(ev_used, 2)
                        dve.wait_ge(ev_used, add(e0 + 2 * b + 2, 24))
                        dve.wait_ge(s["gb_ready"], add(4 * k + b // 2 + 1, 4))
                        link(v.tensor_tensor(tmp[:, b % 2, :], gl[:, b % 2, :], mb[:, 2 + b // 2 % 2, :], ALU.mult))
                    split(tmp[:, b % 2, :], HH[:, b, :], HL[:, b, :], s["hid_ready"])
                    if name == "moe":
                        lower_rest(b + 2, i)
                dst = Fo if name == "ffn" else XT
                for m in range(KT):
                    dve.wait_ge(evac, add(t0 + 2 * hidden + m + 1, 24))
                    e = ev[:, (e0 + 2 * hidden + m) % 4, 2:S + 2]
                    link(v.tensor_tensor(dst[:, m, :], dst[:, m, :], e, ALU.add))
                    v.nop().then_inc(ev_used, 1)
                    if name == "moe" and m % 2:
                        lower_rest(8 + m // 2 + 2, i)
                    if last:
                        v.nop().then_inc(s["acc_added"] if name == "ffn" else x_ready, 1)
                        if m:
                            add_squares((24 if name == "ffn" else 64) + m - 1)
                if last:
                    add_squares((24 if name == "ffn" else 64) + KT - 1)

            norm_recip(2)
            operand(2, "ln_ffn_pre")
            link(v.memset(Fo[:, :, :], 0.0))
            loop(2, 1 + 8 * 6 + 8, lambda i: group("ffn", i, 8))
            group("ffn", 2, 6, last=True)
            norm_recip(3)
            residual(3, "ln_ffn_post")
            norm_recip(4)
            operand(4, "norm_mix")
            link(v.memset(APAD[:, :, 0:CONV_A - 1], 0.0))
            link(v.memset(cpad[:, 0:2], 0.0))
            link(v.memset(upad[:, :, 0:POOL_PAD], 0.0))
            t0, e0 = T0["mix"], E0["mix"]
            taps_done, taps_at = [0] * 4, [None] * 4

            def tap(c):
                j = taps_done[c]
                x, w = APAD[:, c, j:j + S], pr("conv_a_w", c * CONV_A + j)
                if j == 0:
                    ins = v.tensor_scalar(CA[:, c, :], x, w, pr("conv_a_b", c), ALU.mult, ALU.add)
                else:
                    dve.wait_ge(dchain, state["base"] + taps_at[c])
                    ins = v.scalar_tensor_tensor(out=CA[:, c, :], in0=x, scalar=w, in1=CA[:, c, :],
                                                 op0=ALU.mult, op1=ALU.add)
                state["n"] += 1
                ins.then_inc(dchain, 1)
                taps_done[c], taps_at[c] = j + 1, state["n"]

            def some_taps(count, tiles=4):
                for _ in range(count):
                    left = [c for c in range(tiles) if taps_done[c] < CONV_A]
                    if left:
                        tap(min(left, key=lambda c: (taps_at[c] or 0, c)))

            for c in range(4):
                dve.wait_ge(evac, t0 + 2 * c + 2)
                v.tensor_tensor(APAD[:, c, CONV_A - 1:], ev[:, (e0 + 2 * c) % 4, 2:S + 2],
                                ev[:, (e0 + 2 * c + 1) % 4, 2:S + 2], ALU.mult).then_inc(ev_used, 2)
                dve.wait_ge(ev_used, e0 + 2 * c + 2)
                some_taps(TAPS, c + 1)
            for c in range(4):
                t, e = t0 + 8 + 3 * c, e0 + 8 + 3 * c
                some_taps(10)
                dve.wait_ge(evac, t + 2)
                v.tensor_tensor(cpad[:, 2:], ev[:, e % 4, 2:S + 2], ev[:, (e + 1) % 4, 2:S + 2],
                                ALU.mult).then_inc(ev_used, 2)
                dve.wait_ge(ev_used, e + 2)
                link(conv3(tmp[:, 0, :], cpad, [pr("conv_c", 3 * c + x) for x in range(3)]))
                dve.wait_ge(evac, t + 3)
                v.tensor_tensor(tmp[:, 1, :], tmp[:, 0, :], ev[:, (e + 2) % 4, 2:S + 2],
                                ALU.mult).then_inc(ev_used, 1)
                dve.wait_ge(ev_used, e + 3)
                split(tmp[:, 1, :], CH[:, c, :], CL[:, c, :], dchain)
                state["n"] += 1
                some_taps(6)
            for g in range(4):
                t, e = t0 + 20 + g, e0 + 20 + g
                some_taps(6)
                dve.wait_ge(evac, t + 1)
                x = ev[:, e % 4, :]
                cur, oth = upad[:, 0, :], upad[:, 1, :]
                link(v.tensor_tensor(cur[:, POOL_PAD:], x[:, 2:S + 2], x[:, 1:S + 1], ALU.add))
                for step in [2, 4, 8][:g]:
                    link(v.tensor_tensor(oth[:, POOL_PAD:], cur[:, POOL_PAD:],
                                         cur[:, POOL_PAD - step:POOL_PAD - step + S], ALU.add))
                    cur, oth = oth, cur
                link(v.scalar_tensor_tensor(out=PL[:, g, :], in0=cur[:, POOL_PAD:], scalar=0.5 ** (g + 1),
                                            in1=x[:, 2:S + 2], op0=ALU.mult, op1=ALU.subtract))
                link(v.tensor_tensor(tmp[:, 0, 0:POOL_PAD], cur[:, POOL_PAD:2 * POOL_PAD],
                                     cs("invcnt", g * POOL_PAD, (g + 1) * POOL_PAD), ALU.mult))
                v.tensor_tensor(PL[:, g, 0:POOL_PAD], tmp[:, 0, 0:POOL_PAD], x[:, 2:POOL_PAD + 2],
                                ALU.subtract).then_inc(ev_used, 1)
                dve.wait_ge(ev_used, e + 1)
            some_taps(4 * CONV_A)
            dve.wait_ge(dchain, state["base"] + state["n"])

            link(v.tensor_tensor(sqa[:, :], CA[:, 0, :], CA[:, 1, :], ALU.add))
            link(v.tensor_tensor(sqa[:, :], sqa[:, :], CA[:, 2, :], ALU.add))
            v.tensor_tensor(sqa[:, :], sqa[:, :], CA[:, 3, :], ALU.add).then_inc(s["la_in"], 1)
            dve.wait_ge(s["la_mu"], 1)
            for c in range(4):
                v.scalar_tensor_tensor(out=CA[:, c, :], in0=mb[:, 0, :], scalar=-2.0 / D, in1=CA[:, c, :],
                                       op0=ALU.mult, op1=ALU.add).then_inc(s["la_d"], 1)
            for c in range(4):
                dve.wait_ge(s["la_sq"], c + 1)
                if c == 0:
                    v.tensor_copy(sqa[:, :], sq[:, 0, :]).then_inc(s["la_sum"], 1)
                else:
                    dve.wait_ge(s["la_sum"], c)
                    v.tensor_tensor(sqa[:, :], sqa[:, :], sq[:, c % 2, :], ALU.add).then_inc(s["la_sum"], 1)
            dve.wait_ge(s["la_sd"], 1)
            v.reciprocal(hn, hn).then_inc(s["la_rr"], 1)
            dve.wait_ge(s["la_sp"], 1)
            for c in range(4):
                v.tensor_tensor(CA[:, c, :], CA[:, c, :], mb[:, 1, :], ALU.mult).then_inc(s["la_y"], 1)
            for c in range(4):
                dve.wait_ge(s["la_act"], c + 1)
                split(CA[:, c, :], AH[:, c, :], AL[:, c, :], s["ac_ready"])
            dve.wait_ge(s["ac_ready"], 4)
            for m in range(KT):
                t, e = T0["gate"] + 5 * m, E0["gate"] + 5 * m
                tile = lambda x: ev[:, (e + x) % 4, 2:S + 2]
                dve.wait_ge(s["p_mm"], m + 1)
                dve.wait_ge(evac, t + 2)
                link(v.scalar_tensor_tensor(out=tmp[:, 0, :], in0=mb[:, 2 + m % 2, :], scalar=pr("pool_scale", m),
                                            in1=tile(1), op0=ALU.mult, op1=ALU.mult))
                dve.wait_ge(evac, t + 4)
                v.tensor_tensor(tmp[:, 1, :], tile(0), tile(3), ALU.mult).then_inc(ev_used, 2)
                dve.wait_ge(ev_used, e + 2)
                link(v.tensor_tensor(MG[:, m, :], tmp[:, 0, :], tmp[:, 1, :], ALU.add))
                dve.wait_ge(evac, t + 5)
                v.tensor_tensor(tmp[:, 1, :], tile(2), tile(4), ALU.mult).then_inc(ev_used, 3)
                dve.wait_ge(ev_used, e + 5)
                v.tensor_tensor(MG[:, m, :], MG[:, m, :], tmp[:, 1, :], ALU.add).then_inc(s["mg_ready"], 1)

            def add_tile(name, m):
                dve.wait_ge(evac, T0[name] + m + 1)
                link(v.tensor_tensor(XT[:, m, :], XT[:, m, :], ev[:, (E0[name] + m) % 4, 2:S + 2], ALU.add))
                v.nop().then_inc(ev_used, 1)
                v.nop().then_inc(x_ready, 1)

            dve.wait_ge(s["mg_ready"], KT)
            for k in range(KT):
                split(MG[:, k, :], XH[:, k, :], XL[:, k, :], s["mg_ready"])
            for k in range(KT):
                add_squares(40 + k, N_MEM)
            add_tile("o", 0)
            add_tile("o", 1)
            norm_recip(5, 2)
            add_tile("o", 2)
            add_tile("o", 3)
            dve.wait_ge(rb_ready, 6)
            for k in range(KT):
                link(v.scalar_tensor_tensor(out=tmp[:, k % 2, 0:N_MEM], in0=MT[:, k, :], scalar=pr("norm_mem", k),
                                            in1=mb[:, 1, 0:N_MEM], op0=ALU.mult, op1=ALU.mult))
                split(tmp[:, k % 2, 0:N_MEM], MH[:, k, :], ML[:, k, :], s["mem_ready"])
            for m in range(4, KT):
                add_tile("o", m)
            for m in range(KT):
                add_squares(48 + m)

            def x_max(u):
                dve.wait_ge(s["xs_sc"], u + 1)
                link(v.tensor_reduce(mx[:, u % 4:u % 4 + 1], x_bank(u), AX.X, ALU.max))
                v.tensor_scalar(nmx[:, u % 4:u % 4 + 1], mx[:, u % 4:u % 4 + 1], -1.0, None,
                                ALU.mult).then_inc(s["xs_mx"], 1)

            def x_weights(u):
                dve.wait_ge(s["xs_e"], u + 1)
                link(v.reciprocal(rden[:, u % 4:u % 4 + 1], den[:, u % 4:u % 4 + 1]))
                if u >= 2:
                    dve.wait_ge(s["xs_t"], u - 1)
                v.tensor_scalar(PX[:, u % 2, :], EXx[:, u % 2, :], rden[:, u % 4:u % 4 + 1], None,
                                ALU.mult).then_inc(s["xs_p"], 1)

            norm_recip(6)
            operand(6, "norm_x")
            x_max(0)
            x_max(1)
            for u in range(4 * TT):
                x_weights(u)
                if u + 2 < 4 * TT:
                    x_max(u + 2)
                if u % TT == TT - 1:
                    h = u // TT
                    for j in range(2):
                        dve.wait_ge(s["xs_hi"], 2 * h + j + 1)
                        v.tensor_tensor(XL[:, 2 * h + j, :], acc[:, j, :], XH[:, 2 * h + j, :].bitcast(F32),
                                        ALU.subtract).then_inc(s["xs_done"], 1)
            for m in range(KT):
                add_tile("xo", m)
                if m >= 3 and m % 2:
                    add_squares(56 + m - 3)
                    add_squares(56 + m - 2)
            add_squares(62)
            add_squares(63)

            def route():
                r = lambda j: rt[:, j, :].rearrange("p (t c) -> p t c", t=TT)
                red = lambda j: rt[:, j, 0:TT]
                wide = lambda j: rt[:, j, 0:TT].unsqueeze(2).to_broadcast([P, TT, 4])
                rank = cs("rank").unsqueeze(1).to_broadcast([P, TT, 4])

                def best(p, eq, top, hot):
                    link(v.tensor_reduce(red(top), r(p), AX.X, ALU.max))
                    link(v.tensor_tensor(r(eq), r(p), wide(top), ALU.is_equal))
                    link(v.tensor_tensor(r(eq), r(eq), rank, ALU.mult))
                    link(v.tensor_reduce(red(23), r(eq), AX.X, ALU.max))
                    link(v.tensor_tensor(r(hot), r(eq), wide(23), ALU.is_equal))

                def softmax_in(src, to):
                    link(v.tensor_reduce(red(0), src, AX.X, ALU.max))
                    v.tensor_tensor(r(to), src, wide(0), ALU.subtract).then_inc(s["rt_sub"], 1)

                def softmax_out(p):
                    link(v.tensor_reduce(red(0), r(p), AX.X, ALU.add))
                    link(v.reciprocal(red(22), red(0)))
                    link(v.tensor_tensor(r(p), r(p), wide(22), ALU.mult))

                dve.wait_ge(s["rt_lg"], 1)
                link(v.tensor_tensor(lg[:, :, :], acc[:, :, 0:20],
                                     pr("b_router", 0, 20).unsqueeze(1).to_broadcast([P, TT, 20]), ALU.add))
                softmax_in(lg[:, :, 0:4], 1)
                dve.wait_ge(s["rt_exp"], 1)
                softmax_out(2)
                best(2, 3, 4, 5)
                for t in range(TT):
                    link(v.tensor_tensor(rt3[:, t], lg[:, t, 4:20].rearrange("p (g e) -> p g e", g=4),
                                         rt[:, 5, 4 * t:4 * t + 4].unsqueeze(2).to_broadcast([P, 4, 4]), ALU.mult))
                link(v.tensor_reduce(r(10), rt3[:, :, :, :].rearrange("p t g e -> p t e g"), AX.X, ALU.add))
                softmax_in(r(10), 11)
                dve.wait_ge(s["rt_exp"], 2)
                softmax_out(12)
                best(12, 13, 14, 15)
                link(v.scalar_tensor_tensor(out=r(16), in0=r(15), scalar=-2.0, in1=r(12), op0=ALU.mult, op1=ALU.add))
                best(16, 13, 17, 18)
                link(v.tensor_tensor(red(19), red(14), red(17), ALU.add))
                link(v.reciprocal(red(20), red(19)))
                link(v.tensor_tensor(red(20), red(20), red(4), ALU.mult))
                link(v.tensor_tensor(r(15), r(15), r(18), ALU.add))
                v.tensor_tensor(chosen[:, :, :, :], r(15).unsqueeze(1).to_broadcast([P, 4, TT, 4]),
                                r(5).rearrange("p t g -> p g t").unsqueeze(3).to_broadcast([P, 4, TT, 4]),
                                ALU.mult).then_inc(s["f_mask"], 1)
                dve.wait_ge(s["f_mask"], 1)
                link(v.tensor_tensor(r(15), r(15), r(12), ALU.mult))
                link(v.tensor_tensor(r(15), r(15), wide(20), ALU.mult))
                for g in range(4):
                    link(v.tensor_tensor(gateg[:, g], r(15), r(5)[:, :, g:g + 1].to_broadcast([P, TT, 4]), ALU.mult))

            def place(i):
                for src, dst, w in ((posn, pcur, 16), (gparts, gtwo, 32)):
                    src = src[:, :, :, :] if w == 16 else src[:, :, :, :, :]
                    src = src.rearrange("p g t e -> p (g t e)" if w == 16 else "p g t e x -> p (g t e x)")
                    src = src[:, w * i:w * i + w] if isinstance(i, int) else src[:, bass.ds(i * w, w)]
                    dst = dst[:, :, :].rearrange("p t e -> p (t e)") if w == 16 else \
                        dst[:, :, :, :].rearrange("p t e x -> p (t e x)")
                    done = v.tensor_copy(dst, src)
                link(done)
                v.tensor_tensor(G1[:, :, :, :].rearrange("p t e c -> p (t e) c"),
                                cs("count").unsqueeze(1).to_broadcast([P, 16, P]),
                                pcur[:, :, :].rearrange("p t e -> p (t e)").unsqueeze(2).to_broadcast([P, 16, P]),
                                ALU.is_equal).then_inc(s["f_g"], 1)

            def slot_gates(i):
                dve.wait_ge(s["f_gate"], i + 1)
                dve.wait_ge(s["f_hid"], i * 8)
                v.tensor_reduce(gslot[:, :], mb[:, 0, 0:8].rearrange("p (e x) -> p e x", x=2), AX.X,
                                ALU.add).then_inc(s["f_gslot"], 1)

            def gathered_lower(i, h, k, banks=2):
                c = slice(256 * h, 256 * h + 256)
                dve.wait_ge(s["f_xh"], i * 16 + (8 * h + k + 1))
                v.tensor_tensor(XL[:, k, c], acc[:, g_bank(k, banks), 0:2 * P], XH[:, k, c].bitcast(F32),
                                ALU.subtract).then_inc(s["f_xl"], 1)

            def gathered(i, last=False):
                if not last:
                    dve.wait_ge(s["f_turn"], i * 4 + 4)
                    place(i + 1)
                dve.wait_ge(s["f_gslot"], i + 1)

                def hidden_lower(b):
                    dve.wait_ge(s["f_hh"], i * 8 + (b + 1))
                    v.tensor_tensor(GHL[:, b, :], mb[:, 2 + b % 2, 0:P], GHH[:, b, :].bitcast(F32),
                                    ALU.subtract).then_inc(s["f_hl"], 1)

                for b in range(8):
                    dve.wait_ge(s["f_silu"], i * 8 + (b + 1))
                    v.scalar_tensor_tensor(out=tmp[:, b % 2, P:2 * P], in0=acc[:, b % 2, P:2 * P],
                                           scalar=gslot[:, b // 2:b // 2 + 1], in1=tmp[:, b % 2, 0:P],
                                           op0=ALU.mult, op1=ALU.mult).then_inc(s["f_hid"], 1)
                    lower_rest(b + 2, i)
                    if b:
                        hidden_lower(b - 1)
                    if b >= 4 and not last:
                        gathered_lower(i + 1, 0, 2 * (b - 4))
                        gathered_lower(i + 1, 0, 2 * (b - 4) + 1)
                lower_rest(10, i)
                if last:
                    hidden_lower(7)
                else:
                    slot_gates(i + 1)
                    gathered_lower(i + 1, 1, 0)
                    hidden_lower(7)
                    for k in range(1, KT):
                        gathered_lower(i + 1, 1, k)

                def added(b):
                    for j in range(2):
                        m = 2 * b + j
                        dve.wait_ge(s["f_out"], i * 8 + (m + 1))
                        if m == 0:
                            dve.wait_ge(s["f_add"], i * 8)
                        v.tensor_tensor(XT[:, m, :], XT[:, m, :], acc[:, 2 + j, :], ALU.add).then_inc(s["f_add"], 1)
                    if last:
                        for m in (2 * b, 2 * b + 1):
                            add_squares(64 + m)

                for b in range(4):
                    for x in range(2):
                        dve.wait_ge(s["f_yh"], i * 8 + (2 * b + x + 1))
                        v.tensor_tensor(YL[:, b % 2, 2 * x:2 * x + 2, :].rearrange("p a b -> p (a b)"), mb[:, x, :],
                                        YH[:, b % 2, 2 * x:2 * x + 2, :].rearrange("p a b -> p (a b)").bitcast(F32),
                                        ALU.subtract).then_inc(s["f_yl"], 1)
                    if b < 3:
                        lower_rest(11 + b, i)
                    if b:
                        added(b - 1)
                added(3)

            link(v.tensor_copy(identr[:, :], ident))
            link(v.tensor_copy(uptor[:, :], cs("upto")))
            link(v.tensor_copy(onesr[:, :], ones))
            o = PO["w_router"][0]
            wr = par[:, o:o + KT * 20].rearrange("p (k c) -> p k c", k=KT)
            split(wr, wrh[:, :, :], wrl[:, :, :], s["wr_ready"])
            norm_recip(7)
            operand(7, "norm_ffn")
            route()
            gp = gateg[:, :, :, :].rearrange("p g t e -> p (g t e)")
            gq = gparts[:, :, :, :, :].rearrange("p g t e x -> p (g t e) x")
            link(v.tensor_copy(gq[:, :, 0], gp))
            v.tensor_tensor(gq[:, :, 1], gp, gq[:, :, 0].bitcast(F32), ALU.subtract)
            dve.wait_ge(s["f_count"], 1)
            v.tensor_tensor(posn[:, :, :, :], mb[:, 0, 0:TT * 16].rearrange("p (t g e) -> p g t e", t=TT, g=4),
                            chosen[:, :, :, :].bitcast(F32), ALU.mult)
            link(v.tensor_reduce(most[:, 0:1], mb[:, 0, TT * 16:TT * 16 + 16], AX.X, ALU.max))
            link(v.tensor_scalar(most[:, 1:2], most[:, 0:1], P + 0.5, None, ALU.is_gt))
            v.tensor_copy(flag[:, :], most[:, 1:2]).then_inc(s["f_flag"], 1)
            place(0)
            lower_rest(0)
            lower_rest(1)
            dve.wait_ge(s["f_flag"], 1)
            crowded = dve.value_load(flag[0:1, 0:1])
            with dve.If(crowded > 0):
                loop(3, 16 + 8, lambda i: group("moe", i, 8))
                group("moe", 3, 8, last=True)
            with dve.Else():
                before = dict(state)
                state.update(sem=s["fchain"], base=0, n=0)
                for h in range(2):
                    for k in range(KT):
                        gathered_lower(0, h, k, banks=4)
                slot_gates(0)
                loop(3, 1, gathered)
                gathered(3, last=True)
                state.update(before)
            norm_recip(8)
            dve.wait_ge(rb_ready, 9)
            for m in range(KT):
                v.scalar_tensor_tensor(out=XT[:, m, :], in0=XT[:, m, :], scalar=pr("norm_f", m), in1=mb[:, 1, :],
                                       op0=ALU.mult, op1=ALU.mult).then_inc(s["final_ready"], 1)



def pack(inputs):
    import numpy as np

    g = {n: np.asarray(a) for n, a in inputs.items()}
    W = {n: g[n][0] for n in ("w_in", "w_out", "w_up", "w_down", "w_in_2", "w_a_out_2", "w_c_out_2", "w_o_2",
                              "w_xq_2", "w_xkv_2", "w_xo_2", "w_e_gate_2", "w_e_up_2", "w_e_down_2")}

    def tile(w, c):
        t = w[:, c:c + P].reshape(-1, P, P).transpose(1, 0, 2)
        if t.shape[1] < KT:
            t = np.concatenate([t, np.zeros((P, KT - t.shape[1], P), t.dtype)], axis=1)
        return t

    tiles = []
    order = [12 * P, 13 * P] + [c * P for c in (4, 5, 6, 7, 0, 1, 2, 3, 8, 9, 10, 11)] \
        + [c * P for c in range(14, 26)]
    tiles += [tile(W["w_in"], c) for c in order]
    tiles += [tile(W["w_out"], m * P) for m in range(KT)]
    for a, b in ((0, 8), (8, 16), (16, 22)):
        for h in range(a, b):
            tiles += [tile(W["w_up"], h * P), tile(W["w_up"], D_FF + h * P)]
        tiles += [tile(W["w_down"][a * P:b * P], m * P) for m in range(KT)]
    w2 = W["w_in_2"]
    for c in range(4):
        tiles += [tile(w2, c * P), tile(w2, 512 + c * P)]
    for c in range(4):
        tiles += [tile(w2, o + c * P) for o in (2560, 1536, 2048)]
    tiles += [tile(w2, 1024 + c * P) for c in range(4)]
    for m in range(KT):
        tiles += [tile(w2, 3072 + x * D + m * P) for x in (2, 1, 0)]
        tiles.append(np.concatenate([tile(W["w_a_out_2"], m * P)[:, :4], tile(W["w_c_out_2"], m * P)[:, :4]], axis=1))
    tiles += [tile(W["w_o_2"], m * P) for m in range(KT)]
    tiles += [tile(W["w_xkv_2"], m * P) for m in range(2 * KT)]
    tiles += [tile(W["w_xq_2"], m * P) for m in range(KT)]
    tiles += [tile(W["w_xo_2"], m * P) for m in range(KT)]
    down = W["w_e_down_2"].reshape(-1, D)
    for q in range(4):
        for e in range(4 * q, 4 * q + 4):
            for c in range(2):
                tiles += [tile(W["w_e_gate_2"][e], c * P), tile(W["w_e_up_2"][e], c * P)]
        tiles += [tile(down[q * D:(q + 1) * D], m * P) for m in range(KT)]
    ws = np.stack(tiles).reshape(NBLK, 2, P, KT, P).transpose(0, 2, 3, 1, 4)
    ws = np.ascontiguousarray(ws).reshape(NBLK, P, BLK)

    def cols(a):
        return np.asarray(a).reshape(-1, P).T

    def rows(a):
        return np.broadcast_to(np.asarray(a).reshape(1, -1), (P, np.asarray(a).size))

    mu = cols(g["mu_shift"][0])
    cw, cb = g["conv_w"][0], g["conv_b"][0]
    conv = []
    for h in range(22):
        for o in (0, D_FF):
            conv += [cw[x, o + h * P:o + (h + 1) * P] for x in range(3)] + [cb[o + h * P:o + (h + 1) * P]]
    conv = np.stack(conv + [np.zeros(P, cw.dtype)] * 16, axis=1)
    ca = np.concatenate([g["conv_a_w_2"][0][:, c * P:(c + 1) * P].T for c in range(4)], axis=1)
    cc = np.concatenate([g["conv_c_w_2"][0][:, c * P:(c + 1) * P].T for c in range(4)], axis=1)
    router = np.concatenate([g["w_rg_2"][0], g["w_re_2"][0]], axis=1)
    router = router.reshape(KT, P, 20).transpose(1, 0, 2).reshape(P, KT * 20)
    par = {
        "ln_attn_pre": cols(g["ln_attn_pre"]), "mu": mu[:, [12, 13, 4, 5, 6, 7, 0, 1, 2, 3, 8, 9, 10, 11]],
        "w_decay0": cols(g["w_decay0"]), "w_iclr0": cols(g["w_iclr0"]), "k_k": cols(g["k_k"]),
        "k_a": cols(g["k_a"]), "r_k": cols(g["r_k"]), "ln_x_w": cols(g["ln_x_w"]), "ln_x_b": cols(g["ln_x_b"]),
        "subln": cols(g["diff_subln"]), "ln_attn_post": cols(g["ln_attn_post"]),
        "ln_ffn_pre": cols(g["ln_ffn_pre"]), "conv": conv, "ln_ffn_post": cols(g["ln_ffn_post"]),
        "norm_mix": cols(g["norm_mix_g_2"]), "conv_a_w": ca, "conv_a_b": cols(g["conv_a_b_2"]),
        "ln_a_g": cols(g["ln_a_g_2"]), "ln_a_b": cols(g["ln_a_b_2"]), "pool_scale": cols(g["pool_scale_2"]),
        "conv_c": cc, "norm_x": cols(g["norm_x_g_2"]), "norm_mem": cols(g["norm_mem_g_2"]),
        "norm_ffn": cols(g["norm_ffn_g_2"]), "norm_f": cols(g["norm_f_g_2"]), "w_router": router,
        "b_router": np.concatenate([rows(g["b_rg_2"]), rows(g["b_re_2"])], axis=1),
        "lam": np.concatenate([rows(g[n]) for n in ("lambda_q1", "lambda_k1", "lambda_q2", "lambda_k2")], axis=1),
    }
    params = np.ascontiguousarray(np.concatenate([par[n] for n, _ in PCOLS], axis=1))
    lora = np.stack([np.concatenate([g["w_decay_up"][0], g["w_iclr_up"][0]], axis=0), g["w_gate_up"][0]], axis=1)
    xT = g["x"][0].T.reshape(KT, P, S).transpose(1, 0, 2)
    memT = g["mem_2"][0].T.reshape(KT, P, N_MEM).transpose(1, 0, 2)
    poolw = g["w_pool_grp_2"][0].transpose(1, 0, 2)
    return {k: np.ascontiguousarray(a) for k, a in
            dict(xT=xT, memT=memT, wstream=ws, params=params, consts=constants(), lora=lora, poolw=poolw).items()}


def constants():
    import numpy as np

    i, j = np.arange(P)[:, None], np.arange(P)[None, :]
    c = np.arange(S)[None, :] - (S - P)
    same = i // HD == j // HD
    lv = [((i >> l) % 2 == 1) & ((j >> l) % 2 == 0) & (i >> (l + 1) == j >> (l + 1)) for l in range(LEVELS)]
    cnt = [np.minimum(np.arange(POOL_PAD) + 1, 2 ** (g + 1)) for g in range(4)]
    eps = np.broadcast_to(np.array([[1e-6, 1e-5, 64e-5] + [0.0] * 5]), (P, 8))
    tab = {
        "ident": i == j, "ones": np.ones((P, P)), "blk": same, "alibi": np.where(c <= i, c - i, -1e30),
        "mask_nr": np.concatenate([same & (i < j), same & (i <= j)], axis=1),
        "mask_lv": np.concatenate(lv, axis=1), "reset": np.broadcast_to(np.arange(S)[None] % HD != 0, (P, S)),
        "id64": i % HD == np.arange(HD)[None], "invcnt": np.broadcast_to(1.0 / np.concatenate(cnt)[None], (P, 64)),
        "rank": np.broadcast_to(np.array([[4, 3, 2, 1]]), (P, 4)), "eps": eps,
        "upto": i <= j, "count": np.broadcast_to(np.arange(P)[None] + 1, (P, P)),
    }
    return np.concatenate([tab[n].astype(np.float32) for n, _ in CCOLS], axis=1)


def kernel(**inputs):
    import numpy as np
    import concourse.bacc as bacc
    from concourse.bass_utils import run_bass_kernel_spmd

    arrays = pack(inputs)
    nc = bacc.Bacc("TRN2", target_bir_lowering=False, num_devices=1)
    aps = {n: nc.dram_tensor(n, a.shape, F32, kind="ExternalInput").ap() for n, a in arrays.items()}
    out = nc.dram_tensor("out", (P, KT, S), F32, kind="ExternalOutput").ap()
    build(nc, out=out, **aps)
    r = run_bass_kernel_spmd(nc, [arrays], core_ids=[0])
    got = r.results[0]["out"]
    return np.ascontiguousarray(got.transpose(2, 1, 0)).reshape(1, S, D)
```
